# Optimizing a Trainium2 kernel written in Bass

```python
import math
import jax
import jax.numpy as jnp
from jax import lax
import numpy as np
import jax, jax.numpy as jnp

D_MODEL = 1024
BATCH = 1
SEQ = 256
DEPTH = 2

DEEPNORM_ALPHA = (2 * DEPTH) ** 0.25
DEEPNORM_BETA = (8 * DEPTH) ** -0.25
LN_EPS = 1e-5
RMS_EPS = 1e-6
NUM_BUCKETS = 32
REL_MAX_DIST = 2048
REL_HEADS = 4
GDN_HEADS = 6
GDN_DK = 128
GDN_DV = 128
GDN_CONV = 4
GDN_CHUNK = 64
GDN_QK = GDN_HEADS * GDN_DK
GDN_V = GDN_HEADS * GDN_DV
SWA_CONFIGS = ((128, 1), (512, 4), (2048, 16))
SWA_GROUPS = len(SWA_CONFIGS)
SWA_HEADS = 4
SWA_HEAD_DIM = 64
SWA_BLOCK = 128
SWA_QKV = SWA_GROUPS * SWA_HEADS * SWA_HEAD_DIM
SWA_OUT = SWA_HEADS * SWA_HEAD_DIM
DIFF_HEADS = 4
DIFF_HEAD_DIM = 64
DIFF_QK = DIFF_HEADS * 2 * DIFF_HEAD_DIM
DIFF_V = DIFF_HEADS * 2 * DIFF_HEAD_DIM
Q_BLOCK = 128
GLA_HEADS = 4
GLA_DK = 64
GLA_DV = 128
GLA_GATE_RANK = 16
GLA_GATE_TAU = 16.0
GLA_CHUNK = 64
GLA_QK = GLA_HEADS * GLA_DK
GLA_V = GLA_HEADS * GLA_DV
D_FF = 2816
FFN_CONV = 3

EVEN_SIZES = (GDN_QK, GDN_QK, GDN_V, GDN_V, GDN_HEADS, GDN_HEADS, SWA_QKV, SWA_QKV, SWA_QKV)
EVEN_IN = sum(EVEN_SIZES)
EVEN_SPLITS = tuple(int(v) for v in np.cumsum(EVEN_SIZES)[:-1])
EVEN_OUT = GDN_V + SWA_OUT
ODD_SIZES = (DIFF_QK, DIFF_QK, DIFF_V, GLA_QK, GLA_QK, GLA_V, GLA_V, GLA_GATE_RANK)
ODD_IN = sum(ODD_SIZES)
ODD_SPLITS = tuple(int(v) for v in np.cumsum(ODD_SIZES)[:-1])
ODD_OUT = DIFF_V + GLA_V
N_EVEN = (DEPTH + 1) // 2
N_ODD = DEPTH // 2


def layer_norm(x, g, b):
    xf = x.astype(jnp.float32)
    mu = jnp.mean(xf, -1, keepdims=True)
    var = jnp.mean(jnp.square(xf - mu), -1, keepdims=True)
    y = (xf - mu) * lax.rsqrt(var + LN_EPS) * g.astype(jnp.float32) + b.astype(jnp.float32)
    return y.astype(x.dtype)

def rms_norm(x, w):
    xf = x.astype(jnp.float32)
    return xf * lax.rsqrt(jnp.mean(xf * xf, -1, keepdims=True) + RMS_EPS) * w.astype(jnp.float32)

def l2_normalize(x):
    return x * lax.rsqrt(jnp.sum(x * x, -1, keepdims=True) + RMS_EPS)

def causal_depthwise_conv(x, w):
    width, seq = w.shape[0], x.shape[1]
    xp = jnp.pad(x, ((0, 0), (width - 1, 0), (0, 0)))
    y = w[0] * xp[:, :seq]
    for j in range(1, width):
        y = y + w[j] * xp[:, j:j + seq]
    return y

def rel_bucket(dist):
    max_exact = NUM_BUCKETS // 2
    d = jnp.maximum(dist, 1).astype(jnp.float32)
    large = max_exact + (jnp.log(d / max_exact) / math.log(REL_MAX_DIST / max_exact)
                         * (NUM_BUCKETS - max_exact)).astype(jnp.int32)
    large = jnp.minimum(large, NUM_BUCKETS - 1)
    return jnp.where(dist < max_exact, dist, large)

def gated_delta_rule(q, k, v, g, beta):
    bsz, seq, nh, dk = q.shape
    dv = v.shape[-1]
    c = GDN_CHUNK
    n = seq // c

    def chunk(t):
        return jnp.moveaxis(t.reshape((bsz, n, c, nh) + t.shape[3:]), 3, 1)

    qc, kc, vc, gc, bc = chunk(q), chunk(k), chunk(v), chunk(g), chunk(beta)
    gam = jnp.cumsum(gc, axis=-1)
    idx = jnp.arange(c)
    incl = idx[:, None] >= idx[None, :]
    strict = idx[:, None] > idx[None, :]
    decay = jnp.exp(jnp.where(incl, gam[..., :, None] - gam[..., None, :], -jnp.inf))
    kk = jnp.einsum('bhnid,bhnjd->bhnij', kc, kc)
    lower = jnp.eye(c, dtype=jnp.float32) + jnp.where(strict, bc[..., :, None] * kk * decay, 0.0)
    rhs = jnp.concatenate([vc * bc[..., None], kc * (bc * jnp.exp(gam))[..., None]], axis=-1)
    sol = lax.linalg.triangular_solve(lower, rhs, left_side=True, lower=True, unit_diagonal=True)
    u, w = sol[..., :dv], sol[..., dv:]
    qk = jnp.einsum('bhnid,bhnjd->bhnij', qc, kc) * decay
    q_dec = qc * jnp.exp(gam)[..., None]
    k_dec = kc * jnp.exp(gam[..., -1:] - gam)[..., None]
    g_last = jnp.exp(gam[..., -1])

    def step(state, inp):
        u_n, w_n, qk_n, qd_n, kd_n, gl_n = inp
        delta = u_n - jnp.einsum('bhck,bhkv->bhcv', w_n, state)
        o_n = jnp.einsum('bhck,bhkv->bhcv', qd_n, state) + jnp.einsum('bhij,bhjv->bhiv', qk_n, delta)
        state = gl_n[..., None, None] * state + jnp.einsum('bhck,bhcv->bhkv', kd_n, delta)
        return state, o_n

    xs = tuple(jnp.moveaxis(t, 2, 0) for t in (u, w, qk, q_dec, k_dec, g_last))
    state0 = jnp.zeros((bsz, nh, dk, dv), jnp.float32)
    _, o = lax.scan(step, state0, xs)
    return o.transpose(1, 0, 3, 2, 4).reshape(bsz, seq, nh, dv)

def dilated_branch(q, k, v, window, dilation, rel_bias):
    bsz, seq, nh, dh = q.shape
    span = window // dilation
    sub = seq // dilation
    nb = -(-sub // SWA_BLOCK)
    padded = nb * SWA_BLOCK

    def to_blocks(t):
        t = t.reshape(bsz, sub, dilation, nh, dh).transpose(0, 2, 1, 3, 4)
        t = jnp.pad(t, ((0, 0), (0, 0), (0, padded - sub), (0, 0), (0, 0)))
        return t.reshape(bsz, dilation, nb, SWA_BLOCK, nh, dh)

    def with_prev(t):
        prev = jnp.pad(t, ((0, 0), (0, 0), (1, 0), (0, 0), (0, 0), (0, 0)))[:, :, :-1]
        return jnp.concatenate([prev, t], axis=3)

    qb = to_blocks(q)
    kb, vb = with_prev(to_blocks(k)), with_prev(to_blocks(v))
    qi = jnp.arange(SWA_BLOCK)[:, None] + SWA_BLOCK
    kj = jnp.arange(2 * SWA_BLOCK)[None, :]
    rel = qi - kj
    key_sub = jnp.arange(nb)[:, None, None] * SWA_BLOCK + kj[None] - SWA_BLOCK
    mask = (rel >= 0) & (rel <= span) & (key_sub >= 0)
    bias = jnp.moveaxis(rel_bias[rel_bucket(jnp.maximum(rel, 0) * dilation)], -1, 0)
    s = jnp.einsum('bgnqhd,bgnkhd->bgnhqk', qb, kb).astype(jnp.float32) * dh ** -0.5
    s = s + bias.astype(jnp.float32)
    s = jnp.where(mask[None, None, :, None], s, -jnp.inf)
    m = jnp.max(s, axis=-1, keepdims=True)
    p = jnp.exp(s - m)
    l = jnp.sum(p, axis=-1, keepdims=True)
    o = jnp.einsum('bgnhqk,bgnkhd->bgnqhd', (p / l).astype(v.dtype), vb)
    lse = (m + jnp.log(l))[..., 0]
    o = o.reshape(bsz, dilation, padded, nh, dh)[:, :, :sub]
    o = o.transpose(0, 2, 1, 3, 4).reshape(bsz, seq, nh, dh)
    lse = lse.transpose(0, 1, 2, 4, 3).reshape(bsz, dilation, padded, nh)[:, :, :sub]
    lse = lse.transpose(0, 2, 1, 3).reshape(bsz, seq, nh)
    return o, lse

def dilated_attention(q, k, v, rel_bias):
    bsz, seq = q.shape[0], q.shape[1]
    outs, lses = [], []
    for g, (window, dilation) in enumerate(SWA_CONFIGS):
        o, lse = dilated_branch(q[:, :, g], k[:, :, g], v[:, :, g], window, dilation, rel_bias)
        outs.append(o)
        lses.append(lse)
    wts = jax.nn.softmax(jnp.stack(lses, 0), axis=0)
    o = jnp.einsum('gbsh,gbshd->bshd', wts, jnp.stack(outs, 0).astype(jnp.float32))
    return o.reshape(bsz, seq, SWA_OUT)

def even_mixer(x, rel_bias, w_in, conv_w, a_log, dt_bias, norm_w, w_out):
    bsz, seq, _ = x.shape
    f32 = jnp.float32
    q_a, k_a, v_a, z_a, b_a, a_a, q_b, k_b, v_b = jnp.split(x @ w_in, EVEN_SPLITS, axis=-1)
    qkv = jax.nn.silu(causal_depthwise_conv(jnp.concatenate([q_a, k_a, v_a], -1), conv_w)).astype(f32)
    q_a, k_a, v_a = jnp.split(qkv, (GDN_QK, 2 * GDN_QK), axis=-1)
    hk = (bsz, seq, GDN_HEADS, GDN_DK)
    q_a = l2_normalize(q_a.reshape(hk)) * GDN_DK ** -0.5
    k_a = l2_normalize(k_a.reshape(hk))
    v_a = v_a.reshape(bsz, seq, GDN_HEADS, GDN_DV)
    beta = jax.nn.sigmoid(b_a.astype(f32))
    g = -jnp.exp(a_log.astype(f32)) * jax.nn.softplus(a_a.astype(f32) + dt_bias.astype(f32))
    o_a = gated_delta_rule(q_a, k_a, v_a, g, beta)
    o_a = rms_norm(o_a, norm_w) * jax.nn.silu(z_a.astype(f32).reshape(bsz, seq, GDN_HEADS, GDN_DV))
    o_a = o_a.reshape(bsz, seq, GDN_V).astype(x.dtype)
    shp = (bsz, seq, SWA_GROUPS, SWA_HEADS, SWA_HEAD_DIM)
    o_b = dilated_attention(q_b.reshape(shp), k_b.reshape(shp), v_b.reshape(shp), rel_bias).astype(x.dtype)
    return jnp.concatenate([o_a, o_b], axis=-1) @ w_out

def diff_attention(q, k, v, lam, rel_bias):
    bsz, seq, nh, _, dh = q.shape
    nq = seq // Q_BLOCK
    qb = q.reshape(bsz, nq, Q_BLOCK, nh, 2, dh).transpose(1, 0, 3, 4, 2, 5)
    kt = k.transpose(0, 2, 3, 1, 4)
    vt = v.transpose(0, 2, 1, 3)
    k_pos = jnp.arange(seq)

    def block(args):
        q_blk, start = args
        dist = (start + jnp.arange(Q_BLOCK))[:, None] - k_pos[None, :]
        bias = jnp.moveaxis(rel_bias[rel_bucket(jnp.maximum(dist, 0))], -1, 0).astype(jnp.float32)
        s = jnp.einsum('bhcqd,bhckd->bhcqk', q_blk, kt).astype(jnp.float32) * dh ** -0.5
        s = jnp.where(dist >= 0, s + bias[None, :, None], -jnp.inf)
        p = jax.nn.softmax(s, axis=-1)
        attn = p[:, :, 0] - lam * p[:, :, 1]
        return jnp.einsum('bhqk,bhkv->bhqv', attn.astype(v.dtype), vt)

    o = lax.map(block, (qb, jnp.arange(nq) * Q_BLOCK))
    return o.transpose(1, 0, 3, 2, 4).reshape(bsz, seq, nh, 2 * dh)

def gla_chunked(q, k, v, log_a):
    bsz, seq, nh, dk = q.shape
    dv = v.shape[-1]
    c = GLA_CHUNK
    n = seq // c

    def chunk(t):
        return t.reshape(bsz, n, c, nh, t.shape[-1]).transpose(1, 0, 3, 2, 4)

    qc, kc, vc = chunk(q), chunk(k), chunk(v)
    bc = jnp.cumsum(chunk(log_a), axis=3)
    idx = jnp.arange(c)
    incl = (idx[:, None] >= idx[None, :])[:, :, None]

    def step(state, inp):
        q_n, k_n, v_n, b_n = inp
        dec = jnp.exp(jnp.where(incl, b_n[..., :, None, :] - b_n[..., None, :, :], -jnp.inf))
        attn = jnp.einsum('bhik,bhjk,bhijk->bhij', q_n, k_n, dec)
        o_n = jnp.einsum('bhik,bhkv->bhiv', q_n * jnp.exp(b_n), state) + jnp.einsum('bhij,bhjv->bhiv', attn, v_n)
        b_last = b_n[..., -1:, :]
        state = jnp.exp(b_last[..., 0, :])[..., None] * state + jnp.einsum(
            'bhck,bhcv->bhkv', k_n * jnp.exp(b_last - b_n), v_n)
        return state, o_n

    state0 = jnp.zeros((bsz, nh, dk, dv), jnp.float32)
    _, o = lax.scan(step, state0, (qc, kc, vc, bc))
    return o.transpose(1, 0, 3, 2, 4).reshape(bsz, seq, nh, dv)

def odd_mixer(x, rel_bias, w_in, lam_params, diff_norm_w, gla_w_gate, gla_b_gate, gla_norm_w, w_out, lam_init):
    bsz, seq, _ = x.shape
    f32 = jnp.float32
    q_c, k_c, v_c, q_d, k_d, v_d, r_d, g_d = jnp.split(x @ w_in, ODD_SPLITS, axis=-1)
    lp = lam_params.astype(f32)
    lam = jnp.exp(jnp.sum(lp[0] * lp[1])) - jnp.exp(jnp.sum(lp[2] * lp[3])) + lam_init
    shp = (bsz, seq, DIFF_HEADS, 2, DIFF_HEAD_DIM)
    o_c = diff_attention(q_c.reshape(shp), k_c.reshape(shp),
                         v_c.reshape(bsz, seq, DIFF_HEADS, 2 * DIFF_HEAD_DIM), lam, rel_bias)
    o_c = (rms_norm(o_c, diff_norm_w) * (1.0 - lam_init)).reshape(bsz, seq, DIFF_V).astype(x.dtype)
    log_a = jax.nn.log_sigmoid((g_d @ gla_w_gate + gla_b_gate).astype(f32)) / GLA_GATE_TAU
    hk = (bsz, seq, GLA_HEADS, GLA_DK)
    o_d = gla_chunked(q_d.astype(f32).reshape(hk) * GLA_DK ** -0.5, k_d.astype(f32).reshape(hk),
                      v_d.astype(f32).reshape(bsz, seq, GLA_HEADS, GLA_DV), log_a.reshape(hk))
    o_d = rms_norm(o_d, gla_norm_w) * jax.nn.silu(r_d.astype(f32).reshape(bsz, seq, GLA_HEADS, GLA_DV))
    o_d = o_d.reshape(bsz, seq, GLA_V).astype(x.dtype)
    return jnp.concatenate([o_c, o_d], axis=-1) @ w_out

def conv_ffn(x, w_up, conv_w, conv_b, w_down):
    h = causal_depthwise_conv(x @ w_up, conv_w) + conv_b
    gate, val = jnp.split(h, 2, axis=-1)
    return (jax.nn.silu(gate) * val) @ w_down

def first_inputs(seed: int = 0) -> dict:
    key = jax.random.key(seed)
    ks = jax.random.split(key, 24)
    f32 = jnp.float32

    def normal(k, shape, scale):
        return jax.random.normal(k, shape, f32) * scale

    dt = jnp.exp(jax.random.uniform(ks[5], (N_EVEN, GDN_HEADS), f32, math.log(1e-3), math.log(1e-1)))
    return {
        'x': normal(ks[0], (BATCH, SEQ, D_MODEL), 1.0),
        'rel_bias': normal(ks[1], (NUM_BUCKETS, REL_HEADS), 0.1),
        'w_in_even': normal(ks[2], (N_EVEN, D_MODEL, EVEN_IN), D_MODEL ** -0.5),
        'gdn_conv_w': normal(ks[3], (N_EVEN, GDN_CONV, 2 * GDN_QK + GDN_V), GDN_CONV ** -0.5),
        'gdn_a_log': jnp.log(jax.random.uniform(ks[4], (N_EVEN, GDN_HEADS), f32, 1.0, 16.0)),
        'gdn_dt_bias': dt + jnp.log(-jnp.expm1(-dt)),
        'gdn_norm_w': 1.0 + normal(ks[6], (N_EVEN, GDN_DV), 0.05),
        'w_out_even': normal(ks[7], (N_EVEN, EVEN_OUT, D_MODEL), EVEN_OUT ** -0.5 * DEEPNORM_BETA),
        'w_in_odd': normal(ks[8], (N_ODD, D_MODEL, ODD_IN), D_MODEL ** -0.5),
        'diff_lambda': normal(ks[9], (N_ODD, 4, DIFF_HEAD_DIM), 0.1),
        'diff_norm_w': 1.0 + normal(ks[10], (N_ODD, 2 * DIFF_HEAD_DIM), 0.05),
        'gla_w_gate': normal(ks[11], (N_ODD, GLA_GATE_RANK, GLA_QK), GLA_GATE_RANK ** -0.5),
        'gla_b_gate': normal(ks[12], (N_ODD, GLA_QK), 0.1),
        'gla_norm_w': 1.0 + normal(ks[13], (N_ODD, GLA_DV), 0.05),
        'w_out_odd': normal(ks[14], (N_ODD, ODD_OUT, D_MODEL), ODD_OUT ** -0.5 * DEEPNORM_BETA),
        'ffn_w_up': normal(ks[15], (DEPTH, D_MODEL, 2 * D_FF), D_MODEL ** -0.5),
        'ffn_conv_w': normal(ks[16], (DEPTH, FFN_CONV, 2 * D_FF), FFN_CONV ** -0.5),
        'ffn_conv_b': normal(ks[17], (DEPTH, 2 * D_FF), 0.02),
        'ffn_w_down': normal(ks[18], (DEPTH, D_FF, D_MODEL), D_FF ** -0.5 * DEEPNORM_BETA),
        'ln_g': 1.0 + normal(ks[19], (DEPTH, 2, D_MODEL), 0.05),
        'ln_b': normal(ks[20], (DEPTH, 2, D_MODEL), 0.02),
    }

def first_block(x, rel_bias, w_in_even, gdn_conv_w, gdn_a_log, gdn_dt_bias, gdn_norm_w, w_out_even,
              w_in_odd, diff_lambda, diff_norm_w, gla_w_gate, gla_b_gate, gla_norm_w, w_out_odd,
              ffn_w_up, ffn_conv_w, ffn_conv_b, ffn_w_down, ln_g, ln_b):
    h = x
    for layer in range(DEPTH):
        i = layer // 2
        if layer % 2 == 0:
            mix = even_mixer(h, rel_bias, w_in_even[i], gdn_conv_w[i], gdn_a_log[i], gdn_dt_bias[i],
                             gdn_norm_w[i], w_out_even[i])
        else:
            lam_init = 0.8 - 0.6 * math.exp(-0.3 * layer)
            mix = odd_mixer(h, rel_bias, w_in_odd[i], diff_lambda[i], diff_norm_w[i], gla_w_gate[i],
                            gla_b_gate[i], gla_norm_w[i], w_out_odd[i], lam_init)
        h = layer_norm(DEEPNORM_ALPHA * h + mix, ln_g[layer, 0], ln_b[layer, 0])
        ffn = conv_ffn(h, ffn_w_up[layer], ffn_conv_w[layer], ffn_conv_b[layer], ffn_w_down[layer])
        h = layer_norm(DEEPNORM_ALPHA * h + ffn, ln_g[layer, 1], ln_b[layer, 1])
    return h


N_MIXERS = 2
SB_HEADS = 16
SB_HEAD_DIM = D_MODEL // SB_HEADS
RET_HEADS = 8
RET_QK_DIM = D_MODEL // RET_HEADS
RET_V_DIM = 2 * RET_QK_DIM
RET_CHUNK = 128
ROPE_BASE = 10000.0
N_EXPERTS = 16
N_GROUPS = 4
EXPERTS_PER_GROUP = N_EXPERTS // N_GROUPS
TOP_K = 2
D_EXPERT = D_MODEL // 2
N_SB = (DEPTH + 1) // 2
N_RET = DEPTH // 2
DEEPNORM_ALPHA_2 = (2 * DEPTH) ** 0.25
DEEPNORM_BETA_2 = (8 * DEPTH) ** -0.25


def layer_norm_2(x, g, b):
    xf = x.astype(jnp.float32)
    mu = jnp.mean(xf, axis=-1, keepdims=True)
    var = jnp.mean(jnp.square(xf - mu), axis=-1, keepdims=True)
    y = (xf - mu) * lax.rsqrt(var + LN_EPS) * g.astype(jnp.float32) + b.astype(jnp.float32)
    return y.astype(x.dtype)

def adaln_params(c, w, b):
    m = jax.nn.silu(c) @ w + b
    shift, scale, gate = jnp.split(m, 3, axis=-1)
    return shift[:, None, :], scale[:, None, :], gate[:, None, :]

def stick_breaking_attention(h, w_in, w_out):
    B, S, _ = h.shape
    qkv = (h @ w_in).reshape(B, S, 3, SB_HEADS, SB_HEAD_DIM)
    q = qkv[:, :, 0].transpose(0, 2, 1, 3)
    k = qkv[:, :, 1].transpose(0, 2, 1, 3)
    v = qkv[:, :, 2].transpose(0, 2, 1, 3)
    n_blocks = S // Q_BLOCK
    q_blocks = q.reshape(B, SB_HEADS, n_blocks, Q_BLOCK, SB_HEAD_DIM).transpose(2, 0, 1, 3, 4)
    key_pos = jnp.arange(S)
    scale = SB_HEAD_DIM ** -0.5

    def block(args):
        qb, i = args
        z = jnp.einsum('bhqd,bhkd->bhqk', qb, k).astype(jnp.float32) * scale
        q_pos = i * Q_BLOCK + jnp.arange(Q_BLOCK)
        causal = key_pos[None, :] < q_pos[:, None]
        log_keep = jnp.where(causal, jax.nn.log_sigmoid(-z), 0.0)
        suffix = lax.cumsum(log_keep, axis=3, reverse=True) - log_keep
        a = jnp.where(causal, jnp.exp(jax.nn.log_sigmoid(z) + suffix), 0.0)
        return jnp.einsum('bhqk,bhkd->bhqd', a.astype(v.dtype), v)

    o = lax.map(block, (q_blocks, jnp.arange(n_blocks)))
    o = o.transpose(1, 0, 3, 2, 4).reshape(B, S, D_MODEL)
    return o @ w_out

def rotary(x, cos, sin):
    half = x.shape[-1] // 2
    x1, x2 = x[..., :half], x[..., half:]
    return jnp.concatenate([x1 * cos - x2 * sin, x2 * cos + x1 * sin], axis=-1)

def retention(h, positions, w_in, gn_g, w_out):
    B, S, _ = h.shape
    f32 = jnp.float32
    proj = h @ w_in
    q, k, v, g = jnp.split(proj, [D_MODEL, 2 * D_MODEL, 4 * D_MODEL], axis=-1)
    q = q.reshape(B, S, RET_HEADS, RET_QK_DIM).astype(f32)
    k = k.reshape(B, S, RET_HEADS, RET_QK_DIM).astype(f32) * (RET_QK_DIM ** -0.5)
    v = v.reshape(B, S, RET_HEADS, RET_V_DIM).astype(f32)
    inv_freq = 1.0 / (ROPE_BASE ** (jnp.arange(0, RET_QK_DIM, 2, dtype=f32) / RET_QK_DIM))
    ang = positions.astype(f32)[..., None] * inv_freq
    cos = jnp.cos(ang)[:, :, None, :]
    sin = jnp.sin(ang)[:, :, None, :]
    q = rotary(q, cos, sin)
    k = rotary(k, cos, sin)

    log_gamma = jnp.log(1.0 - jnp.exp2(-5.0 - jnp.arange(RET_HEADS, dtype=f32)))
    n = jnp.arange(RET_CHUNK, dtype=f32)
    diff = n[:, None] - n[None, :]
    dmask = jnp.where(diff >= 0, jnp.exp(jnp.maximum(diff, 0.0) * log_gamma[:, None, None]), 0.0)
    xi = jnp.exp((n + 1.0) * log_gamma[:, None])
    zeta = jnp.exp((RET_CHUNK - 1.0 - n) * log_gamma[:, None])
    chunk_decay = jnp.exp(RET_CHUNK * log_gamma)
    n_chunks = S // RET_CHUNK

    def chunks(t):
        return t.reshape(B, n_chunks, RET_CHUNK, RET_HEADS, t.shape[-1]).transpose(1, 0, 3, 2, 4)

    def step(state, xs):
        qc, kc, vc = xs
        qk = jnp.einsum('bhnd,bhmd->bhnm', qc, kc) * dmask
        inner = jnp.einsum('bhnm,bhme->bhne', qk, vc)
        cross = jnp.einsum('bhnd,bhde->bhne', qc, state) * xi[None, :, :, None]
        state = state * chunk_decay[None, :, None, None] + jnp.einsum(
            'bhmd,bhme->bhde', kc * zeta[None, :, :, None], vc)
        return state, inner + cross

    state0 = jnp.zeros((B, RET_HEADS, RET_QK_DIM, RET_V_DIM), f32)
    _, o = lax.scan(step, state0, (chunks(q), chunks(k), chunks(v)))
    o = o.transpose(1, 0, 3, 2, 4).reshape(B, S, RET_HEADS, RET_V_DIM)
    mu = jnp.mean(o, axis=-1, keepdims=True)
    var = jnp.mean(jnp.square(o - mu), axis=-1, keepdims=True)
    o = ((o - mu) * lax.rsqrt(var + LN_EPS)).reshape(B, S, 2 * D_MODEL) * gn_g.astype(f32)
    return (jax.nn.silu(g) * o.astype(h.dtype)) @ w_out

def grouped_moe(h, router_w, router_b, w_gate, w_up, w_down):
    B, S, Dm = h.shape
    t = h.reshape(B * S, Dm)
    logits = t.astype(jnp.float32) @ router_w.astype(jnp.float32) + router_b.astype(jnp.float32)
    probs = jax.nn.softmax(logits, axis=-1)
    grouped = probs.reshape(-1, N_GROUPS, EXPERTS_PER_GROUP)
    group_score = jnp.sum(lax.top_k(grouped, TOP_K)[0], axis=-1)
    sel_group = jnp.argmax(group_score, axis=-1)
    expert_group = jnp.arange(N_EXPERTS) // EXPERTS_PER_GROUP
    in_group = expert_group[None, :] == sel_group[:, None]
    masked = jnp.where(in_group, logits, -jnp.inf)
    top_val, top_idx = lax.top_k(masked, TOP_K)
    top_w = jax.nn.softmax(top_val, axis=-1)
    combine = jnp.sum(jax.nn.one_hot(top_idx, N_EXPERTS, dtype=jnp.float32) * top_w[..., None], axis=1)
    out = jnp.zeros(t.shape, jnp.float32)
    for e in range(N_EXPERTS):
        hidden = jax.nn.silu(t @ w_gate[e]) * (t @ w_up[e])
        out = out + combine[:, e:e + 1] * (hidden @ w_down[e]).astype(jnp.float32)
    return out.astype(h.dtype).reshape(B, S, Dm)

def second_inputs(seed: int = 0) -> dict:
    key = jax.random.key(seed)
    ks = jax.random.split(key, 20)
    D, F = D_MODEL, D_EXPERT
    nrm = jax.random.normal
    x = nrm(ks[0], (BATCH, SEQ, D), jnp.float32)
    c = nrm(ks[1], (BATCH, D), jnp.float32)
    positions = jnp.broadcast_to(jnp.arange(SEQ, dtype=jnp.int32)[None, :], (BATCH, SEQ))
    ada_w = nrm(ks[2], (DEPTH, 2, D, 3 * D), jnp.float32) * (0.5 * D ** -0.5)
    ada_b = nrm(ks[3], (DEPTH, 2, 3 * D), jnp.float32) * 0.02
    ln_g = 1.0 + 0.02 * nrm(ks[4], (DEPTH, 2, D), jnp.float32)
    ln_b = 0.02 * nrm(ks[5], (DEPTH, 2, D), jnp.float32)
    sb_col = jnp.concatenate([jnp.ones((2 * D,), jnp.float32), jnp.full((D,), DEEPNORM_BETA_2, jnp.float32)])
    sb_w_in = nrm(ks[6], (N_SB, D, 3 * D), jnp.float32) * (D ** -0.5) * sb_col
    sb_w_out = nrm(ks[7], (N_SB, D, D), jnp.float32) * (D ** -0.5) * DEEPNORM_BETA_2
    ret_col = jnp.concatenate([jnp.ones((2 * D,), jnp.float32), jnp.full((2 * D,), DEEPNORM_BETA_2, jnp.float32),
                               jnp.ones((2 * D,), jnp.float32)])
    ret_w_in = nrm(ks[8], (N_RET, D, 6 * D), jnp.float32) * (D ** -0.5) * ret_col
    ret_gn_g = 1.0 + 0.02 * nrm(ks[9], (N_RET, 2 * D), jnp.float32)
    ret_w_out = nrm(ks[10], (N_RET, 2 * D, D), jnp.float32) * ((2 * D) ** -0.5) * DEEPNORM_BETA_2
    router_w = nrm(ks[11], (D, N_EXPERTS), jnp.float32) * (D ** -0.5)
    router_b = nrm(ks[12], (N_EXPERTS,), jnp.float32) * 0.01
    moe_w_gate = nrm(ks[13], (DEPTH, N_EXPERTS, D, F), jnp.float32) * (D ** -0.5)
    moe_w_up = nrm(ks[14], (DEPTH, N_EXPERTS, D, F), jnp.float32) * (D ** -0.5) * DEEPNORM_BETA_2
    moe_w_down = nrm(ks[15], (DEPTH, N_EXPERTS, F, D), jnp.float32) * (F ** -0.5) * DEEPNORM_BETA_2
    return {"x": x, "c": c, "positions": positions, "ada_w": ada_w, "ada_b": ada_b,
            "ln_g": ln_g, "ln_b": ln_b, "sb_w_in": sb_w_in, "sb_w_out": sb_w_out,
            "ret_w_in": ret_w_in, "ret_gn_g": ret_gn_g, "ret_w_out": ret_w_out,
            "router_w": router_w, "router_b": router_b, "moe_w_gate": moe_w_gate,
            "moe_w_up": moe_w_up, "moe_w_down": moe_w_down}

def second_block(x, c, positions, ada_w, ada_b, ln_g, ln_b, sb_w_in, sb_w_out, ret_w_in, ret_gn_g,
              ret_w_out, router_w, router_b, moe_w_gate, moe_w_up, moe_w_down):
    for i in range(DEPTH):
        shift, scale, gate = adaln_params(c, ada_w[i, 0], ada_b[i, 0])
        h = x * (1.0 + scale) + shift
        if i % N_MIXERS == 0:
            y = stick_breaking_attention(h, sb_w_in[i // 2], sb_w_out[i // 2])
        else:
            y = retention(h, positions, ret_w_in[i // 2], ret_gn_g[i // 2], ret_w_out[i // 2])
        x = layer_norm_2(DEEPNORM_ALPHA_2 * x + (1.0 + gate) * y, ln_g[i, 0], ln_b[i, 0])
        shift, scale, gate = adaln_params(c, ada_w[i, 1], ada_b[i, 1])
        h = x * (1.0 + scale) + shift
        y = grouped_moe(h, router_w, router_b, moe_w_gate[i], moe_w_up[i], moe_w_down[i])
        x = layer_norm_2(DEEPNORM_ALPHA_2 * x + (1.0 + gate) * y, ln_g[i, 1], ln_b[i, 1])
    return x


def setup_inputs(seed=0):
    out = dict(first_inputs(seed))
    for name, value in second_inputs(seed + 1).items():
        if name != "x":
            out[name + "_2"] = value
    return out


def reference(
    x, rel_bias, w_in_even, gdn_conv_w, gdn_a_log, gdn_dt_bias, gdn_norm_w, w_out_even,
    w_in_odd, diff_lambda, diff_norm_w, gla_w_gate, gla_b_gate, gla_norm_w, w_out_odd, ffn_w_up,
    ffn_conv_w, ffn_conv_b, ffn_w_down, ln_g, ln_b, c_2, positions_2, ada_w_2, ada_b_2, ln_g_2,
    ln_b_2, sb_w_in_2, sb_w_out_2, ret_w_in_2, ret_gn_g_2, ret_w_out_2, router_w_2, router_b_2,
    moe_w_gate_2, moe_w_up_2, moe_w_down_2,
):
    x = first_block(
        x, rel_bias, w_in_even, gdn_conv_w, gdn_a_log, gdn_dt_bias, gdn_norm_w, w_out_even,
        w_in_odd, diff_lambda, diff_norm_w, gla_w_gate, gla_b_gate, gla_norm_w, w_out_odd,
        ffn_w_up, ffn_conv_w, ffn_conv_b, ffn_w_down, ln_g, ln_b,
    )
    return second_block(
        x, c_2, positions_2, ada_w_2, ada_b_2, ln_g_2, ln_b_2, sb_w_in_2, sb_w_out_2,
        ret_w_in_2, ret_gn_g_2, ret_w_out_2, router_w_2, router_b_2, moe_w_gate_2, moe_w_up_2,
        moe_w_down_2,
    )


_drawn_inputs = setup_inputs


def setup_inputs(seed=0):
    import zlib

    import numpy as np

    out = dict(_drawn_inputs(seed))
    spreads = {}
    factors = {'gdn_norm_w': 3.852,
     'diff_lambda': 3.701,
     'diff_norm_w': 2.851,
     'gla_b_gate': 3.303,
     'gla_norm_w': 3.129,
     'ffn_conv_b': 2.767,
     'ret_gn_g_2': 8.0,
     'router_b_2': 4.097}
    for name, (base, spread) in spreads.items():
        noise = np.random.default_rng([zlib.crc32(name.encode()), seed]).standard_normal(out[name].shape)
        drawn = base * np.exp(spread * noise) if base else spread * noise
        out[name] = jnp.asarray(drawn.astype(out[name].dtype))
    for name, factor in factors.items():
        out[name] = (out[name] * factor).astype(out[name].dtype)
    return out
```

```python
import math
from contextlib import ExitStack

import numpy as np
import concourse.bass as bass
from concourse import mybir

F32 = mybir.dt.float32
I32 = mybir.dt.int32
ALU = mybir.AluOpType
ACT = mybir.ActivationFunctionType
X = mybir.AxisListType.X
ALPHA = 4 ** 0.25
LAM0 = 0.8 - 0.6 * math.exp(-0.3)
SLOTS = 4
NEG = -1e30


class Queue:

    def __init__(self, sem, link):
        self.sem, self.link, self.ops, self.n, self.seen = sem, link, [], 0, {}

    def wait(self, *toks):
        for tok in toks:
            if tok is None:
                continue
            if isinstance(tok, list):
                self.wait(*tok)
                continue
            sem, v = tok
            if self.seen.get(id(sem), 0) < v:
                self.seen[id(sem)] = v
                self.ops.append(lambda e, s=sem, v=v: e.wait_ge(s, v))

    def __call__(self, fn, *toks, inc=True):
        self.wait(*toks)
        if self.link and self.n:
            self.wait((self.sem, self.n))
        if inc:
            self.n += 1
            self.ops.append(lambda e: fn(e).then_inc(self.sem, 1))
            return (self.sem, self.n)
        self.ops.append(fn)
        return None

    def raw(self, fn):
        self.ops.append(fn)

    def now(self):
        return (self.sem, self.n) if self.n else None


class Buf:
    def __init__(self, ap):
        self.ap, self.rel = ap, []


class Pool:

    def __init__(self, aps):
        self.free = [Buf(a) for a in aps]

    def get(self):
        return self.free.pop(0)

    def put(self, buf, *toks):
        buf.rel = [t for t in toks if t is not None]
        self.free.append(buf)


def consts():
    f = np.float32
    p = np.arange(128)[:, None]
    i = np.arange(128)[None, :]
    out, at = [], {}

    def add(name, a):
        a = np.asarray(a, f)
        if a.shape[0] < 128:
            a = np.concatenate([a, np.zeros((128 - a.shape[0], a.shape[1]), f)])
        at[name] = (sum(x.shape[1] for x in out), a.shape[1])
        out.append(a)

    add("ident", p == i)
    add("exch", p + i == 127)
    rot = np.zeros((128, 128), f)
    for m in range(64):
        rot[m + 64, m] = -1.0
        rot[m, m + 64] = 1.0
    add("rot", rot)
    add("tri", p <= i)
    add("ntri", -(p >= i).astype(f))
    add("cmt", np.where(i < p, f(NEG), f(0)))
    for s in (1, 2, 4, 8, 16, 32, 64):
        add(f"m{s}", (p // (2 * s) == i // (2 * s)) & (p % (2 * s) < s) & (i % (2 * s) >= s))
    y = np.arange(256)[None, :]
    rel = p + 128 - y
    for n, d in enumerate((1, 4, 16)):
        ok = (rel >= 0) & (rel <= 128 * d) & (rel % d == 0)
        add(f"dm{n}", np.where(ok, f(0), f(NEG)))
    add("cm", np.where(rel >= 0, f(0), f(NEG)))
    dist = 255 - np.arange(384)
    d = np.maximum(dist, 1).astype(f)
    large = 16 + (np.log(d / f(16)) / f(math.log(128.0)) * f(16)).astype(np.int32)
    b = np.where(dist < 16, dist, np.minimum(large, 31))
    add("hot", (b[None, :] == np.arange(32)[:, None]) & (dist >= 0)[None, :])
    add("freq", np.tile((1.0 / (f(10000.0) ** (np.arange(0, 128, 2).astype(f) / f(128)))).astype(f), 2)[:, None])
    add("e16", np.broadcast_to(16.0 - (np.arange(32) % 16), (128, 32)))
    add("g4", np.broadcast_to(4.0 - (np.arange(8) % 4), (128, 8)))
    lg = np.log(f(1) - np.exp2(f(-5) - np.arange(8).astype(f))).astype(f)
    yy = np.arange(256)[None, :]
    dec = [np.where(yy >= p, np.exp(np.maximum(yy - p, 0).astype(f) * lg[h]), f(0)) for h in range(8)]
    return np.concatenate(out, 1).astype(f), at, np.concatenate(dec, 1).astype(f)


PARAMS = [("gconv", 72), ("fw0", 132), ("fb0", 44), ("fw1", 132), ("fb1", 44), ("gnw", 1), ("dnw", 1),
          ("lnw", 1), ("lbg", 2), ("rgn", 16), ("adab", 64), ("c", 8), ("dl", 4), ("rb", 4),
          ("lwg", 256), ("rw", 128), ("wba", 96), ("wgd", 128)]
ROWS = [("alog", 6), ("dtb", 6), ("rtb", 16)]


def offsets(spec):
    at, n = {}, 0
    for name, w in spec:
        at[name] = (n, w)
        n += w
    return at, n


def build(nc, ins, out):
    ctx = ExitStack()
    with ctx:
        emit(nc, ctx, ins, out)


def emit(nc, ctx, ins, out):
    _, kat, _ = consts()
    pat, npar = offsets(PARAMS)
    rat, nrow = offsets(ROWS)
    ncon = ins["kc"].shape[1]

    def sb(name, cols, dt=F32):
        return ctx.enter_context(nc.sbuf_tensor(name, [128, cols], dt))

    def sem(name):
        return ctx.enter_context(nc.semaphore(name))

    ring = sb("ring", SLOTS * 4096)
    kc = sb("kc_sb", ncon)
    cp = sb("cp_sb", npar)
    rp = sb("rp_sb", nrow)
    ones = sb("ones", 128)
    neg1 = sb("neg1", 128)
    half = sb("half", 16)
    xs = sb("xs", 2048)
    xTs = sb("xTs", 2048)
    lnp = sb("lnp", 2048)
    gbr = sb("gbr", 1024)
    gate = sb("gate", 1024)
    mods = sb("mods", 32)
    TPs = sb("TPs", 1024)
    small = sb("small", 640)
    NA = 20900
    arena = sb("arena", NA)
    psum = ctx.enter_context(nc.psum_tensor("ps", [128, 8, 512], F32))
    scratch = nc.dram_tensor("scratch", [4, 384], F32)

    T = Queue(sem("s_pe"), False)
    V = Queue(sem("s_dve"), True)
    A = Queue(sem("s_act"), True)
    G = Queue(sem("s_pool"), True)
    S = Queue(sem("s_sp"), False)
    s_par = sem("s_par")
    s_ring = [sem(f"s_ring{i}") for i in range(SLOTS)]
    s_row = sem("s_row")
    s_dec = sem("s_dec")
    s_scr = sem("s_scr")
    s_hank = sem("s_hank")
    s_out = sem("s_out")

    PS = Pool([psum[:, i, :] for i in range(8)])

    def K(name):
        o, w = kat[name]
        return kc[:, o:o + w]

    def C(name, a=0, b=None):
        o, w = pat[name]
        return cp[:, o + a:o + (w if b is None else b)]

    def R(name):
        o, w = rat[name]
        return rp[:, o:o + w]

    ident = K("ident")
    x = xs[:, :].rearrange("p (t n) -> p t n", t=2)
    xT = xTs[:, :].rearrange("p (k n) -> p k n", k=8)

    def mm(o, l, r, start, stop, *toks, inc=False):
        return T(lambda e: e.matmul(o, l, r, start=start, stop=stop, skip_group_check=True), *toks, inc=inc)

    def tp(o, i, *toks, inc=False):
        n = i.shape[0]
        return T(lambda e: e.transpose(o, i, ident[0:n, 0:n]), *toks, inc=inc)

    def act(o, i, f, *toks, **kw):
        return A(lambda e: e.activation(o, i, f, **kw), *toks)

    def tt(q, o, a, b, op, *toks):
        return q(lambda e: e.tensor_tensor(o, a, b, op), *toks)

    def ts(q, o, a, s1, s2, op0, op1, *toks):
        if s2 is None:
            return q(lambda e: e.tensor_scalar(o, a, s1, None, op0), *toks)
        return q(lambda e: e.tensor_scalar(o, a, s1, s2, op0, op1), *toks)

    def stt(o, a, s, b, op0, op1, *toks):
        return V(lambda e: e.scalar_tensor_tensor(out=o, in0=a, scalar=s, in1=b, op0=op0, op1=op1), *toks)

    def cpy(q, o, i, *toks):
        if q is A:
            return act(o, i, ACT.Copy, *toks)
        return q(lambda e: e.tensor_copy(o, i), *toks)

    def bc(ap, shape):
        return ap.broadcast_to(shape)

    def tables(name):
        A.raw(lambda e: e.preload_act_table_set(name))

    nload = [0]
    ring_rel = [[] for _ in range(SLOTS)]

    def load(src, kt):
        n = nload[0]
        nload[0] += 1
        s = n % SLOTS
        w = src.shape[1]
        S.wait(*ring_rel[s])
        dst = ring[:, s * 4096:s * 4096 + w]
        S.raw(lambda e: e.dma_start(dst, src).then_inc(s_ring[s], 16))
        view = dst.rearrange("p (k n) -> p k n", k=kt)
        return view, (s_ring[s], 16 * (n // SLOTS + 1)), s

    def done(s, tok):
        ring_rel[s] = [tok]

    top = [0]

    def take(cols):
        a = top[0]
        top[0] += cols
        assert top[0] <= NA, top[0]
        return arena[:, a:a + cols]

    def barrier():
        toks = [q.now() for q in (T, V, A, G)]
        for q in (T, V, A, G, S):
            if q is not S:
                q.wait(*toks)
        top[0] = 0
        return toks

    A.raw(lambda e: e.dma_start(kc[:, :], ins["kc"]).then_inc(s_par, 16))
    A.raw(lambda e: e.dma_start(cp[:, :], ins["cp"]).then_inc(s_par, 16))
    A.raw(lambda e: e.dma_start(rp[:, :], ins["rp"].broadcast_to([128, nrow])).then_inc(s_par, 16))
    A.raw(lambda e: e.dma_start(x[:, 0, :], ins["x"][0:128, :]).then_inc(s_par, 16))
    A.raw(lambda e: e.dma_start(x[:, 1, :], ins["x"][128:256, :]).then_inc(s_par, 16))
    PAR = (s_par, 80)
    m1 = G(lambda e: e.memset(ones[:, :], 1.0))
    m2 = G(lambda e: e.memset(neg1[:, :], -1.0))
    m3 = G(lambda e: e.memset(half[:, :], -0.5))
    for q in (T, V, A, G):
        q.wait(PAR, m3)
    nrows = [0]

    def load_rows(i, gated, *toks):
        A.wait(*toks)
        k = 3 if gated else 2
        for dst, r in ((lnp[:, 0:1024], 3 * i), (lnp[:, 1024:2048], 3 * i + 1), (gbr[:, :], 3 * i + 2))[:k]:
            A.raw(lambda e, dst=dst, r=r: e.dma_start(dst, ins["rows"][r:r + 1, :].broadcast_to([128, 1024]))
                  .then_inc(s_row, 16))
            nrows[0] += 1
        return (s_row, 16 * nrows[0])

    top[0] = 0
    hrow = take(384)
    hank = take(1024)
    b = PS.get()
    t = mm(b.ap[0:4, 0:384], C("rb")[0:32, :], K("hot")[0:32, :], True, True, inc=True)
    t = cpy(V, hrow[0:4, :], b.ap[0:4, 0:384], t)
    PS.put(b, t)
    A.wait(t)
    A.raw(lambda e: e.dma_start(scratch[:, :], hrow[0:4, :]).then_inc(s_scr, 16))
    A.wait((s_scr, 16))
    hsrc = bass.AP(tensor=scratch[:, :].tensor, offset=0, ap=[[1, 128], [384, 4], [1, 256]])
    A.raw(lambda e: e.dma_start(hank.rearrange("p (h n) -> p h n", h=4), hsrc).then_inc(s_hank, 16))
    TP = TPs[:, :].rearrange("p (h n) -> p h n", h=4)
    for c in range(2):
        b = PS.get()
        t = mm(b.ap, K("exch"), hank[:, 512 * c:512 * c + 512], True, True, (s_hank, 16), b.rel, inc=True)
        t = cpy(V, TPs[:, 512 * c:512 * c + 512], b.ap, t)
        PS.put(b, t)
    TPt = t

    def transposed(tok, mod=None):
        last = []
        for kp in range(4):
            b = PS.get()
            v = b.ap.rearrange("p (k t n) -> p k t n", k=2, t=2)
            for k in range(2):
                for t in range(2):
                    f = 2 * kp + k
                    r = tp(v[:, k, t, :], x[:, t, f * 128:f * 128 + 128], tok, b.rel, inc=(k == 1 and t == 1))
            w = b.ap.rearrange("p (k n) -> p k n", k=2)
            if mod is None:
                e = cpy(A if kp % 2 else V, xT[:, 2 * kp:2 * kp + 2, :], w, r)
            else:
                e = []
                for k in range(2):
                    f = 2 * kp + k
                    e = ts(V, xT[:, f, :], w[:, k, :], mod[0][:, 8 + f:9 + f], mod[0][:, f:f + 1],
                           ALU.mult, ALU.add, r, mod[1])
            PS.put(b, e)
            last.append(e)
        return last

    def proj_T(src, ntile, tok, evac, kt=8, act_in=None):
        a = xT if act_in is None else act_in
        view, arrived, slot = load(src, kt)
        for c in range(ntile):
            b = PS.get()
            for k in range(kt):
                r = mm(b.ap[:, 0:256], view[:, k, c * 128:c * 128 + 128], a[:, k, :], k == 0, k == kt - 1,
                       arrived, tok, b.rel, inc=(k == kt - 1))
            if c == ntile - 1:
                done(slot, r)
            PS.put(b, evac(c, b.ap[:, 0:256], r))

    def proj_rows(src, cols, tok, evac):
        view, arrived, slot = load(src, 8)
        for t in range(2):
            b = PS.get()
            for k in range(8):
                r = mm(b.ap[:, 0:cols], xT[:, k, t * 128:t * 128 + 128], view[:, k, :], k == 0, k == 7,
                       arrived, tok, b.rel, inc=(k == 7))
            if t == 1:
                done(slot, r)
            PS.put(b, evac(t, b.ap[:, 0:cols], r))

    def down(srcs, lhs, tok):
        banks = [PS.get() for _ in range(4)]
        total = sum(s.shape[1] // 1024 for s in srcs)
        k0 = 0
        for src in srcs:
            kt = src.shape[1] // 1024
            view, arrived, slot = load(src, kt)
            for k in range(kt):
                f = k0 + k
                for t in range(2):
                    for c in range(2):
                        b = banks[2 * t + c]
                        r = mm(b.ap, lhs[:, f, t * 128:t * 128 + 128], view[:, k, c * 512:c * 512 + 512],
                               f == 0, f == total - 1, arrived, tok, b.rel,
                               inc=(k == kt - 1 and t == 1 and c == 1))
            done(slot, r)
            k0 += kt
        return banks, r

    def norm(src, stok, rtok, gated, last=False):
        toks = []
        st = small[:, 600:624]
        for t in range(2):
            for c in range(2):
                xx = x[:, t, c * 512:c * 512 + 512]
                if isinstance(src, list):
                    s = src[2 * t + c].ap
                else:
                    s = src[:, t, c * 512:c * 512 + 512]
                if gated:
                    d = s if not isinstance(src, list) else tmpn[:, 0:512]
                    r = tt(V, d, s, gate[:, c * 512:c * 512 + 512], ALU.mult, stok)
                    if isinstance(src, list):
                        PS.put(src[2 * t + c], r)
                    s = d
                r = stt(xx, xx, ALPHA, s, ALU.mult, ALU.add, stok)
                if isinstance(src, list) and not gated:
                    PS.put(src[2 * t + c], r)
                V(lambda e, c=c, xx=xx, t=t: e.bn_stats(small[:, 560 + 12 * t + 6 * c:566 + 12 * t + 6 * c], xx))
            mv = st[:, 4 * t:4 * t + 2]
            V(lambda e, mv=mv, t=t: e.bn_aggr(mv, small[:, 560 + 12 * t:572 + 12 * t]))
            r = ts(V, st[:, 4 * t + 2:4 * t + 3], mv[:, 1:2], 1e-5, None, ALU.add, None)
            r = tt(G, st[:, 4 * t + 3:4 * t + 4], st[:, 4 * t + 2:4 * t + 3], half[:, 0:1], ALU.pow, r)
            ts(V, x[:, t, :], x[:, t, :], mv[:, 0:1], st[:, 4 * t + 3:4 * t + 4], ALU.subtract, ALU.mult, r)
            tt(V, x[:, t, :], x[:, t, :], lnp[:, 0:1024], ALU.mult, rtok)
            r = tt(V, x[:, t, :], x[:, t, :], lnp[:, 1024:2048], ALU.add)
            toks.append(r)
            if last:
                A.wait(r)
                A.raw(lambda e, t=t: e.dma_start(out[t * 128:t * 128 + 128, :], x[:, t, :]).then_inc(s_out, 16))
        return toks

    def inv_sqrt(dst, sums, scale, eps, add, tok):
        epsc[eps]
        r = act(dst, sums, ACT.Ln, tok, scale=scale, bias=epsc[eps])
        if add:
            return r, act(dst, dst, ACT.Exp, scale=-0.5, bias=epsc[add])
        return r, act(dst, dst, ACT.Exp, scale=-0.5)

    epsc = {}
    for n, v in enumerate((1e-6, 1e-5, math.log(128 ** -0.5), math.pi / 2)):
        epsc[v] = small[:, 624 + n:625 + n]
        r = V(lambda e, n=n, v=v: e.memset(small[:, 624 + n:625 + n], v))
    A.wait(r)
    LQ = math.log(128 ** -0.5)

    rows_tok = load_rows(0, False)
    xt = transposed(None)
    barrier()
    tables("silu_and_others")
    qkvz = take(24 * 256)
    QT = qkvz.rearrange("p (n m) -> p n m", n=24)
    qbk = take(12 * 256).rearrange("p (n m) -> p n m", n=12)
    vbt = take(1536).rearrange("p (t n) -> p t n", t=2)
    oTf = take(2048)
    oT = oTf.rearrange("p (n m) -> p n m", n=8)
    temp0 = top[0]

    qkv_tok = {}

    def evac_even(c0):
        def f(c, ps, r):
            n = c0 + c
            y = QT[:, n, :]
            if n < 18:
                w = C("gconv")
                r1 = act(y, ps, ACT.Copy, r, scale=w[:, 4 * n + 3:4 * n + 4])
                for s in (1, 2, 3):
                    r1 = stt(y[:, s:256], ps[:, 0:256 - s], w[:, 4 * n + 3 - s:4 * n + 4 - s], y[:, s:256],
                             ALU.mult, ALU.add, r1)
                qkv_tok[n] = act(y, y, ACT.Silu, r1)
                return r1
            qkv_tok[n] = act(y, ps, ACT.Silu, r)
            return qkv_tok[n]
        return f

    for j in range(6):
        proj_T(ins["we"][j], 4, xt, evac_even(4 * j))

    def evac_b(c0):
        def f(c, ps, r):
            n = c0 + c
            if n < 6:
                r = ts(V, qbk[:, n, :], ps, 0.125, None, ALU.mult, None, r)
            else:
                r = cpy(V if n % 2 else A, qbk[:, n, :], ps, r)
            b_tok[n] = r
            return r
        return f

    b_tok = {}
    for j in range(3):
        proj_T(ins["we"][6 + j], 4, xt, evac_b(4 * j))

    def evac_rows(dst, c0, q):
        def f(t, ps, r):
            r = cpy(q, dst[:, t, c0:c0 + ps.shape[1]], ps, r)
            row_tok.append(r)
            return r
        return f

    row_tok = []
    proj_rows(ins["wev"][0], 512, xt, evac_rows(vbt, 0, V))
    proj_rows(ins["wev2"][0], 256, xt, evac_rows(vbt, 512, A))
    b = PS.get()
    wba = C("wba").rearrange("p (k n) -> p k n", k=8)
    for t in range(2):
        for k in range(8):
            r = mm(b.ap[:, 12 * t:12 * t + 12], xT[:, k, t * 128:t * 128 + 128], wba[:, k, :], k == 0, k == 7,
                   b.rel, inc=(k == 7))
    ba = small[:, 0:24].rearrange("p (t n) -> p t n", t=2)
    r = cpy(V, small[:, 0:24], b.ap[:, 0:24], r)
    PS.put(b, r)

    tables("natural_log_exp_and_others")

    def softplus(dst, src, tmp, tok):
        act(tmp, src, ACT.Abs, tok)
        act(tmp, tmp, ACT.Exp, scale=-1.0)
        r = act(tmp, tmp, ACT.Ln, bias=1.0)
        return stt(dst, src, 0.0, tmp, ALU.max, ALU.add, r)

    def cols(a):
        return small[:, a:a + 12]

    def two(ap):
        return ap.rearrange("p (t n) -> p t n", t=2)

    r = act(two(cols(24)), ba[:, :, 0:6], ACT.Exp, r, scale=-1.0)
    r = ts(V, cols(24), cols(24), 1.0, None, ALU.add, None, r)
    r = V(lambda e: e.reciprocal(cols(24), cols(24)))
    r = tt(V, two(cols(96)), ba[:, :, 6:12], bc(R("dtb").rearrange("p (a n) -> p a n", a=1), [128, 2, 6]), ALU.add)
    r = softplus(cols(96), cols(96), cols(108), r)
    e1 = act(small[:, 120:126], R("alog"), ACT.Exp)
    r = stt(two(cols(36)), two(cols(96)), -1.0,
            bc(small[:, 120:126].rearrange("p (a n) -> p a n", a=1), [128, 2, 6]), ALU.mult, ALU.mult, e1)
    b = PS.get()
    mm(b.ap[:, 0:12], K("tri"), cols(36), True, True, r, b.rel)
    rg = mm(b.ap[:, 12:24], ones[:, :], cols(36), True, True, inc=True)
    cpy(V, small[:, 130:154], b.ap[:, 0:24], rg)
    r = cpy(V, cols(48), b.ap[:, 0:12])
    PS.put(b, r)
    ts(V, cols(84), cols(48), -1.0, None, ALU.mult, None)
    r = tt(V, cols(72), small[:, 142:154], cols(48), ALU.subtract)
    act(cols(72), cols(72), ACT.Exp, r)
    r = act(cols(60), cols(48), ACT.Exp)
    gates = tt(V, cols(60), cols(60), cols(24), ALU.mult, r)

    top[0] = temp0
    sS = Pool([take(768) for _ in range(3)])
    sP = Pool([take(768) for _ in range(3)])
    stat = Pool([small[:, 160 + 4 * i:164 + 4 * i] for i in range(6)])
    DM = kc[:, kat["dm0"][0]:kat["dm0"][0] + 768].rearrange("p (g n) -> p g n", g=3)
    o_tok = []
    for h in range(4):
        base = (h % 2) * 64
        ob = PS.get()
        for t in range(2):
            nk = 128 * (t + 1)
            off = 256 - nk
            s = sS.get()
            sv = s.ap[:, 0:3 * nk].rearrange("p (g n) -> p g n", g=3)
            gs = [(0, 3)] if t == 0 else [(0, 2), (2, 3)]
            for g0, g1 in gs:
                b = PS.get()
                for g in range(g0, g1):
                    n = g * 2 + h // 2
                    r = mm(b.ap[:, (g - g0) * nk:(g - g0) * nk + nk], qbk[base:base + 64, n, t * 128:t * 128 + 128],
                           qbk[base:base + 64, 6 + n, 0:nk], True, True, b.rel, b_tok[n], b_tok[6 + n], inc=True)
                r = tt(V, sv[:, g0:g1, :], b.ap[:, 0:(g1 - g0) * nk].rearrange("p (g n) -> p g n", g=g1 - g0),
                       bc(TP[:, h:h + 1, off:256], [128, g1 - g0, nk]), ALU.add, r, s.rel, TPt)
                PS.put(b, r)
            r = tt(V, sv, sv, DM[:, :, off:256], ALU.add)
            sm = stat.get()
            r = V(lambda e, sm=sm, s=s, nk=nk: e.tensor_reduce(sm.ap[:, 0:1], s.ap[:, 0:3 * nk], X, ALU.max, negate=True),
                  sm.rel)
            r = act(s.ap[:, 0:3 * nk], s.ap[:, 0:3 * nk], ACT.Exp, r, bias=sm.ap[:, 0:1], accum_out=sm.ap[:, 1:2])
            V(lambda e, sm=sm: e.reciprocal(sm.ap[:, 2:3], sm.ap[:, 1:2]), r)
            r = ts(V, s.ap[:, 0:3 * nk], s.ap[:, 0:3 * nk], sm.ap[:, 2:3], None, ALU.mult, None)
            stat.put(sm, r)
            p = sP.get()
            nt = 3 * (t + 1)
            for c0 in range(0, nt, 4):
                c1 = min(c0 + 4, nt)
                b = PS.get()
                for c in range(c0, c1):
                    r2 = tp(b.ap[:, (c - c0) * 128:(c - c0) * 128 + 128], s.ap[:, c * 128:c * 128 + 128], r, b.rel,
                            inc=(c == c1 - 1))
                r3 = cpy(A if c0 else V, p.ap[:, c0 * 128:c1 * 128], b.ap[:, 0:(c1 - c0) * 128], r2, p.rel)
                if c0 == 0:
                    r30 = r3
                PS.put(b, r3)
            sS.put(s, r2)
            for c in range(nt):
                g, jt = c // (t + 1), c % (t + 1)
                r = mm(ob.ap[base:base + 64, t * 128:t * 128 + 128], vbt[:, jt, g * 256 + h * 64:g * 256 + h * 64 + 64],
                       p.ap[:, c * 128:c * 128 + 128], c == 0, c == nt - 1, r30, r3, ob.rel, row_tok, inc=(c == nt - 1))
            sP.put(p, r)
        r = cpy(A, oT[base:base + 64, 6 + h // 2, :], ob.ap[base:base + 64, 0:256], r)
        o_tok.append(r)
        PS.put(ob, r)

    swa_end = [q.now() for q in (T, V, A, G)]
    for q in (T, V, A, G):
        q.wait(*swa_end)
    top[0] = temp0
    sq = Pool([take(512) for _ in range(2)])
    for n in range(0, 12, 2):
        pair = qkvz[:, n * 256:n * 256 + 512]
        s = sq.get()
        r = act(s.ap, pair, ACT.Square, s.rel)
        b = PS.get()
        r = mm(b.ap, ones[:, :], s.ap, True, True, r, b.rel, inc=True)
        r1, r2 = inv_sqrt(s.ap, b.ap, 1.0, 1e-6, LQ if n < 6 else None, r)
        PS.put(b, r1)
        r = tt(V, pair, pair, s.ap, ALU.mult, r2)
        sq.put(s, r)
    l2 = r
    top[0] = temp0
    Sst = take(768)

    def bufs():
        return {k: take(384) for k in ("a", "b", "DT", "EG", "LT", "QK", "E", "D", "L", "kbe", "kd", "vb")}

    sets = [bufs()]
    M3 = [128, 3, 128]

    def v3(ap):
        return ap.rearrange("p (h n) -> p h n", h=3)

    def k3(name):
        return bc(K(name).rearrange("p (a n) -> p a n", a=1), M3)

    def col3(a, n):
        return bc(small[:, a + n:a + n + 3].rearrange("p (n a) -> p n a", a=1), M3)

    T.wait(l2)
    for t in range(2):
        for hg in range(2):
            u = sets[0]
            n0 = 6 * t + 3 * hg
            hs = range(3 * hg, 3 * hg + 3)
            tk = slice(t * 128, t * 128 + 128)

            def three(l, r, toks, acc=None):
                b = PS.get()
                for i in range(3):
                    a1, b1 = l(i), r(i)
                    k = mm(b.ap[:, i * 128:i * 128 + 128], a1, b1, True, acc is None, toks, b.rel, inc=(i == 2))
                    if acc is not None:
                        k = mm(b.ap[:, i * 128:i * 128 + 128], acc[0](i), acc[1](i), False, True, toks, inc=(i == 2))
                return b, k

            def cs(ap):
                return lambda i: ap[:, i * 128:i * 128 + 128]

            r = cpy(V, v3(u["a"]), col3(36, n0), T.now())
            b, k = three(cs(u["a"]), lambda i: K("tri"), r)
            B = b.ap[:, 0:384]
            r = cpy(V, v3(u["b"]), col3(24, n0))
            b2, k2 = three(cs(u["b"]), lambda i: ident, r)
            r = tt(V, v3(u["DT"]), v3(B), k3("cmt"), ALU.add, k)
            re = act(u["EG"], B, ACT.Exp, r)
            PS.put(b, re)
            for i in range(3):
                r = act(u["DT"][:, i * 128:i * 128 + 128], u["DT"][:, i * 128:i * 128 + 128], ACT.Exp,
                        bias=small[:, 84 + n0 + i:85 + n0 + i])
            r2 = tt(V, u["LT"], u["DT"], b2.ap[:, 0:384], ALU.mult, r, k2)
            PS.put(b2, r2)
            b, k = three(lambda i: QT[:, 6 + 3 * hg + i, tk], lambda i: QT[:, 6 + 3 * hg + i, tk], None)
            b2, k2 = three(lambda i: QT[:, 6 + 3 * hg + i, tk], lambda i: QT[:, 3 * hg + i, tk], None)
            r = tt(V, u["LT"], u["LT"], b.ap[:, 0:384], ALU.mult, k)
            PS.put(b, r)
            r = tt(V, u["QK"], u["DT"], b2.ap[:, 0:384], ALU.mult, k2)
            PS.put(b2, r)
            tt(V, v3(u["E"]), v3(u["LT"]), k3("m1"), ALU.mult)
            r = tt(V, v3(u["E"]), k3("ident"), v3(u["E"]), ALU.subtract)

            def flip(src, toks):
                b = PS.get()
                for i in range(3):
                    k = tp(b.ap[:, i * 128:i * 128 + 128], src(i), toks, b.rel, inc=(i == 2))
                return b, k

            b, k = flip(cs(u["E"]), r)
            r = cpy(A, u["D"], b.ap[:, 0:384], k)
            PS.put(b, r)
            b, k = flip(lambda i: QT[:, 6 + 3 * hg + i, tk], None)
            r1 = tt(V, v3(u["kbe"]), v3(b.ap[:, 0:384]), col3(60, n0), ALU.mult, k)
            r1 = tt(V, v3(u["kd"]), v3(b.ap[:, 0:384]), col3(72, n0), ALU.mult)
            PS.put(b, r1)
            b, k = flip(lambda i: QT[:, 12 + 3 * hg + i, tk], None)
            r1 = tt(V, v3(u["vb"]), v3(b.ap[:, 0:384]), col3(24, n0), ALU.mult, k)
            PS.put(b, r1)
            rD = r
            for s in (2, 4, 8, 16, 32, 64):
                r = tt(V, v3(u["L"]), v3(u["LT"]), k3(f"m{s}"), ALU.mult, T.now())
                b, k = three(cs(u["L"]), cs(u["D"]), [r, rD])
                r = cpy(A, u["a"], b.ap[:, 0:384], k)
                PS.put(b, r)
                b2, k2 = three(cs(u["a"]), cs(u["E"]), r)
                if s < 64:
                    b, k = three(cs(u["E"]), cs(u["a"]), r)
                r = tt(V, u["E"], u["E"], b2.ap[:, 0:384], ALU.subtract, k2, T.now())
                PS.put(b2, r)
                if s < 64:
                    rD = tt(V, u["D"], u["D"], b.ap[:, 0:384], ALU.subtract, k)
                    PS.put(b, rD)
            E = u["E"]
            if t == 0:
                b, k = three(cs(E), cs(u["vb"]), r)
                r = cpy(V, u["a"], b.ap[:, 0:384], k)
                PS.put(b, r)
                delta = u["a"]
                b, k = three(cs(u["kd"]), cs(delta), r)
                rS = cpy(A, Sst[:, hg * 384:hg * 384 + 384], b.ap[:, 0:384], k)
                PS.put(b, rS)
                b, k = three(cs(delta), cs(u["QK"]), r)
            else:
                b, k = three(cs(u["kbe"]), cs(E), r)
                r = ts(V, u["b"], b.ap[:, 0:384], -1.0, None, ALU.mult, None, k)
                PS.put(b, r)
                Sg = Sst[:, hg * 384:hg * 384 + 384]
                b, k = three(cs(E), cs(u["vb"]), [r, A.now()], (cs(u["b"]), cs(Sg)))
                r = cpy(V, u["a"], b.ap[:, 0:384], k)
                PS.put(b, r)
                delta = u["a"]
                r2 = tt(V, v3(u["EG"]), v3(u["EG"]), QT[:, 3 * hg:3 * hg + 3, tk], ALU.mult, A.now())
                b, k = three(cs(delta), cs(u["QK"]), r2, (cs(Sg), cs(u["EG"])))
            r = cpy(V, oT[:, 3 * hg:3 * hg + 3, tk], v3(b.ap[:, 0:384]), k)
            PS.put(b, r)

    def rms_out(o, g, w, sz, tmp, tok):
        r = act(tmp[:, 0:sz], o, ACT.Square, tok)
        b = PS.get()
        r = mm(b.ap[:, 0:sz], ones[:, :], tmp[:, 0:sz], True, True, r, b.rel, inc=True)
        r1, r2 = inv_sqrt(tmp[:, 0:sz], b.ap[:, 0:sz], 1.0 / 128, 1e-6, None, r)
        PS.put(b, r1)
        tt(V, o, o, tmp[:, 0:sz], ALU.mult, r2)
        return stt(o, o, w, g, ALU.mult, ALU.mult)

    for n in range(3):
        r = rms_out(oTf[:, n * 512:n * 512 + 512], qkvz[:, (18 + 2 * n) * 256:(20 + 2 * n) * 256], C("gnw"), 512,
                    sets[0]["DT"] if False else arena[:, temp0 + 768:temp0 + 1280], [r, T.now()])
    banks, k = down([ins["woe"][0], ins["woe"][1]], oT, [r] + o_tok)
    lt = norm(banks, k, rows_tok, False)

    def ffn(l, ln_i, tok):
        rows = load_rows(ln_i, False, tok)
        xt = transposed(tok)
        barrier()
        tables("silu_and_others")
        gT = take(22 * 256).rearrange("p (n m) -> p n m", n=22)
        yg = Pool([take(512) for _ in range(6)])
        wv = C(f"fw{l}")
        bv = C(f"fb{l}")
        last = [None]
        for j in range(11):
            ys = []

            def f(c, ps, r, j=j, ys=ys):
                n = 2 * j + c if c < 2 else 22 + 2 * j + c - 2
                if c < 2:
                    buf = yg.get()
                    ys.append(buf)
                    y = buf.ap[:, 0:256]
                else:
                    buf = ys[c - 2]
                    y = buf.ap[:, 256:512]
                r = act(y, ps, ACT.Identity, r, buf.rel, scale=wv[:, 3 * n + 2:3 * n + 3], bias=bv[:, n:n + 1])
                for s in (1, 2):
                    r = stt(y[:, s:256], ps[:, 0:256 - s], wv[:, 3 * n + 2 - s:3 * n + 3 - s], y[:, s:256],
                            ALU.mult, ALU.add, r)
                if c < 2:
                    act(y, y, ACT.Silu, r)
                else:
                    g = 2 * j + c - 2
                    last[0] = tt(G, gT[:, g, :], buf.ap[:, 0:256], y, ALU.mult, r, A.now())
                    yg.put(buf, last[0])
                return r

            proj_T(ins[f"wu{l}"][j], 4, xt, f)
        banks, k = down([ins[f"wd{l}"][i] for i in range(5)] + [ins[f"wdl{l}"][0]], gT, last[0])
        return norm(banks, k, rows, False)

    lt = ffn(0, 1, lt)

    rows_tok = load_rows(2, False, lt)
    xt = transposed(lt)
    barrier()
    qc = take(2048).rearrange("p (n m) -> p n m", n=8)
    gl = take(1024)
    glv = gl.rearrange("p (n m) -> p n m", n=4)
    rT = take(1024).rearrange("p (n m) -> p n m", n=4)
    vc = take(1024).rearrange("p (t n) -> p t n", t=2)
    vd = take(1024).rearrange("p (t n) -> p t n", t=2)
    oTf = take(2048)
    oT = oTf.rearrange("p (n m) -> p n m", n=8)
    TC = take(1024).rearrange("p (h n) -> p h n", h=4)
    gdT = take(256)
    la = take(512)
    Bc = take(512)
    pT = {}

    def evac_odd(c0):
        def f(c, ps, r):
            n = c0 + c
            if n < 8:
                r = ts(V, qc[:, n, :], ps, 0.125, None, ALU.mult, None, r) if n < 4 else cpy(A, qc[:, n, :], ps, r)
            elif n < 12:
                m = n - 8
                r = ts(V, glv[:, m, :], ps, 0.125, None, ALU.mult, None, r) if m < 2 else cpy(A, glv[:, m, :], ps, r)
            else:
                r = act(rT[:, n - 12, :], ps, ACT.Silu, r)
            pT[n] = r
            return r
        return f

    for j in range(4):
        proj_T(ins["wo"][j], 4, xt, evac_odd(4 * j))
    tables("natural_log_exp_and_others")
    row_tok = []
    proj_rows(ins["wov"][0], 512, xt, evac_rows(vc, 0, V))
    proj_rows(ins["wov"][1], 512, xt, evac_rows(vd, 0, A))
    wgd = C("wgd").rearrange("p (k n) -> p k n", k=8)
    b = PS.get()
    for k in range(8):
        r = mm(b.ap[0:16, 0:256], wgd[:, k, :], xT[:, k, :], k == 0, k == 7, b.rel, xt, inc=(k == 7))
    r = cpy(V, gdT[0:16, :], b.ap[0:16, 0:256], r)
    PS.put(b, r)
    lwg = C("lwg")
    b = PS.get()
    for m in range(2):
        k = mm(b.ap[:, m * 256:m * 256 + 256], lwg[0:16, m * 128:m * 128 + 128], gdT[0:16, :], True, True, r, b.rel,
               inc=(m == 1))
    for m in range(2):
        r = ts(V, la[:, m * 256:m * 256 + 256], b.ap[:, m * 256:m * 256 + 256], C("lbg", m, m + 1), -1.0,
               ALU.add, ALU.mult, k)
    PS.put(b, r)
    r = softplus(la, la, Bc, r)
    r = ts(V, la, la, -1.0 / 16, None, ALU.mult, None)
    for i in range(4):
        s = slice(i * 128, i * 128 + 128)
        V(lambda e, s=s: e.tensor_tensor_scan(Bc[:, s], ones[:, :], la[:, s], 0.0, ALU.mult, ALU.add))
    tt(V, small[0:64, 200:202], C("dl")[0:64, 0:4:2], C("dl")[0:64, 1:4:2], ALU.mult)
    b = PS.get()
    r = mm(b.ap[:, 0:2], ones[0:64, :], small[0:64, 200:202], True, True, V.now(), b.rel, inc=True)
    r = act(small[:, 202:204], b.ap[:, 0:2], ACT.Exp, r)
    PS.put(b, r)
    tt(V, small[:, 204:205], small[:, 203:204], small[:, 202:203], ALU.subtract, r)
    ts(V, small[:, 205:206], small[:, 204:205], -LAM0, None, ALU.add, None)
    ts(V, small[:, 206:207], C("dnw"), 1.0 - LAM0, None, ALU.mult, None)
    r = tt(V, TC, TP, bc(K("cm").rearrange("p (a n) -> p a n", a=1), [128, 4, 256]), ALU.add)
    temp1 = top[0]
    sS = Pool([take(512) for _ in range(3)])
    sP = Pool([take(256) for _ in range(2)])
    stat = Pool([small[:, 160 + 6 * i:166 + 6 * i] for i in range(4)])
    for h in range(4):
        ob = PS.get()
        for t in range(2):
            nk = 128 * (t + 1)
            off = 256 - nk
            s = sS.get()
            sv = s.ap[:, 0:2 * nk].rearrange("p (c n) -> p c n", c=2)
            two_b = [PS.get(), PS.get()]
            for c in range(2):
                b = two_b[c]
                r = mm(b.ap[:, 0:nk], qc[c * 64:c * 64 + 64, h, t * 128:t * 128 + 128],
                       qc[c * 64:c * 64 + 64, 4 + h, 0:nk], True, True, b.rel, pT[h], pT[4 + h], inc=True)
                r = tt(V, sv[:, c, :], b.ap[:, 0:nk], TC[:, h, off:256], ALU.add, r, s.rel)
                PS.put(b, r)
            sm = stat.get()
            r = V(lambda e, sm=sm, sv=sv: e.tensor_reduce(sm.ap[:, 0:2], sv, X, ALU.max, negate=True), sm.rel)
            for c in range(2):
                r = act(s.ap[:, c * nk:c * nk + nk], s.ap[:, c * nk:c * nk + nk], ACT.Exp, r,
                        bias=sm.ap[:, c:c + 1], accum_out=sm.ap[:, 2 + c:3 + c])
            V(lambda e, sm=sm: e.reciprocal(sm.ap[:, 4:6], sm.ap[:, 2:4]), r)
            ts(V, sm.ap[:, 5:6], sm.ap[:, 5:6], small[:, 205:206], None, ALU.mult, None)
            ts(V, s.ap[:, 0:nk], s.ap[:, 0:nk], sm.ap[:, 4:5], None, ALU.mult, None)
            r = stt(s.ap[:, 0:nk], s.ap[:, nk:2 * nk], sm.ap[:, 5:6], s.ap[:, 0:nk], ALU.mult, ALU.add)
            stat.put(sm, r)
            b = PS.get()
            for j in range(t + 1):
                r2 = tp(b.ap[:, j * 128:j * 128 + 128], s.ap[:, j * 128:j * 128 + 128], r, b.rel, inc=(j == t))
            sS.put(s, r2)
            p = sP.get()
            r3 = cpy(A, p.ap[:, 0:nk], b.ap[:, 0:nk], r2, p.rel)
            PS.put(b, r3)
            for j in range(t + 1):
                r = mm(ob.ap[:, t * 128:t * 128 + 128], vc[:, j, h * 128:h * 128 + 128], p.ap[:, j * 128:j * 128 + 128],
                       j == 0, j == t, r3, ob.rel, row_tok, inc=(j == t))
            sP.put(p, r)
        r = cpy(V, oT[:, h, :], ob.ap[:, 0:256], r)
        PS.put(ob, r)
        dtok = r
    b_end = [q.now() for q in (T, V, A, G)]
    for q in (T, V, A, G):
        q.wait(*b_end)
    top[0] = temp1
    tmp = take(512)
    for n in range(2):
        o = oTf[:, n * 512:n * 512 + 512]
        r = act(tmp, o, ACT.Square, V.now())
        b = PS.get()
        r = mm(b.ap, ones[:, :], tmp, True, True, r, b.rel, inc=True)
        r1, r2 = inv_sqrt(tmp, b.ap, 1.0 / 128, 1e-6, None, r)
        PS.put(b, r1)
        stt(o, o, small[:, 206:207], tmp, ALU.mult, ALU.mult, r2)
    qs = Pool([take(512) for _ in range(2)])
    ks = Pool([take(512) for _ in range(2)])
    ee = Pool([take(512) for _ in range(2)])
    acc = [take(512) for _ in range(2)]
    mt = [take(512) for _ in range(2)]
    qd = take(256).rearrange("p (n m) -> p n m", n=2)
    kdT = take(256).rearrange("p (n m) -> p n m", n=2)
    kdt = take(256).rearrange("p (n m) -> p n m", n=2)
    Sg = take(256).rearrange("p (n m) -> p n m", n=2)
    q4 = gl[:, 0:512]
    k4 = gl[:, 512:1024]
    B4 = Bc.rearrange("p (n m) -> p n m", n=4)
    Btok = V.now()
    A.wait(Btok)
    acc_tok = [None, None]
    for li, s in enumerate((0, 1, 2, 4, 8, 16, 32, 64)):
        if s == 0:
            qv, kv, rr = q4, k4, [pT[8], pT[9], pT[10], pT[11]]
        else:
            qb, kb, eb = qs.get(), ks.get(), ee.get()
            z1 = G(lambda e, qb=qb: e.memset(qb.ap, 0.0), qb.rel)
            z2 = G(lambda e, kb=kb: e.memset(kb.ap, 0.0), kb.rel)
            nb = 256 // s

            def blocks(ap):
                return ap.rearrange("p (b n) -> p b n", n=2 * s)

            ref = blocks(Bc)[:, :, s - 1:s]
            ev = eb.ap.rearrange("p (w b n) -> p w b n", w=2, n=s)
            tt(V, ev[:, 0], blocks(Bc)[:, :, s:2 * s], bc(ref, [128, nb, s]), ALU.subtract, eb.rel)
            r = tt(V, ev[:, 1], bc(ref, [128, nb, s]), blocks(Bc)[:, :, 0:s], ALU.subtract)
            r = act(eb.ap, eb.ap, ACT.Exp, r)
            tt(V, blocks(qb.ap)[:, :, s:2 * s], blocks(q4)[:, :, s:2 * s], ev[:, 0], ALU.mult, r, z1, z2)
            rr = tt(V, blocks(kb.ap)[:, :, 0:s], blocks(k4)[:, :, 0:s], ev[:, 1], ALU.mult)
            ee.put(eb, rr)
            qv, kv = qb.ap, kb.ap
        mask = bc(K("ident" if s == 0 else f"m{s}").rearrange("p (a n) -> p a n", a=1), [128, 2, 128])
        for t in range(2):
            dst = (acc[t] if s == 0 else mt[t]).rearrange("p (m a n) -> p m a n", m=2, a=2)
            for a in range(2):
                b = PS.get()
                for m in range(2):
                    seg = 2 * m + t
                    k = mm(b.ap[:, m * 128:m * 128 + 128], kv[64 * a:64 * a + 64, seg * 128:seg * 128 + 128],
                           qv[64 * a:64 * a + 64, seg * 128:seg * 128 + 128], True, True, rr, b.rel, inc=(m == 1))
                r = tt(V, dst[:, :, a, :], b.ap[:, 0:256].rearrange("p (m n) -> p m n", m=2), mask, ALU.mult, k,
                       None if s == 0 else acc_tok[t])
                PS.put(b, r)
            acc_tok[t] = r if s == 0 else tt(G, acc[t], acc[t], mt[t], ALU.add, r)
        if s:
            qs.put(qb, k)
            ks.put(kb, k)
    Bq = Bc.rearrange("p (n t m) -> p n t m", n=2, t=2)
    r = act(qd, Bq[:, :, 1, :], ACT.Exp)
    tt(V, qd, qd, gl[:, 0:512].rearrange("p (n t m) -> p n t m", n=2, t=2)[:, :, 1, :], ALU.mult, r)
    r = tt(V, kdT, bc(Bq[:, :, 0, 127:128], [128, 2, 128]), Bq[:, :, 0, :], ALU.subtract)
    r = act(kdT, kdT, ACT.Exp, r)
    r = tt(V, kdT, kdT, gl[:, 512:1024].rearrange("p (n t m) -> p n t m", n=2, t=2)[:, :, 0, :], ALU.mult, r)
    b = PS.get()
    for m in range(2):
        k = tp(b.ap[:, m * 128:m * 128 + 128], kdT[:, m, :], r, b.rel, inc=(m == 1))
    r = cpy(V, kdt, b.ap[:, 0:256].rearrange("p (n m) -> p n m", n=2), k)
    PS.put(b, r)
    b = PS.get()
    for h in range(4):
        base = (h % 2) * 64
        k = mm(b.ap[base:base + 64, (h // 2) * 128:(h // 2) * 128 + 128], kdt[:, h // 2, base:base + 64],
               vd[:, 0, h * 128:h * 128 + 128], True, True, r, b.rel, row_tok, inc=(h == 3))
    r = cpy(V, Sg, b.ap[:, 0:256].rearrange("p (n m) -> p n m", n=2), k)
    PS.put(b, r)
    for h in range(4):
        base = (h % 2) * 64
        b = PS.get()
        mm(b.ap[:, 0:128], vd[:, 0, h * 128:h * 128 + 128], acc[0][:, h * 128:h * 128 + 128], True, True,
           acc_tok[0], acc_tok[1], b.rel, r)
        mm(b.ap[:, 128:256], vd[:, 1, h * 128:h * 128 + 128], acc[1][:, h * 128:h * 128 + 128], True, False)
        k = mm(b.ap[:, 128:256], Sg[base:base + 64, h // 2, :], qd[base:base + 64, h // 2, :], False, True, inc=True)
        r2 = cpy(V, oT[:, 4 + h, :], b.ap[:, 0:256], k)
        PS.put(b, r2)
    for n in range(2):
        r = rms_out(oTf[:, 1024 + n * 512:1536 + n * 512], rT.rearrange("p n m -> p (n m)")[:, n * 512:n * 512 + 512],
                    C("lnw"), 512, tmp, [V.now()])
    banks, k = down([ins["woo"][0], ins["woo"][1]], oT, r)
    lt = norm(banks, k, rows_tok, False)
    lt = ffn(1, 3, lt)

    def adaln(i):
        tables("silu_and_others")
        sc = small[:, 210:218]
        r = act(sc, C("c"), ACT.Silu, T.now())
        scb = take(1024).rearrange("p (k n) -> p k n", k=8)
        r = cpy(V, scb, bc(sc.rearrange("p (k a) -> p k a", a=1), [128, 8, 128]), r)
        b = PS.get()
        for j in range(4):
            view, arrived, slot = load(ins["ada"][6 * i + j], 8)
            for c in range(4):
                for k in range(8):
                    m = mm(b.ap[:, 4 * j + c:4 * j + c + 1], view[:, k, c * 128:c * 128 + 128], sc[:, k:k + 1],
                           k == 0, k == 7, arrived, r, b.rel, inc=(k == 7))
            done(slot, m)
        m = tt(V, mods[:, 0:16], b.ap[:, 0:16], C("adab", 16 * i, 16 * i + 16), ALU.add, m)
        PS.put(b, m)
        mod_tok = ts(V, mods[:, 8:16], mods[:, 8:16], 1.0, None, ALU.add, None)
        for j in range(2):
            view, arrived, slot = load(ins["ada"][6 * i + 4 + j], 8)
            b = PS.get()
            for k in range(8):
                m = mm(b.ap, scb[:, k, :], view[:, k, :], k == 0, k == 7, arrived, b.rel, inc=(k == 7))
            done(slot, m)
            m = stt(gate[:, j * 512:j * 512 + 512], b.ap, 1.0, gbr[:, j * 512:j * 512 + 512], ALU.add, ALU.add, m, rows_tok)
            PS.put(b, m)
        return mod_tok

    rows_tok = load_rows(4, True, lt)
    barrier()
    tmpn = take(512)
    mod_tok = adaln(0)
    xt = transposed(lt, (mods, mod_tok))
    qk = take(16 * 256).rearrange("p (n m) -> p n m", n=16)
    vs = take(2048).rearrange("p (t n) -> p t n", t=2)
    oT = take(2048).rearrange("p (n m) -> p n m", n=8)
    tables("natural_log_exp_and_others")
    pT = {}

    def evac_sb(c0):
        def f(c, ps, r):
            n = c0 + c
            r = ts(V, qk[:, n, :], ps, 0.125, None, ALU.mult, None, r) if n < 8 else cpy(A, qk[:, n, :], ps, r)
            pT[n] = r
            return r
        return f

    for j in range(4):
        proj_T(ins["ws"][j], 4, xt, evac_sb(4 * j))
    row_tok = []
    for j in range(2):
        proj_rows(ins["ws"][4 + j], 512, xt, evac_rows(vs, 512 * j, A if j else V))
    az = Pool([take(384) for _ in range(4)])
    sp = Pool([take(384) for _ in range(4)])

    def diag(ap):
        return ap.rearrange("p (n m) -> p n m", n=3)[:, 0:3:2, :]

    sb_tok = []
    for h0 in range(0, 16, 4):
        st = []
        for h in range(h0, h0 + 4):
            base, n = (h % 2) * 64, h // 2
            b = PS.get()
            kk, qq = qk[base:base + 64, 8 + n, :], qk[base:base + 64, n, :]
            mm(b.ap[:, 0:256], kk[:, 0:128], qq, True, False, b.rel, pT[n], pT[8 + n])
            r = mm(b.ap[:, 256:384], kk[:, 128:256], qq[:, 128:256], False, False, inc=True)
            st.append([h, b, r])
        for e in st:
            h, b, r = e
            a, s = az.get(), sp.get()
            z = b.ap[:, 0:384]
            act(a.ap, z, ACT.Abs, r, a.rel)
            act(a.ap, a.ap, ACT.Exp, scale=-1.0)
            r = act(a.ap, a.ap, ACT.Ln, bias=1.0)
            r = stt(s.ap, z, 0.0, a.ap, ALU.max, ALU.add, r, s.rel)
            r = G(lambda e, s=s: e.affine_select(out=diag(s.ap), in_=diag(s.ap), compare_op=ALU.is_gt, fill=0.0, base=0,
                                                 pattern=[[0, 2], [1, 128]], channel_multiplier=-1), r)
            e += [a, s, r]
        for e in st:
            h, b, _, a, s, r = e
            mm(b.ap[:, 0:256], K("ntri"), s.ap[:, 0:256], False, False, r)
            mm(b.ap[:, 128:256], neg1[:, :], s.ap[:, 256:384], False, False)
            k = mm(b.ap[:, 256:384], K("ntri"), s.ap[:, 256:384], False, True, inc=True)
            sp.put(s, k)
            r = act(a.ap, b.ap[:, 0:384], ACT.Exp, k)
            PS.put(b, r)
            r = G(lambda e, a=a: e.affine_select(out=diag(a.ap), in_=diag(a.ap), compare_op=ALU.is_gt, fill=0.0, base=0,
                                                 pattern=[[0, 2], [1, 128]], channel_multiplier=-1), r)
            e.append(r)
        for e in st:
            h, b, _, a, s, _, r = e
            base, n = (h % 2) * 64, h // 2
            b = PS.get()
            o = b.ap[base:base + 64, :]
            mm(o[:, 0:256], vs[:, 0, h * 64:h * 64 + 64], a.ap[:, 0:256], True, False, r, b.rel, row_tok)
            k = mm(o[:, 128:256], vs[:, 1, h * 64:h * 64 + 64], a.ap[:, 256:384], False, True, inc=True)
            az.put(a, k)
            r = cpy(V, oT[base:base + 64, n, :], o[:, 0:256], k)
            PS.put(b, r)
            sb_tok.append(r)
    banks, k = down([ins["wso"][0], ins["wso"][1]], oT, sb_tok)
    lt = norm(banks, k, rows_tok, True)

    def moe(l, i, tok, last=False):
        nonlocal rows_tok, tmpn
        rows_tok = load_rows(4 + i, True, tok)
        barrier()
        tmpn = take(512)
        mod_tok = adaln(i)
        xt = transposed(tok, (mods, mod_tok))
        accv = take(2048).rearrange("p (t n) -> p t n", t=2)
        rw = C("rw").rearrange("p (k n) -> p k n", k=8)
        b = PS.get()
        for t in range(2):
            for k in range(8):
                r = mm(b.ap[:, 16 * t:16 * t + 16], xT[:, k, t * 128:t * 128 + 128], rw[:, k, :], k == 0, k == 7,
                       b.rel, xt, inc=(k == 7))

        def s32(n):
            return small[:, 220 + 32 * n:252 + 32 * n]

        def tv(ap):
            return ap.rearrange("p (t n) -> p t n", t=2)

        def t1(ap, n=16):
            return bc(ap.rearrange("p (t a) -> p t a", a=1), [128, 2, n])

        def g1(ap):
            return bc(ap.rearrange("p (g a) -> p g a", a=1), [128, 8, 4])

        def gv(ap):
            return ap.rearrange("p (g n) -> p g n", n=4)

        def red(o, i, op=ALU.max):
            return V(lambda e: e.tensor_reduce(o, i, X, op))

        L, Pn, Mk, O1, O2, W = (s32(n) for n in range(6))
        q = small[:, 412:560]
        r = tt(V, tv(L), b.ap[:, 0:32].rearrange("p (t n) -> p t n", t=2),
               bc(R("rtb").rearrange("p (a n) -> p a n", a=1), [128, 2, 16]), ALU.add, r)
        PS.put(b, r)
        red(q[:, 0:2], tv(L))
        r = tt(V, tv(Pn), tv(L), t1(q[:, 0:2]), ALU.subtract)
        r = act(Pn, Pn, ACT.Exp, r)
        V(lambda e: e.tensor_reduce(q[:, 2:4], tv(Pn), X, ALU.add), r)
        V(lambda e: e.reciprocal(q[:, 4:6], q[:, 2:4]))
        tt(V, tv(Pn), tv(Pn), t1(q[:, 4:6]), ALU.mult)
        prs = [(0, 1), (0, 2), (0, 3), (1, 2), (1, 3), (2, 3)]
        pr = q[:, 8:56].rearrange("p (g n) -> p g n", n=6)
        for n, (a1, b1) in enumerate(prs):
            tt(V, pr[:, :, n:n + 1], gv(Pn)[:, :, a1:a1 + 1], gv(Pn)[:, :, b1:b1 + 1], ALU.add)
        gsc = q[:, 56:64]
        red(gsc, pr)
        g2 = gsc.rearrange("p (t n) -> p t n", t=2)

        def first(dst, src, width, wts, mx):
            red(mx, src)
            tt(V, dst, src, t1(mx, width), ALU.is_equal)
            tt(V, dst, dst, wts, ALU.mult)
            red(q[:, 72:74], dst)
            return tt(V, dst, dst, t1(q[:, 72:74], width), ALU.is_equal)

        sel = q[:, 64:72]
        first(sel.rearrange("p (t n) -> p t n", t=2), g2, 4, K("g4").rearrange("p (t n) -> p t n", t=2), q[:, 74:76])
        ts(V, sel, sel, 1.0, 1e30, ALU.subtract, ALU.mult)
        tt(V, gv(Mk), gv(L), g1(sel), ALU.add)
        first(tv(O1), tv(Mk), 16, tv(K("e16")), q[:, 76:78])
        stt(Mk, O1, -1e32, Mk, ALU.mult, ALU.add)
        first(tv(O2), tv(Mk), 16, tv(K("e16")), q[:, 78:80])
        r = tt(V, q[:, 80:82], q[:, 78:80], q[:, 76:78], ALU.subtract)
        r = act(q[:, 80:82], q[:, 80:82], ACT.Exp, r)
        ts(V, q[:, 82:84], q[:, 80:82], 1.0, None, ALU.add, None, r)
        V(lambda e: e.reciprocal(q[:, 84:86], q[:, 82:84]))
        tt(V, q[:, 86:88], q[:, 80:82], q[:, 84:86], ALU.mult)
        tt(V, tv(O1), tv(O1), t1(q[:, 84:86]), ALU.mult)
        tt(V, tv(O2), tv(O2), t1(q[:, 86:88]), ALU.mult)
        tt(V, W, O1, O2, ALU.add)
        tables("silu_and_others")
        hp = Pool([take(1024) for _ in range(2)])
        sg = Pool([take(256) for _ in range(3)])
        for e in range(16):
            g, ga, gs_ = load(ins["mg"][l * 16 + e], 8)
            u, ua, us_ = load(ins["mu"][l * 16 + e], 8)
            hb = hp.get()
            hT = hb.ap.rearrange("p (n m) -> p n m", n=4)
            for f in range(4):
                b = PS.get()
                for k in range(8):
                    mm(b.ap[:, 0:256], g[:, k, f * 128:f * 128 + 128], xT[:, k, :], k == 0, k == 7, ga, b.rel, xt)
                for k in range(8):
                    r = mm(b.ap[:, 256:512], u[:, k, f * 128:f * 128 + 128], xT[:, k, :], k == 0, k == 7, ua,
                           inc=(k == 7))
                s = sg.get()
                r1 = act(s.ap, b.ap[:, 0:256], ACT.Silu, r, s.rel)
                hk = tt(V, hT[:, f, :], s.ap, b.ap[:, 256:512], ALU.mult, r1, hb.rel)
                sg.put(s, hk)
                PS.put(b, hk)
            done(gs_, r)
            done(us_, r)
            d, da, ds_ = load(ins["md"][l * 16 + e], 4)
            for t in range(2):
                for c in range(2):
                    b = PS.get()
                    for f in range(4):
                        r = mm(b.ap, hT[:, f, t * 128:t * 128 + 128], d[:, f, c * 512:c * 512 + 512], f == 0, f == 3,
                               da, hk, b.rel, inc=(f == 3))
                    o = accv[:, t, c * 512:c * 512 + 512]
                    w = W[:, 16 * t + e:16 * t + e + 1]
                    if e == 0:
                        v = ts(V, o, b.ap, w, None, ALU.mult, None, r)
                    else:
                        v = stt(o, b.ap, w, o, ALU.mult, ALU.add, r)
                    PS.put(b, v)
            done(ds_, r)
            hp.put(hb, r)
        return norm(accv, v, rows_tok, True, last)

    lt = moe(0, 1, lt)

    rows_tok = load_rows(6, True, lt)
    bar = barrier()
    tmpn = take(512)
    scr_top = top[0]
    mod_tok = adaln(2)
    xt = transposed(lt, (mods, mod_tok))
    qk = take(16 * 256).rearrange("p (n m) -> p n m", n=16)
    gTf = take(16 * 256)
    gT = gTf.rearrange("p (n m) -> p n m", n=16)
    vr = take(4096).rearrange("p (t n) -> p t n", t=2)
    dec = take(2048)
    cs_ = take(512)
    tmpr = Pool([take(512) for _ in range(2)])
    A.wait(*bar)
    A.raw(lambda e: e.dma_start(dec, ins["dec"]).then_inc(s_dec, 16))
    posi = sb("posi", 256, I32)
    A.raw(lambda e: e.dma_start(posi[:, :], ins["pos"].broadcast_to([128, 256])).then_inc(s_dec, 16))
    DEC = (s_dec, 32)
    cosT, sinT = cs_[:, 0:256], cs_[:, 256:512]
    tb = tmpr.get()
    ang, kq = tb.ap[:, 0:256], tb.ap[:, 256:512]
    cpy(V, ang, posi[:, :], DEC)
    ts(V, ang, ang, K("freq"), None, ALU.mult, None)
    ki = posi[:, :]
    C1, C2 = 6.28125, 2 * math.pi - 6.28125
    C2a = float(np.float32(np.round(C2 * 2 ** 20) / 2 ** 20))
    C2b = C2 - C2a
    for dst, shift in ((sinT, 0.0), (cosT, 0.25)):
        ts(V, kq, ang, 1.0 / (2 * math.pi), shift, ALU.mult, ALU.add)
        cpy(V, ki, kq)
        cpy(V, kq, ki)
        stt(dst, kq, -C1, ang, ALU.mult, ALU.add)
        stt(dst, kq, -C2a, dst, ALU.mult, ALU.add)
        stt(dst, kq, -C2b, dst, ALU.mult, ALU.add)
        if shift:
            ts(V, dst, dst, math.pi / 2, None, ALU.add, None)
        r = ts(V, dst, dst, math.pi, -math.pi, ALU.min, ALU.max)
        rc = act(dst, dst, ACT.Sin, r)
    tmpr.put(tb, V.now())
    qtok = {}

    def evac_ret(c0):
        def f(c, ps, r):
            n = c0 + c
            if n >= 16:
                r = act(gT[:, n - 16, :], ps, ACT.Silu, r)
                return r
            tb = tmpr.get()
            raw, t2 = tb.ap[:, 0:256], tb.ap[:, 256:512]
            rel = act(raw, ps, ACT.Copy, r, tb.rel, scale=1.0 if n < 8 else 128 ** -0.5)
            b = PS.get()
            k = mm(b.ap[:, 0:256], K("rot"), raw, True, True, rel, b.rel, inc=True)
            r1 = tt(V, t2, b.ap[:, 0:256], sinT, ALU.mult, k, rc)
            PS.put(b, r1)
            tt(V, raw, raw, cosT, ALU.mult)
            qtok[n] = tt(V, qk[:, n, :], raw, t2, ALU.add)
            tmpr.put(tb, qtok[n])
            return rel
        return f

    for j in range(8):
        proj_T(ins["wr"][j], 4, xt, evac_ret(4 * j))
    row_tok = []
    for j in range(4):
        proj_rows(ins["wrv"][j], 512, xt, evac_rows(vr, 512 * j, A if j % 2 else V))
    tables("natural_log_exp_and_others")
    rtmp = Pool([take(384) for _ in range(2)])
    otmp = Pool([take(512) for _ in range(2)])
    gtok = A.now()
    for h in range(8):
        b = PS.get()
        mm(b.ap[:, 0:256], qk[:, 8 + h, 0:128], qk[:, h, :], True, True, b.rel, qtok[h], qtok[8 + h])
        k = mm(b.ap[:, 256:384], qk[:, 8 + h, 128:256], qk[:, h, 128:256], True, True, inc=True)
        p = rtmp.get()
        tt(V, p.ap[:, 0:256], b.ap[:, 0:256], dec[:, h * 256:h * 256 + 256], ALU.mult, k, p.rel, DEC)
        r = tt(V, p.ap[:, 256:384], b.ap[:, 256:384], dec[:, h * 256:h * 256 + 128], ALU.mult)
        PS.put(b, r)
        b = PS.get()
        for d in range(2):
            c = h * 256 + d * 128
            mm(b.ap[:, d * 256:d * 256 + 256], vr[:, 0, c:c + 128], p.ap[:, 0:256], True, False, r, b.rel, row_tok)
            k = mm(b.ap[:, d * 256 + 128:d * 256 + 256], vr[:, 1, c:c + 128], p.ap[:, 256:384], False, True, inc=True)
        rtmp.put(p, k)
        o = otmp.get()
        r = cpy(A, o.ap, b.ap, k, o.rel)
        PS.put(b, r)
        b = PS.get()
        mm(b.ap[:, 0:256], ones[:, :], o.ap[:, 0:256], True, False, r, b.rel)
        k = mm(b.ap[:, 0:256], ones[:, :], o.ap[:, 256:512], False, True, inc=True)
        for d in range(2):
            r = stt(o.ap[:, d * 256:d * 256 + 256], b.ap[:, 0:256], -1.0 / 256, o.ap[:, d * 256:d * 256 + 256],
                    ALU.mult, ALU.add, k)
        PS.put(b, r)
        tb = tmpr.get()
        r = act(tb.ap, o.ap, ACT.Square, r, tb.rel)
        b = PS.get()
        mm(b.ap[:, 0:256], ones[:, :], tb.ap[:, 0:256], True, False, r, b.rel)
        k = mm(b.ap[:, 0:256], ones[:, :], tb.ap[:, 256:512], False, True, inc=True)
        r1, r2 = inv_sqrt(tb.ap[:, 0:256], b.ap[:, 0:256], 1.0 / 256, 1e-5, None, k)
        PS.put(b, r1)
        for d in range(2):
            od = o.ap[:, d * 256:d * 256 + 256]
            tt(V, od, od, tb.ap[:, 0:256], ALU.mult, r2)
            r = stt(gT[:, 2 * h + d, :], od, C("rgn", 2 * h + d, 2 * h + d + 1), gT[:, 2 * h + d, :],
                    ALU.mult, ALU.mult, gtok)
        tmpr.put(tb, r)
        otmp.put(o, r)
    banks, k = down([ins["wro"][j] for j in range(4)], gT, r)
    lt = norm(banks, k, rows_tok, True)
    moe(1, 3, lt, True)
    A.wait((s_out, 32))
    A.wait(*[q.now() for q in (T, V, G)])

    block = ctx.enter_context(nc.Block())

    @block.tensor
    def _(e):
        for f in T.ops:
            f(e)

    @block.vector
    def _(e):
        for f in V.ops:
            f(e)

    @block.scalar
    def _(e):
        for f in A.ops:
            f(e)

    @block.gpsimd
    def _(e):
        for f in G.ops:
            f(e)

    @block.sync
    def _(e):
        for f in S.ops:
            f(e)


def kernel(**inputs):
    import numpy as _np
    import concourse.bacc as _bacc
    from concourse import mybir as _mybir
    from concourse.bass_utils import run_bass_kernel_spmd as _run

    a = {k: _np.ascontiguousarray(v) for k, v in inputs.items()}

    def tiles(w, kt, cols):
        n = w.shape[1] // cols
        return w.reshape(kt, 128, n, cols).transpose(2, 1, 0, 3).reshape(n, 128, kt * cols)

    def rowtiles(w, kt):
        n = w.shape[0] // (kt * 128)
        return w.reshape(n, kt, 128, w.shape[1]).transpose(0, 2, 1, 3).reshape(n, 128, kt * w.shape[1])

    def col(v, n):
        v = v.reshape(-1, n, 128)
        return v.transpose(2, 1, 0).reshape(128, -1)

    def pad(v):
        return _np.concatenate([v, _np.zeros((128 - v.shape[0], v.shape[1]), v.dtype)])

    we, wo = a["w_in_even"][0], a["w_in_odd"][0]
    ins = {"x": a["x"][0]}
    ins["we"] = tiles(_np.concatenate([we[:, 0:3072], we[:, 3084:4620]], 1), 8, 512)
    ins["wev"] = tiles(we[:, 4620:5132], 8, 512)
    ins["wev2"] = tiles(we[:, 5132:5388], 8, 256)
    ins["woe"] = rowtiles(a["w_out_even"][0], 4)
    ins["woo"] = rowtiles(a["w_out_odd"][0], 4)
    ins["wo"] = tiles(_np.concatenate([wo[:, 0:1024], wo[:, 1536:2048], wo[:, 2560:3072]], 1), 8, 512)
    ins["wov"] = tiles(_np.concatenate([wo[:, 1024:1536], wo[:, 2048:2560]], 1), 8, 512)
    for l in range(2):
        u = a["ffn_w_up"][l].reshape(1024, 2, 11, 256).transpose(0, 2, 1, 3).reshape(1024, 5632)
        ins[f"wu{l}"] = tiles(u, 8, 512)
        d = a["ffn_w_down"][l]
        ins[f"wd{l}"] = rowtiles(d[0:2560], 4)
        ins[f"wdl{l}"] = rowtiles(d[2560:2816], 2)
    ins["ada"] = _np.concatenate([tiles(w, 8, 512) for w in a["ada_w_2"].reshape(4, 1024, 3072)])
    ins["ws"] = tiles(a["sb_w_in_2"][0], 8, 512)
    ins["wso"] = rowtiles(a["sb_w_out_2"][0], 4)
    wr = a["ret_w_in_2"][0]
    ins["wr"] = tiles(_np.concatenate([wr[:, 0:2048], wr[:, 4096:6144]], 1), 8, 512)
    ins["wrv"] = tiles(wr[:, 2048:4096], 8, 512)
    ins["wro"] = rowtiles(a["ret_w_out_2"][0], 4)
    ins["mg"] = _np.concatenate([tiles(w, 8, 512) for w in a["moe_w_gate_2"].reshape(32, 1024, 512)])
    ins["mu"] = _np.concatenate([tiles(w, 8, 512) for w in a["moe_w_up_2"].reshape(32, 1024, 512)])
    ins["md"] = _np.concatenate([rowtiles(w, 4) for w in a["moe_w_down_2"].reshape(32, 512, 1024)])
    adab = a["ada_b_2"].reshape(4, 3072)
    par = {
        "gconv": col(a["gdn_conv_w"][0], 18), "fw0": col(a["ffn_conv_w"][0], 44), "fb0": col(a["ffn_conv_b"][0], 44),
        "fw1": col(a["ffn_conv_w"][1], 44), "fb1": col(a["ffn_conv_b"][1], 44), "gnw": col(a["gdn_norm_w"][0], 1),
        "dnw": col(a["diff_norm_w"][0], 1), "lnw": col(a["gla_norm_w"][0], 1), "lbg": col(a["gla_b_gate"][0], 2),
        "rgn": col(a["ret_gn_g_2"][0], 16), "adab": _np.concatenate([col(b[0:2048], 16) for b in adab], 1),
        "c": col(a["c_2"][0], 8), "dl": pad(a["diff_lambda"][0].T), "rb": pad(a["rel_bias"]),
        "lwg": pad(a["gla_w_gate"][0]), "rw": tiles(a["router_w_2"], 8, 16)[0],
        "wba": tiles(we[:, 3072:3084], 8, 12)[0], "wgd": tiles(wo[:, 3072:3088], 8, 16)[0],
    }
    assert all(par[n].shape == (128, w) for n, w in PARAMS), {n: par[n].shape for n, _ in PARAMS}
    ins["cp"] = _np.concatenate([par[n] for n, _ in PARAMS], 1)
    ins["rp"] = _np.concatenate([a["gdn_a_log"][0], a["gdn_dt_bias"][0], a["router_b_2"]])[None, :]
    g1, b1 = a["ln_g"].reshape(4, 1024), a["ln_b"].reshape(4, 1024)
    g2, b2 = a["ln_g_2"].reshape(4, 1024), a["ln_b_2"].reshape(4, 1024)
    rows = []
    for i in range(4):
        rows += [g1[i], b1[i], b1[i]]
    for i in range(4):
        rows += [g2[i], b2[i], adab[i, 2048:]]
    ins["rows"] = _np.stack(rows)
    ins["kc"], _, ins["dec"] = consts()
    ins["pos"] = a["positions_2"]

    nc = _bacc.Bacc("TRN2", target_bir_lowering=False, num_devices=1)
    arrays, args = {}, {}
    for name, v in ins.items():
        v = _np.ascontiguousarray(v)
        arrays[f"in_{name}"] = v
        args[name] = nc.dram_tensor(f"in_{name}", v.shape, _mybir.dt.from_np(v.dtype), kind="ExternalInput").ap()
    out = nc.dram_tensor("out_0", (256, 1024), _mybir.dt.float32, kind="ExternalOutput").ap()
    build(nc, args, out)
    r = _run(nc, [arrays], core_ids=[0])
    return r.results[0]["out_0"].reshape(1, 256, 1024)
```

```python
import math
from contextlib import ExitStack

import numpy as np
import concourse.bass as bass
from concourse import mybir

F32 = mybir.dt.float32
F32R = mybir.dt.float32r
I32 = mybir.dt.int32
ALU = mybir.AluOpType
ACT = mybir.ActivationFunctionType
X = mybir.AxisListType.X
ALPHA = 4 ** 0.25
LAM0 = 0.8 - 0.6 * math.exp(-0.3)
SLOTS = 3
NEG = -1e30


class Queue:

    def __init__(self, sem, link):
        self.sem, self.link, self.ops, self.n, self.seen = sem, link, [], 0, {}

    def wait(self, *toks):
        for tok in toks:
            if tok is None:
                continue
            if isinstance(tok, list):
                self.wait(*tok)
                continue
            sem, v = tok
            if self.seen.get(id(sem), 0) < v:
                self.seen[id(sem)] = v
                self.ops.append(lambda e, s=sem, v=v: e.wait_ge(s, v))

    def __call__(self, fn, *toks, inc=True):
        self.wait(*toks)
        if self.link and self.n:
            self.wait((self.sem, self.n))
        if inc:
            self.n += 1
            self.ops.append(lambda e: fn(e).then_inc(self.sem, 1))
            return (self.sem, self.n)
        self.ops.append(fn)
        return None

    def raw(self, fn):
        self.ops.append(fn)

    def now(self):
        return (self.sem, self.n) if self.n else None


class Buf:
    def __init__(self, ap):
        self.ap, self.rel = ap, []


class Pool:

    def __init__(self, aps):
        self.free = [Buf(a) for a in aps]

    def get(self):
        return self.free.pop(0)

    def put(self, buf, *toks):
        buf.rel = [t for t in toks if t is not None]
        self.free.append(buf)


def consts():
    f = np.float32
    p = np.arange(128)[:, None]
    i = np.arange(128)[None, :]
    out, at = [], {}

    def add(name, a):
        a = np.asarray(a, f)
        if a.shape[0] < 128:
            a = np.concatenate([a, np.zeros((128 - a.shape[0], a.shape[1]), f)])
        at[name] = (sum(x.shape[1] for x in out), a.shape[1])
        out.append(a)

    add("ident", p == i)
    add("exch", p + i == 127)
    rot = np.zeros((128, 128), f)
    for m in range(64):
        rot[m + 64, m] = -1.0
        rot[m, m + 64] = 1.0
    add("rot", rot)
    add("tri", p <= i)
    add("ntri", -(p >= i).astype(f))
    add("cmt", np.where(i < p, f(NEG), f(0)))
    for s in (1, 2, 4, 8, 16, 32, 64):
        add(f"m{s}", (p // (2 * s) == i // (2 * s)) & (p % (2 * s) < s) & (i % (2 * s) >= s))
    y = np.arange(256)[None, :]
    rel = p + 128 - y
    for n, d in enumerate((1, 4, 16)):
        ok = (rel >= 0) & (rel <= 128 * d) & (rel % d == 0)
        add(f"dm{n}", np.where(ok, f(0), f(NEG)))
    add("cm", np.where(rel >= 0, f(0), f(NEG)))
    dist = 255 - np.arange(384)
    d = np.maximum(dist, 1).astype(f)
    large = 16 + (np.log(d / f(16)) / f(math.log(128.0)) * f(16)).astype(np.int32)
    b = np.where(dist < 16, dist, np.minimum(large, 31))
    add("hot", (b[None, :] == np.arange(32)[:, None]) & (dist >= 0)[None, :])
    add("freq", np.tile((1.0 / (f(10000.0) ** (np.arange(0, 128, 2).astype(f) / f(128)))).astype(f), 2)[:, None])
    add("e16", np.broadcast_to(16.0 - (np.arange(32) % 16), (128, 32)))
    add("g4", np.broadcast_to(4.0 - (np.arange(8) % 4), (128, 8)))
    lg = np.log(f(1) - np.exp2(f(-5) - np.arange(8).astype(f))).astype(f)
    yy = np.arange(256)[None, :]
    dec = [np.where(yy >= p, np.exp(np.maximum(yy - p, 0).astype(f) * lg[h]), f(0)) for h in range(8)]
    return np.concatenate(out, 1).astype(f), at, np.concatenate(dec, 1).astype(f)


PARAMS = [("gconv", 72), ("fw0", 132), ("fb0", 44), ("fw1", 132), ("fb1", 44), ("gnw", 1), ("dnw", 1),
          ("lnw", 1), ("lbg", 2), ("rgn", 16), ("adab", 96), ("lng", 64), ("lnb", 64), ("c", 8), ("dl", 4), ("rb", 4),
          ("lwg", 256), ("rw", 128), ("wba", 96), ("wgd", 128)]
ROWS = [("alog", 6), ("dtb", 6), ("rtb", 16)]


def offsets(spec):
    at, n = {}, 0
    for name, w in spec:
        at[name] = (n, w)
        n += w
    return at, n


def build(nc, ins, out):
    ctx = ExitStack()
    with ctx:
        emit(nc, ctx, ins, out)


def emit(nc, ctx, ins, out):
    _, kat, _ = consts()
    pat, npar = offsets(PARAMS)
    rat, nrow = offsets(ROWS)
    ncon = ins["kc"].shape[1]

    def sb(name, cols, dt=F32):
        return ctx.enter_context(nc.sbuf_tensor(name, [128, cols], dt))

    def sem(name):
        return ctx.enter_context(nc.semaphore(name))

    ring = sb("ring", SLOTS * 4096)
    kc = sb("kc_sb", ncon)
    cp = sb("cp_sb", npar)
    rp = sb("rp_sb", nrow)
    ones = sb("ones", 128)
    neg1 = sb("neg1", 128)
    half = sb("half", 16)
    xs = sb("xs", 2048)
    xTs = sb("xTs", 2048)
    lnp = sb("lnp", 2048)
    gate = sb("gate", 1024)
    mods = sb("mods", 96)
    lnc = sb("lnc", 128)
    tmpn = sb("tmpn", 1024)
    TPs = sb("TPs", 1024)
    small = sb("small", 640)
    adacc = tmpn
    posi = sb("posi", 256, I32)
    psum = ctx.enter_context(nc.psum_tensor("ps", [128, 8, 512], F32))
    scratch = nc.dram_tensor("scratch", [4, 384], F32)

    T = Queue(sem("s_pe"), False)
    V = Queue(sem("s_dve"), True)
    A = Queue(sem("s_act"), True)
    G = Queue(sem("s_pool"), True)
    S = Queue(sem("s_sp"), False)
    s_par = sem("s_par")
    s_ring = [sem(f"s_ring{i}") for i in range(SLOTS)]
    s_row = sem("s_row")
    s_dec = sem("s_dec")
    s_scr = sem("s_scr")
    s_hank = sem("s_hank")
    s_out = sem("s_out")

    PS = Pool([psum[:, i, :] for i in range(8)])

    def K(name):
        o, w = kat[name]
        return kc[:, o:o + w]

    def C(name, a=0, b=None):
        o, w = pat[name]
        return cp[:, o + a:o + (w if b is None else b)]

    def R(name):
        o, w = rat[name]
        return rp[:, o:o + w]

    ident = K("ident")
    x = xs[:, :].rearrange("p (t n) -> p t n", t=2)
    xT = xTs[:, :].rearrange("p (k n) -> p k n", k=8)

    def mm(o, l, r, start, stop, *toks, inc=False):
        return T(lambda e: e.matmul(o, l, r, start=start, stop=stop, skip_group_check=True), *toks, inc=inc)

    def tp(o, i, *toks, inc=False):
        n = i.shape[0]
        return T(lambda e: e.transpose(o, i, ident[0:n, 0:n]), *toks, inc=inc)

    def act(o, i, f, *toks, **kw):
        return A(lambda e: e.activation(o, i, f, **kw), *toks)

    def tt(q, o, a, b, op, *toks):
        return q(lambda e: e.tensor_tensor(o, a, b, op), *toks)

    def ts(q, o, a, s1, s2, op0, op1, *toks):
        if s2 is None:
            return q(lambda e: e.tensor_scalar(o, a, s1, None, op0), *toks)
        return q(lambda e: e.tensor_scalar(o, a, s1, s2, op0, op1), *toks)

    def stt(o, a, s, b, op0, op1, *toks):
        return V(lambda e: e.scalar_tensor_tensor(out=o, in0=a, scalar=s, in1=b, op0=op0, op1=op1), *toks)

    def cpy(q, o, i, *toks):
        if q is A:
            return act(o, i, ACT.Copy, *toks)
        return q(lambda e: e.tensor_copy(o, i), *toks)

    def bc(ap, shape):
        return ap.broadcast_to(shape)

    def tables(name):
        A.raw(lambda e: e.preload_act_table_set(name))

    nload = [0]
    ring_rel = [[] for _ in range(SLOTS)]

    def load(src, kt):
        n = nload[0]
        nload[0] += 1
        s = n % SLOTS
        w = src.shape[1]
        S.wait(*ring_rel[s])
        dst = ring[:, s * 4096:s * 4096 + w]
        S.raw(lambda e: e.dma_start(dst, src).then_inc(s_ring[s], 16))
        view = dst.rearrange("p (k n) -> p k n", k=kt)
        return view, (s_ring[s], 16 * (n // SLOTS + 1)), s

    def done(s, tok):
        ring_rel[s] = [tok]

    top = [0]
    stage = [None, None, 0, None]

    def open_stage(cols, toks, split=True):
        if stage[0] is not None:
            stage[0].close()
        stage[0] = ExitStack()
        stage[2] = cols
        n = nstage[0]
        nstage[0] += 1
        stage[1] = stage[0].enter_context(nc.sbuf_tensor(f"arena{n}", [128, cols], F32))
        top[0] = 0
        for q in (V, A, G):
            q.wait(*toks)
        if not split:
            return None
        w = stage[0].enter_context(nc.sbuf_tensor(f"wsplit{n}", [128, 4, 2, 1024], F32R))
        xsp = stage[0].enter_context(nc.sbuf_tensor(f"xsplit{n}", [128, 2, 8, 256], F32R))
        stage[3] = Pool([w[:, i, :, :] for i in range(4)])
        return xsp

    def take(cols):
        a = top[0]
        top[0] += cols
        assert top[0] <= stage[2], (top[0], stage[2])
        return stage[1][:, a:a + cols]

    nstage = [0]

    def snap():
        return [q.now() for q in (T, V, A, G)]

    def run(gens, width, fill=None):
        gens, live = list(gens), []
        while gens or live:
            while gens and len(live) < width:
                live.append(gens.pop(0))
            for g in list(live):
                if next(g, 0) == 0:
                    live.remove(g)
            if fill is not None and next(fill, 0) == 0:
                fill = None
        for _ in fill or ():
            pass

    A.raw(lambda e: e.dma_start(kc[:, :], ins["kc"]).then_inc(s_par, 16))
    A.raw(lambda e: e.dma_start(cp[:, :], ins["cp"]).then_inc(s_par, 16))
    A.raw(lambda e: e.dma_start(rp[:, :], ins["rp"].broadcast_to([128, nrow])).then_inc(s_par, 16))
    A.raw(lambda e: e.dma_start(x[:, 0, :], ins["x"][0:128, :]).then_inc(s_par, 16))
    A.raw(lambda e: e.dma_start(x[:, 1, :], ins["x"][128:256, :]).then_inc(s_par, 16))
    PAR = (s_par, 80)
    S.wait(PAR)
    m1 = G(lambda e: e.memset(ones[:, :], 1.0))
    m2 = G(lambda e: e.memset(neg1[:, :], -1.0))
    m3 = G(lambda e: e.memset(half[:, :], -0.5))
    for q in (T, V, A, G):
        q.wait(PAR, m3)
    gxt = [None]
    nrows = [0]

    def load_rows(i):
        G.wait(G.now())
        for c in range(2):
            dst = lnp[:, 1024 * c:1024 * c + 1024]
            r = 2 * i + c
            G.raw(lambda e, dst=dst, r=r: e.dma_start(dst, ins["rows"][r:r + 1, :].broadcast_to([128, 1024]))
                  .then_inc(s_row, 16))
            nrows[0] += 1
        return (s_row, 16 * nrows[0])

    open_stage(24800, [], False)
    top[0] = 23000
    hrow = take(384)
    hank = take(1024)
    b = PS.get()
    t = mm(b.ap[0:4, 0:384], C("rb")[0:32, :], K("hot")[0:32, :], True, True, inc=True)
    t = cpy(V, hrow[0:4, :], b.ap[0:4, 0:384], t)
    PS.put(b, t)
    A.wait(t)
    A.raw(lambda e: e.dma_start(scratch[:, :], hrow[0:4, :]).then_inc(s_scr, 16))
    A.wait((s_scr, 16))
    hsrc = bass.AP(tensor=scratch[:, :].tensor, offset=0, ap=[[1, 128], [384, 4], [1, 256]])
    A.raw(lambda e: e.dma_start(hank.rearrange("p (h n) -> p h n", h=4), hsrc).then_inc(s_hank, 16))
    def transposed(toks, cols=None, rows=None, split=None):
        last = []
        for t in range(2):
            for kp in range(2):
                b = PS.get()
                for k in range(4):
                    f = 4 * kp + k
                    r = tp(b.ap[:, 128 * k:128 * k + 128], x[:, t, f * 128:f * 128 + 128], toks[t], b.rel, inc=(k == 3))
                w = b.ap.rearrange("p (k n) -> p k n", k=4)
                dst = xT[:, 4 * kp:4 * kp + 4, t * 128:t * 128 + 128]
                if cols is None:
                    e = [cpy(A if kp % 2 else V, dst, w, r)]
                else:
                    g, b2 = cols
                    e = []
                    onv = t == 1 and kp == 0
                    for k in range(4):
                        f = 4 * kp + k
                        if onv:
                            q = ts(V, dst[:, k, :], w[:, k, :], g[:, f:f + 1], b2[:, f:f + 1], ALU.mult, ALU.add, r)
                        else:
                            q = act(dst[:, k, :], w[:, k, :], ACT.Identity, r, scale=g[:, f:f + 1], bias=b2[:, f:f + 1])
                    e = [q]
                PS.put(b, *e)
                if split is not None:
                    hi = split[:, 0, 4 * kp:4 * kp + 4, t * 128:t * 128 + 128]
                    lo = split[:, 1, 4 * kp:4 * kp + 4, t * 128:t * 128 + 128]
                    q = cpy(A, hi, dst, e)
                    e = [tt(V, lo, dst, hi.bitcast(F32), ALU.subtract, q, e)]
                last += e
            if rows is not None:
                tt(G, x[:, t, :], x[:, t, :], lnp[:, 0:1024], ALU.mult, rows, r)
                gxt[0] = tt(G, x[:, t, :], x[:, t, :], lnp[:, 1024:2048], ALU.add)
        return last

    def proj_T(src, ntile, tok, evac, kt=8, act_in=None):
        a = xT if act_in is None else act_in
        view, arrived, slot = load(src, kt)
        for c in range(ntile):
            b = PS.get()
            for k in range(kt):
                r = mm(b.ap[:, 0:256], view[:, k, c * 128:c * 128 + 128], a[:, k, :], k == 0, k == kt - 1,
                       arrived, tok, b.rel, inc=(k == kt - 1))
            if c == ntile - 1:
                done(slot, r)
            PS.put(b, evac(c, b.ap[:, 0:256], r))
            yield 1

    def tiles_of(src, n):
        return [(src, 8, "cols", c, c == n - 1) for c in range(n)]

    def rows_of_piece(src):
        k = src.shape[1] // 1024
        return [(src, k, "row", c, c == k - 1) for c in range(k)]

    def stream(chunks):
        it, ready, view = iter(chunks), [], [None]

        def get():
            while len(ready) < 3 and (stage[3].free or not ready):
                c = next(it, None)
                if c is None:
                    break
                src, kt, how, i, last = c
                if i == 0:
                    view[0] = load(src, kt)
                v, arrived, slot = view[0]
                buf = stage[3].get()
                if how == "cols":
                    part = v[:, :, i * 128:i * 128 + 128]
                    hi, lo = (buf.ap[:, j, :].rearrange("p (k n) -> p k n", k=8) for j in range(2))
                else:
                    part = v[:, i, :]
                    hi, lo = buf.ap[:, 0, :], buf.ap[:, 1, :]
                r = cpy(A, hi, part, arrived, buf.rel)
                r = tt(V, lo, part, hi.bitcast(F32), ALU.subtract, r, arrived)
                if last:
                    done(slot, r)
                ready.append((buf, hi, lo, r))
            return ready.pop(0)

        return get

    def tile3(o, get, xsp, start, tok, rel):
        buf, hi, lo, r = get()
        for k in range(8):
            for n, (w, j) in enumerate(((hi, 0), (hi, 1), (lo, 0))):
                m = mm(o, w[:, k, :], xsp[:, j, k, :], k == 0 and n == 0, k == 7 and n == 2, r, tok, rel,
                       inc=(k == 7 and n == 2))
        stage[3].put(buf, m)
        return m

    def proj_S(get, ntile, xsp, tok, evac):
        for c in range(ntile):
            b = PS.get()
            m = tile3(b.ap[:, 0:256], get, xsp, True, tok, b.rel)
            PS.put(b, evac(c, b.ap[:, 0:256], m))
            yield 1

    def down3(get, total, lhs, tok):
        banks = [PS.get() for _ in range(4)]
        tail = []
        for f in range(total):
            c4 = get()
            if f < total - 2:
                tail.append([(f, c4, t) for t in range(2)])
            elif f == total - 2:
                last = c4
            else:
                tail.append([(f - 1, last, 0), (f, c4, 0), (f - 1, last, 1), (f, c4, 1)])
            if f == total - 2:
                continue
            for f1, (buf, hi, lo, r), t in tail.pop():
                tk = slice(t * 128, t * 128 + 128)
                for c in range(2):
                    b = banks[2 * t + c]
                    cc = slice(c * 512, c * 512 + 512)
                    for n, (a, w) in enumerate(((0, hi), (0, lo), (1, hi))):
                        m = mm(b.ap, lhs[a][:, f1, tk], w[:, cc], f1 == 0 and n == 0, f1 == total - 1 and n == 2, r, tok,
                               b.rel, inc=(n == 2 and c == 1))
                if t == 0:
                    m0 = m
                if t == 1:
                    stage[3].put(buf, m)
        return banks, [m0, m]

    def proj_rows(src, cols, tok, evac):
        view, arrived, slot = load(src, 8)
        for t in range(2):
            b = PS.get()
            for k in range(8):
                r = mm(b.ap[:, 0:cols], xT[:, k, t * 128:t * 128 + 128], view[:, k, :], k == 0, k == 7,
                       arrived, tok, b.rel, inc=(k == 7))
            if t == 1:
                done(slot, r)
            PS.put(b, evac(t, b.ap[:, 0:cols], r))
            yield 1

    def down(srcs, lhs, tok):
        banks = [PS.get() for _ in range(4)]
        total = sum(s.shape[1] // 1024 for s in srcs)
        k0 = 0
        fin = [None, None]
        for src in srcs:
            kt = src.shape[1] // 1024
            view, arrived, slot = load(src, kt)
            end = k0 + kt == total
            order = [(k, t) for t in range(2) for k in range(kt)] if end else [(k, t) for k in range(kt) for t in range(2)]
            for k, t in order:
                f = k0 + k
                for c in range(2):
                    r = mm(banks[2 * t + c].ap, lhs[:, f, t * 128:t * 128 + 128], view[:, k, c * 512:c * 512 + 512],
                           f == 0, f == total - 1, arrived, tok, banks[2 * t + c].rel,
                           inc=(k == kt - 1 and c == 1))
                if end and k == kt - 1:
                    fin[t] = r
            done(slot, r)
            k0 += kt
        return banks, fin

    mark = [None]

    def norm(src, stok, gated, last=None):
        toks = []
        st = small[:, 600:624]
        mark[0] = snap()
        for t in range(2):
            for c in range(2):
                xx = x[:, t, c * 512:c * 512 + 512]
                bank = isinstance(src, list)
                s = src[2 * t + c].ap if bank else src[:, t, c * 512:c * 512 + 512]
                if gated:
                    d = tmpn[:, c * 512:c * 512 + 512]
                    r = tt(V, d, s, gate[:, c * 512:c * 512 + 512], ALU.mult, stok[t])
                    if bank:
                        PS.put(src[2 * t + c], r)
                    s = d
                r = stt(xx, xx, ALPHA, s, ALU.mult, ALU.add, stok[t], gxt[0])
                if bank and not gated:
                    PS.put(src[2 * t + c], r)
                V(lambda e, c=c, xx=xx, t=t: e.bn_stats(small[:, 560 + 12 * t + 6 * c:566 + 12 * t + 6 * c], xx))
            mv = st[:, 4 * t:4 * t + 2]
            V(lambda e, mv=mv, t=t: e.bn_aggr(mv, small[:, 560 + 12 * t:572 + 12 * t]))
            r = ts(V, st[:, 4 * t + 2:4 * t + 3], mv[:, 1:2], 1e-5, None, ALU.add, None)
            r = tt(G, st[:, 4 * t + 3:4 * t + 4], st[:, 4 * t + 2:4 * t + 3], half[:, 0:1], ALU.pow, r)
            r = ts(V, x[:, t, :], x[:, t, :], mv[:, 0:1], st[:, 4 * t + 3:4 * t + 4], ALU.subtract, ALU.mult, r)
            if last is not None:
                tt(V, x[:, t, :], x[:, t, :], lnp[:, 0:1024], ALU.mult, last)
                r = tt(V, x[:, t, :], x[:, t, :], lnp[:, 1024:2048], ALU.add)
                A.wait(r)
                A.raw(lambda e, t=t: e.dma_start(out[t * 128:t * 128 + 128, :], x[:, t, :]).then_inc(s_out, 16))
            toks.append(r)
        return toks

    def inv_sqrt(dst, sums, scale, eps, add, tok):
        epsc[eps]
        r = act(dst, sums, ACT.Ln, tok, scale=scale, bias=epsc[eps])
        if add:
            return r, act(dst, dst, ACT.Exp, scale=-0.5, bias=epsc[add])
        return r, act(dst, dst, ACT.Exp, scale=-0.5)

    epsc = {}
    for n, v in enumerate((1e-6, 1e-5, math.log(128 ** -0.5), math.pi / 2)):
        epsc[v] = small[:, 624 + n:625 + n]
        r = V(lambda e, n=n, v=v: e.memset(small[:, 624 + n:625 + n], v))
    A.wait(r)
    LQ = math.log(128 ** -0.5)

    scc = small[:, 210:218]
    tables("silu_and_others")
    sc_tok = act(scc, C("c"), ACT.Silu)
    ada_buf = Pool([adacc[:, 0:512], adacc[:, 512:1024]])

    def adaln(i):
        for j in range(6):
            view, arrived, slot = load(ins["ada"][6 * i + j], 8)
            a = ada_buf.get()
            for k in range(8):
                if k == 0:
                    r = ts(V, a.ap, view[:, k, :], scc[:, k:k + 1], None, ALU.mult, None, arrived, sc_tok, a.rel)
                else:
                    r = stt(a.ap, view[:, k, :], scc[:, k:k + 1], a.ap, ALU.mult, ALU.add)
                if k % 4 == 3:
                    if k == 7:
                        done(slot, r)
                    yield 1
            b = PS.get()
            for c in range(4):
                m = mm(b.ap[:, c:c + 1], a.ap[:, 128 * c:128 * c + 128], ones[:, 0:1], True, True, r, b.rel, inc=(c == 3))
            ada_buf.put(a, m)
            o = 24 * i + 4 * j
            m = stt(mods[:, o:o + 4], b.ap[:, 0:4], 0.0 if j < 2 else 1.0, C("adab", o, o + 4), ALU.add, ALU.add, m)
            PS.put(b, m)
        sh, sc = mods[:, 24 * i:24 * i + 8], mods[:, 24 * i + 8:24 * i + 16]
        o = 8 * (3 + i)
        tt(V, lnc[:, o:o + 8], C("lng", o, o + 8), sc, ALU.mult)
        tt(V, lnc[:, 64 + o:72 + o], C("lnb", o, o + 8), sc, ALU.mult)
        tt(V, lnc[:, 64 + o:72 + o], lnc[:, 64 + o:72 + o], sh, ALU.add)

    def chained(*gens):
        for g in gens:
            yield from g

    def after(i):
        if i < 3:
            return C("lng", 8 * i, 8 * i + 8), C("lnb", 8 * i, 8 * i + 8)
        return lnc[:, 8 * i:8 * i + 8], lnc[:, 64 + 8 * i:72 + 8 * i]

    rows = load_rows(0)
    xt = transposed([None, None])
    top[0] = 0
    qkvz = take(24 * 256)
    QT = qkvz.rearrange("p (n m) -> p n m", n=24)
    oTf = take(2048)
    oT = oTf.rearrange("p (n m) -> p n m", n=8)
    top_gdn = top[0]
    qbk = take(12 * 256).rearrange("p (n m) -> p n m", n=12)
    vbt = take(1536).rearrange("p (t n) -> p t n", t=2)
    temp0 = top[0]

    conv_tok = {}

    def evac_even(c0):
        def f(c, ps, r):
            n = c0 + c
            y = QT[:, n, :]
            if n < 18:
                w = C("gconv")
                r1 = act(y, ps, ACT.Copy, r, scale=w[:, 4 * n + 3:4 * n + 4])
                for s in (1, 2, 3):
                    r1 = stt(y[:, s:256], ps[:, 0:256 - s], w[:, 4 * n + 3 - s:4 * n + 4 - s], y[:, s:256],
                             ALU.mult, ALU.add, r1)
            else:
                r1 = cpy(A, y, ps, r)
            conv_tok[n] = r1
            return r1
        return f

    def evac_b(c0):
        def f(c, ps, r):
            n = c0 + c
            if n < 6:
                r = ts(V, qbk[:, n, :], ps, 0.125, None, ALU.mult, None, r)
            else:
                r = cpy(V if n % 2 else A, qbk[:, n, :], ps, r)
            b_tok[n] = r
            return r
        return f

    b_tok = {}
    tables("natural_log_exp_and_others")

    def evac_rows(dst, c0, q):
        def f(t, ps, r):
            r = cpy(q, dst[:, t, c0:c0 + ps.shape[1]], ps, r)
            row_tok.append(r)
            return r
        return f

    row_tok = []
    run([proj_T(ins["we"][6 + j], 4, xt, evac_b(4 * j)) for j in range(3)]
        + [proj_rows(ins["wev"][0], 512, xt, evac_rows(vbt, 0, V)),
           proj_rows(ins["wev2"][0], 256, xt, evac_rows(vbt, 512, A))], 1, adaln(0))
    b = PS.get()
    wba = C("wba").rearrange("p (k n) -> p k n", k=8)
    for t in range(2):
        for k in range(8):
            r = mm(b.ap[:, 12 * t:12 * t + 12], xT[:, k, t * 128:t * 128 + 128], wba[:, k, :], k == 0, k == 7,
                   b.rel, inc=(k == 7))
    ba = small[:, 0:24].rearrange("p (t n) -> p t n", t=2)
    r = cpy(V, small[:, 0:24], b.ap[:, 0:24], r)
    PS.put(b, r)

    def softplus(dst, src, tmp, tok):
        act(tmp, src, ACT.Abs, tok)
        act(tmp, tmp, ACT.Exp, scale=-1.0)
        r = act(tmp, tmp, ACT.Ln, bias=1.0)
        return stt(dst, src, 0.0, tmp, ALU.max, ALU.add, r)

    def cols(a):
        return small[:, a:a + 12]

    def two(ap):
        return ap.rearrange("p (t n) -> p t n", t=2)

    r = act(two(cols(24)), ba[:, :, 0:6], ACT.Exp, r, scale=-1.0)
    r = ts(V, cols(24), cols(24), 1.0, None, ALU.add, None, r)
    r = V(lambda e: e.reciprocal(cols(24), cols(24)))
    r = tt(V, two(cols(96)), ba[:, :, 6:12], bc(R("dtb").rearrange("p (a n) -> p a n", a=1), [128, 2, 6]), ALU.add)
    r = softplus(cols(96), cols(96), cols(108), r)
    e1 = act(small[:, 120:126], R("alog"), ACT.Exp)
    r = stt(two(cols(36)), two(cols(96)), -1.0,
            bc(small[:, 120:126].rearrange("p (a n) -> p a n", a=1), [128, 2, 6]), ALU.mult, ALU.mult, e1)
    b = PS.get()
    mm(b.ap[:, 0:12], K("tri"), cols(36), True, True, r, b.rel)
    rg = mm(b.ap[:, 12:24], ones[:, :], cols(36), True, True, inc=True)
    cpy(V, small[:, 130:154], b.ap[:, 0:24], rg)
    r = cpy(V, cols(48), b.ap[:, 0:12])
    PS.put(b, r)
    ts(V, cols(84), cols(48), -1.0, None, ALU.mult, None)
    r = tt(V, cols(72), small[:, 142:154], cols(48), ALU.subtract)
    act(cols(72), cols(72), ACT.Exp, r)
    r = act(cols(60), cols(48), ACT.Exp)
    gates = tt(V, cols(60), cols(60), cols(24), ALU.mult, r)

    TP = TPs[:, :].rearrange("p (h n) -> p h n", h=4)
    for c in range(2):
        b = PS.get()
        t = mm(b.ap, K("exch"), hank[:, 512 * c:512 * c + 512], True, True, (s_hank, 16), b.rel, inc=True)
        t = cpy(V, TPs[:, 512 * c:512 * c + 512], b.ap, t)
        PS.put(b, t)
    TPt = t

    top[0] = temp0
    sS = Pool([take(768) for _ in range(4)])
    sP = Pool([take(768) for _ in range(4)])
    stat = Pool([small[:, 160 + 4 * i:164 + 4 * i] for i in range(6)])
    DM = kc[:, kat["dm0"][0]:kat["dm0"][0] + 768].rearrange("p (g n) -> p g n", g=3)
    o_tok = []

    def swa_unit(h, t):
        base = (h % 2) * 64
        nk = 128 * (t + 1)
        off = 256 - nk
        s = sS.get()
        sv = s.ap[:, 0:3 * nk].rearrange("p (g n) -> p g n", g=3)
        for g0, g1 in ([(0, 3)] if t == 0 else [(0, 2), (2, 3)]):
            b = PS.get()
            for g in range(g0, g1):
                n = g * 2 + h // 2
                r = mm(b.ap[:, (g - g0) * nk:(g - g0) * nk + nk], qbk[base:base + 64, n, t * 128:t * 128 + 128],
                       qbk[base:base + 64, 6 + n, 0:nk], True, True, b.rel, b_tok[n], b_tok[6 + n], inc=(g == g1 - 1))
            r = tt(V, sv[:, g0:g1, :], b.ap[:, 0:(g1 - g0) * nk].rearrange("p (g n) -> p g n", g=g1 - g0),
                   bc(TP[:, h:h + 1, off:256], [128, g1 - g0, nk]), ALU.add, r, s.rel, TPt)
            PS.put(b, r)
        r = tt(V, sv, sv, DM[:, :, off:256], ALU.add)
        sm = stat.get()
        r = V(lambda e: e.tensor_reduce(sm.ap[:, 0:1], s.ap[:, 0:3 * nk], X, ALU.max, negate=True), sm.rel)
        r = act(s.ap[:, 0:3 * nk], s.ap[:, 0:3 * nk], ACT.Exp, r, bias=sm.ap[:, 0:1], accum_out=sm.ap[:, 1:2])
        yield 1
        V(lambda e: e.reciprocal(sm.ap[:, 2:3], sm.ap[:, 1:2]), r)
        r = ts(V, s.ap[:, 0:3 * nk], s.ap[:, 0:3 * nk], sm.ap[:, 2:3], None, ALU.mult, None)
        stat.put(sm, r)
        yield 1
        p = sP.get()
        nt = 3 * (t + 1)
        pt = []
        for c0 in range(0, nt, 4):
            c1 = min(c0 + 4, nt)
            b = PS.get()
            for c in range(c0, c1):
                r2 = tp(b.ap[:, (c - c0) * 128:(c - c0) * 128 + 128], s.ap[:, c * 128:c * 128 + 128], r, b.rel,
                        inc=(c == c1 - 1))
            r3 = cpy(A if c0 else V, p.ap[:, c0 * 128:c1 * 128], b.ap[:, 0:(c1 - c0) * 128], r2, p.rel)
            pt.append(r3)
            PS.put(b, r3)
        sS.put(s, r2)
        yield 1
        ob = PS.get()
        for c in range(nt):
            g, jt = c // (t + 1), c % (t + 1)
            r = mm(ob.ap[base:base + 64, 0:128], vbt[:, jt, g * 256 + h * 64:g * 256 + h * 64 + 64],
                   p.ap[:, c * 128:c * 128 + 128], c == 0, c == nt - 1, pt, ob.rel, row_tok, inc=(c == nt - 1))
        sP.put(p, r)
        r = cpy(A, oT[base:base + 64, 6 + h // 2, t * 128:t * 128 + 128], ob.ap[base:base + 64, 0:128], r)
        o_tok.append(r)
        PS.put(ob, r)
        yield 1

    def projections():
        for j in range(6):
            yield from proj_T(ins["we"][j], 4, xt, evac_even(4 * j))

    run([swa_unit(h, t) for h in range(4) for t in range(2)], 3, projections())
    tables("silu_and_others")
    for n in range(6):
        silu_tok = act(qkvz[:, 1024 * n:1024 * n + 1024], qkvz[:, 1024 * n:1024 * n + 1024], ACT.Silu,
                       [conv_tok[4 * n + i] for i in range(4)])
    tables("natural_log_exp_and_others")

    for q in (V, A, G):
        q.wait(*snap())
    top[0] = top_gdn
    take(768)
    sq = Pool([take(512) for _ in range(3)])
    l2 = {}

    def l2_unit(n):
        pair = qkvz[:, n * 256:n * 256 + 512]
        s = sq.get()
        r = act(s.ap, pair, ACT.Square, s.rel, silu_tok)
        yield 1
        b = PS.get()
        r = mm(b.ap, ones[:, :], s.ap, True, True, r, b.rel, inc=True)
        r1, r2 = inv_sqrt(s.ap, b.ap, 1.0, 1e-6, LQ if n < 6 else None, r)
        PS.put(b, r1)
        r = tt(V, pair, pair, s.ap, ALU.mult, r2)
        l2[n] = l2[n + 1] = r
        sq.put(s, r)
        yield 1

    run([l2_unit(n) for n in range(0, 12, 2)], 3)
    top[0] = top_gdn
    Sst = take(768)
    for q in (V, A, G):
        q.wait(*snap())
    NAMES = ("a", "b", "DT", "EG", "LT", "QK", "E", "D", "kbe", "vb")
    sets = Pool([{k: take(384) for k in NAMES} for _ in range(4)])
    M3 = [128, 3, 128]

    def v3(ap):
        return ap.rearrange("p (h n) -> p h n", h=3)

    def k3(name):
        return bc(K(name).rearrange("p (a n) -> p a n", a=1), M3)

    def col3(a, n):
        return bc(small[:, a + n:a + n + 3].rearrange("p (n a) -> p n a", a=1), M3)

    def cs(ap):
        return lambda i: ap[:, i * 128:i * 128 + 128]

    def three(l, r, toks, acc=None):
        b = PS.get()
        for i in range(3):
            k = mm(b.ap[:, i * 128:i * 128 + 128], l(i), r(i), True, acc is None, toks, b.rel,
                   inc=(i == 2 and acc is None))
            if acc is not None:
                k = mm(b.ap[:, i * 128:i * 128 + 128], acc[0](i), acc[1](i), False, True, toks, inc=(i == 2))
        return b, k

    def flip(src, toks):
        b = PS.get()
        for i in range(3):
            k = tp(b.ap[:, i * 128:i * 128 + 128], src(i), toks, b.rel, inc=(i == 2))
        return b, k

    S_tok, gdn_tok = {}, []
    T.wait(silu_tok, l2[11])

    def gdn_unit(t, hg):
        ub = sets.get()
        u = ub.ap
        n0 = 6 * t + 3 * hg
        tk = slice(t * 128, t * 128 + 128)

        def head(j):
            return lambda i: QT[:, j + 3 * hg + i, tk]

        cpy(V, v3(u["a"]), col3(36, n0), ub.rel)
        r = cpy(V, v3(u["b"]), col3(24, n0))
        b, k = three(cs(u["a"]), lambda i: K("tri"), r)
        b2, k2 = three(cs(u["b"]), lambda i: ident, r)
        B = b.ap[:, 0:384]
        r = tt(V, v3(u["DT"]), v3(B), k3("cmt"), ALU.add, k)
        re = act(u["EG"], B, ACT.Exp, r)
        PS.put(b, re)
        for i in range(3):
            r = act(u["DT"][:, i * 128:i * 128 + 128], u["DT"][:, i * 128:i * 128 + 128], ACT.Exp,
                    bias=small[:, 84 + n0 + i:85 + n0 + i])
        r2 = tt(V, u["LT"], u["DT"], b2.ap[:, 0:384], ALU.mult, r, k2)
        PS.put(b2, r2)
        yield 1
        b, k = three(head(6), head(6), None)
        b2, k2 = three(head(6), head(0), None)
        r = tt(V, u["LT"], u["LT"], b.ap[:, 0:384], ALU.mult, k)
        PS.put(b, r)
        r = tt(V, u["QK"], u["DT"], b2.ap[:, 0:384], ALU.mult, k2)
        PS.put(b2, r)
        tt(V, v3(u["E"]), v3(u["LT"]), k3("m1"), ALU.mult)
        r = tt(V, v3(u["E"]), k3("ident"), v3(u["E"]), ALU.subtract)
        rL = tt(V, v3(u["DT"]), v3(u["LT"]), k3("m2"), ALU.mult)
        yield 1
        b, k = flip(cs(u["E"]), r)
        rD = cpy(A, u["D"], b.ap[:, 0:384], k)
        PS.put(b, rD)
        b, k = flip(head(6), None)
        if t == 0:
            r1 = tt(V, v3(u["EG"]), v3(b.ap[:, 0:384]), col3(72, n0), ALU.mult, k, re)
        else:
            r1 = tt(V, v3(u["kbe"]), v3(b.ap[:, 0:384]), col3(60, n0), ALU.mult, k)
        PS.put(b, r1)
        if t == 1:
            tt(V, v3(u["EG"]), v3(u["EG"]), QT[:, 3 * hg:3 * hg + 3, tk], ALU.mult, re)
        b, k = flip(head(12), None)
        rv = tt(V, v3(u["vb"]), v3(b.ap[:, 0:384]), col3(24, n0), ALU.mult, k)
        PS.put(b, rv)
        L = u["DT"]
        rE = rv
        for s in (2, 4, 8, 16, 32, 64):
            b, k = three(cs(L), cs(u["D"]), [rL, rD])
            ra = cpy(A, u["a"], b.ap[:, 0:384], k)
            PS.put(b, ra)
            if s < 64:
                rL = tt(V, v3(L), v3(u["LT"]), k3(f"m{2 * s}"), ALU.mult, k)
            yield 1
            b2, k2 = three(cs(u["a"]), cs(u["E"]), [ra, rE])
            if s < 64:
                b, k = three(cs(u["E"]), cs(u["a"]), None)
            else:
                k = k2
            rE = tt(V, u["E"], u["E"], b2.ap[:, 0:384], ALU.subtract, k)
            PS.put(b2, rE)
            if s < 64:
                rD = tt(V, u["D"], u["D"], b.ap[:, 0:384], ALU.subtract, k)
                PS.put(b, rD)
            yield 1
        E = u["E"]
        Sg = Sst[:, hg * 384:hg * 384 + 384]
        if t == 0:
            b, k = three(cs(E), cs(u["vb"]), rE)
            r = cpy(V, u["a"], b.ap[:, 0:384], k)
            PS.put(b, r)
            yield 1
            b, k = three(cs(u["EG"]), cs(u["a"]), r)
            S_tok[hg] = cpy(A, Sg, b.ap[:, 0:384], k)
            PS.put(b, S_tok[hg])
            b, k = three(cs(u["a"]), cs(u["QK"]), r)
        else:
            b, k = three(cs(u["kbe"]), cs(E), rE)
            r = ts(V, u["b"], b.ap[:, 0:384], -1.0, None, ALU.mult, None, k)
            PS.put(b, r)
            yield 1
            b, k = three(cs(E), cs(u["vb"]), [r, S_tok[hg]], (cs(u["b"]), cs(Sg)))
            r = cpy(V, u["a"], b.ap[:, 0:384], k)
            PS.put(b, r)
            yield 1
            b, k = three(cs(u["a"]), cs(u["QK"]), r, (cs(Sg), cs(u["EG"])))
        r = cpy(V, oT[:, 3 * hg:3 * hg + 3, tk], v3(b.ap[:, 0:384]), k)
        PS.put(b, r)
        sets.put(ub, r, k)
        gdn_tok.append(r)
        yield 1

    run([gdn_unit(t, hg) for t in range(2) for hg in range(2)], 4)

    def rms_out(o, g, w, sz, tmp, tok):
        r = act(tmp[:, 0:sz], o, ACT.Square, tok)
        b = PS.get()
        r = mm(b.ap[:, 0:sz], ones[:, :], tmp[:, 0:sz], True, True, r, b.rel, inc=True)
        r1, r2 = inv_sqrt(tmp[:, 0:sz], b.ap[:, 0:sz], 1.0 / 128, 1e-6, None, r)
        PS.put(b, r1)
        tt(V, o, o, tmp[:, 0:sz], ALU.mult, r2)
        return stt(o, o, w, g, ALU.mult, ALU.mult)

    tmp3 = [sets.free[0].ap[k] for k in ("a", "DT", "LT")] + [sets.free[1].ap[k] for k in ("a", "DT", "LT")]
    for n in range(6):
        r = rms_out(oT[:, n, :], QT[:, 18 + n, :], C("gnw"), 256, tmp3[n][:, 0:256], gdn_tok + [T.now()])
    banks, k = down([ins["woe"][0], ins["woe"][1]], oT, [r] + o_tok)
    lt = norm(banks, k, False)

    def ffn(l, ln_i, tok):
        xsp = open_stage(2048, mark[0])
        gsp = stage[0].enter_context(nc.sbuf_tensor(f"gsplit{l}", [128, 2, 22, 256], F32R))
        xt = transposed(tok, after(ln_i - 1), rows_of[0], xsp)
        rows_of[0] = load_rows(ln_i)
        tables("silu_and_others")
        yg = Pool([take(512) for _ in range(4)])
        wv = C(f"fw{l}")
        bv = C(f"fb{l}")
        last, later, silu_of = [None], [], {}
        up = [c for j in range(11) for c in tiles_of(ins[f"wu{l}"][j], 4)]
        dn = [c for i in range(5) for c in rows_of_piece(ins[f"wd{l}"][i])] + rows_of_piece(ins[f"wdl{l}"][0])
        get = stream(up + dn)
        for j in range(11):
            ys = []

            def f(c, ps, r, j=j, ys=ys):
                n = 2 * j + c if c < 2 else 22 + 2 * j + c - 2
                if c < 2:
                    buf = yg.get()
                    ys.append(buf)
                    y = buf.ap[:, 0:256]
                else:
                    buf = ys[c - 2]
                    y = buf.ap[:, 256:512]
                for g in later:
                    g()
                later.clear()
                r = act(y, ps, ACT.Identity, r, buf.rel, scale=wv[:, 3 * n + 2:3 * n + 3], bias=bv[:, n:n + 1])
                for s in (1, 2):
                    r = stt(y[:, s:256], ps[:, 0:256 - s], wv[:, 3 * n + 2 - s:3 * n + 3 - s], y[:, s:256],
                            ALU.mult, ALU.add, r)
                if c < 2:
                    def silu():
                        silu_of[n] = act(y, y, ACT.Silu, r)
                    later.append(silu)
                else:
                    g = 2 * j + c - 2
                    q = tt(G, y, buf.ap[:, 0:256], y, ALU.mult, r, silu_of.get(g) or r)

                    def split():
                        k = cpy(A, gsp[:, 0, g, :], y, q)
                        last[0] = tt(G, gsp[:, 1, g, :], y, gsp[:, 0, g, :].bitcast(F32), ALU.subtract, k)
                        yg.put(buf, last[0])
                    later.append(split)
                return r

            run([proj_S(get, 4, xsp, xt, f)], 1)
        for g in later:
            g()
        banks, k = down3(get, 22, (gsp[:, 0], gsp[:, 1]), last[0])
        return norm(banks, k, False)

    rows_of = [rows]
    lt = ffn(0, 1, lt)

    open_stage(21000, mark[0], False)
    xt = transposed(lt, after(1), rows_of[0])
    rows_of[0] = load_rows(2)
    tables("silu_and_others")
    qc = take(2048).rearrange("p (n m) -> p n m", n=8)
    gl = take(1024)
    glv = gl.rearrange("p (n m) -> p n m", n=4)
    rT = take(1024).rearrange("p (n m) -> p n m", n=4)
    vc = take(1024).rearrange("p (t n) -> p t n", t=2)
    vd = take(1024).rearrange("p (t n) -> p t n", t=2)
    oTf = take(2048)
    oT = oTf.rearrange("p (n m) -> p n m", n=8)
    TC = take(1024).rearrange("p (h n) -> p h n", h=4)
    gdT = take(256)
    la = take(512)
    Bc = take(512)
    pT = {}

    def evac_odd(c0):
        def f(c, ps, r):
            n = c0 + c
            if n < 8:
                r = ts(V, qc[:, n, :], ps, 0.125, None, ALU.mult, None, r) if n < 4 else cpy(A, qc[:, n, :], ps, r)
            elif n < 12:
                m = n - 8
                r = ts(V, glv[:, m, :], ps, 0.125, None, ALU.mult, None, r) if m < 2 else cpy(A, glv[:, m, :], ps, r)
            else:
                r = act(rT[:, n - 12, :], ps, ACT.Silu, r)
            pT[n] = r
            return r
        return f

    run([proj_T(ins["wo"][j], 4, xt, evac_odd(4 * j)) for j in range(4)], 1, adaln(1))
    tables("natural_log_exp_and_others")
    row_tok = []
    run([proj_rows(ins["wov"][0], 512, xt, evac_rows(vc, 0, V)),
         proj_rows(ins["wov"][1], 512, xt, evac_rows(vd, 0, A))], 1)
    wgd = C("wgd").rearrange("p (k n) -> p k n", k=8)
    b = PS.get()
    for k in range(8):
        r = mm(b.ap[0:16, 0:256], wgd[:, k, :], xT[:, k, :], k == 0, k == 7, b.rel, xt, inc=(k == 7))
    r = cpy(V, gdT[0:16, :], b.ap[0:16, 0:256], r)
    PS.put(b, r)
    lwg = C("lwg")
    b = PS.get()
    for m in range(2):
        k = mm(b.ap[:, m * 256:m * 256 + 256], lwg[0:16, m * 128:m * 128 + 128], gdT[0:16, :], True, True, r, b.rel,
               inc=(m == 1))
    for m in range(2):
        r = ts(V, la[:, m * 256:m * 256 + 256], b.ap[:, m * 256:m * 256 + 256], C("lbg", m, m + 1), -1.0,
               ALU.add, ALU.mult, k)
    PS.put(b, r)
    r = softplus(la, la, Bc, r)
    r = ts(V, la, la, -1.0 / 16, None, ALU.mult, None)
    for i in range(4):
        s = slice(i * 128, i * 128 + 128)
        V(lambda e, s=s: e.tensor_tensor_scan(Bc[:, s], ones[:, :], la[:, s], 0.0, ALU.mult, ALU.add))
    tt(V, small[0:64, 200:202], C("dl")[0:64, 0:4:2], C("dl")[0:64, 1:4:2], ALU.mult)
    b = PS.get()
    r = mm(b.ap[:, 0:2], ones[0:64, :], small[0:64, 200:202], True, True, V.now(), b.rel, inc=True)
    r = act(small[:, 202:204], b.ap[:, 0:2], ACT.Exp, r)
    PS.put(b, r)
    tt(V, small[:, 204:205], small[:, 203:204], small[:, 202:203], ALU.subtract, r)
    ts(V, small[:, 205:206], small[:, 204:205], -LAM0, None, ALU.add, None)
    ts(V, small[:, 206:207], C("dnw"), 1.0 - LAM0, None, ALU.mult, None)
    r = tt(V, TC, TP, bc(K("cm").rearrange("p (a n) -> p a n", a=1), [128, 4, 256]), ALU.add)
    temp1 = top[0]
    sS = Pool([take(512) for _ in range(4)])
    sP = Pool([take(256) for _ in range(4)])
    stat = Pool([small[:, 160 + 6 * i:166 + 6 * i] for i in range(5)])

    def diff_unit(h, t):
        nk = 128 * (t + 1)
        off = 256 - nk
        s = sS.get()
        sv = s.ap[:, 0:2 * nk].rearrange("p (c n) -> p c n", c=2)
        pair = [PS.get(), PS.get()]
        for c in range(2):
            b = pair[c]
            r = mm(b.ap[:, 0:nk], qc[c * 64:c * 64 + 64, h, t * 128:t * 128 + 128],
                   qc[c * 64:c * 64 + 64, 4 + h, 0:nk], True, True, b.rel, pT[h], pT[4 + h], inc=True)
            r = tt(V, sv[:, c, :], b.ap[:, 0:nk], TC[:, h, off:256], ALU.add, r, s.rel)
            PS.put(b, r)
        sm = stat.get()
        r = V(lambda e: e.tensor_reduce(sm.ap[:, 0:2], sv, X, ALU.max, negate=True), sm.rel)
        for c in range(2):
            r = act(s.ap[:, c * nk:c * nk + nk], s.ap[:, c * nk:c * nk + nk], ACT.Exp, r,
                    bias=sm.ap[:, c:c + 1], accum_out=sm.ap[:, 2 + c:3 + c])
        yield 1
        V(lambda e: e.reciprocal(sm.ap[:, 4:6], sm.ap[:, 2:4]), r)
        ts(V, sm.ap[:, 5:6], sm.ap[:, 5:6], small[:, 205:206], None, ALU.mult, None)
        ts(V, s.ap[:, 0:nk], s.ap[:, 0:nk], sm.ap[:, 4:5], None, ALU.mult, None)
        r = stt(s.ap[:, 0:nk], s.ap[:, nk:2 * nk], sm.ap[:, 5:6], s.ap[:, 0:nk], ALU.mult, ALU.add)
        stat.put(sm, r)
        yield 1
        b = PS.get()
        for j in range(t + 1):
            r2 = tp(b.ap[:, j * 128:j * 128 + 128], s.ap[:, j * 128:j * 128 + 128], r, b.rel, inc=(j == t))
        sS.put(s, r2)
        p = sP.get()
        r3 = cpy(A, p.ap[:, 0:nk], b.ap[:, 0:nk], r2, p.rel)
        PS.put(b, r3)
        yield 1
        ob = PS.get()
        for j in range(t + 1):
            r = mm(ob.ap[:, 0:128], vc[:, j, h * 128:h * 128 + 128], p.ap[:, j * 128:j * 128 + 128],
                   j == 0, j == t, r3, ob.rel, row_tok, inc=(j == t))
        sP.put(p, r)
        r = cpy(A, oT[:, h, t * 128:t * 128 + 128], ob.ap[:, 0:128], r)
        PS.put(ob, r)
        dtok.append(r)
        yield 1

    dtok = []
    tmp = take(512)

    def diff_norm(n):
        o = oTf[:, n * 512:n * 512 + 512]
        r = act(tmp, o, ACT.Square)
        b = PS.get()
        r = mm(b.ap, ones[:, :], tmp, True, True, r, b.rel, inc=True)
        r1, r2 = inv_sqrt(tmp, b.ap, 1.0 / 128, 1e-6, None, r)
        PS.put(b, r1)
        stt(o, o, small[:, 206:207], tmp, ALU.mult, ALU.mult, r2)

    qs = Pool([take(512) for _ in range(2)])
    ks = Pool([take(512) for _ in range(2)])
    ee = Pool([take(512) for _ in range(2)])
    acc = [take(512) for _ in range(2)]
    mt = [take(512) for _ in range(2)]
    qd = take(256).rearrange("p (n m) -> p n m", n=2)
    kdT = take(256).rearrange("p (n m) -> p n m", n=2)
    kdt = take(256).rearrange("p (n m) -> p n m", n=2)
    Sg = take(256).rearrange("p (n m) -> p n m", n=2)
    q4 = gl[:, 0:512]
    k4 = gl[:, 512:1024]
    B4 = Bc.rearrange("p (n m) -> p n m", n=4)
    Btok = V.now()
    A.wait(Btok)
    acc_tok = [None, None]
    def gla_level(s):
        if s == 0:
            qv, kv, rr = q4, k4, [pT[8], pT[9], pT[10], pT[11]]
        else:
            qb, kb, eb = qs.get(), ks.get(), ee.get()
            z1 = G(lambda e, qb=qb: e.memset(qb.ap, 0.0), qb.rel)
            z2 = G(lambda e, kb=kb: e.memset(kb.ap, 0.0), kb.rel)
            nb = 256 // s

            def blocks(ap):
                return ap.rearrange("p (b n) -> p b n", n=2 * s)

            ref = blocks(Bc)[:, :, s - 1:s]
            ev = eb.ap.rearrange("p (w b n) -> p w b n", w=2, n=s)
            tt(V, ev[:, 0], blocks(Bc)[:, :, s:2 * s], bc(ref, [128, nb, s]), ALU.subtract, eb.rel)
            r = tt(V, ev[:, 1], bc(ref, [128, nb, s]), blocks(Bc)[:, :, 0:s], ALU.subtract)
            r = act(eb.ap, eb.ap, ACT.Exp, r)
            tt(V, blocks(qb.ap)[:, :, s:2 * s], blocks(q4)[:, :, s:2 * s], ev[:, 0], ALU.mult, r, z1, z2)
            rr = tt(V, blocks(kb.ap)[:, :, 0:s], blocks(k4)[:, :, 0:s], ev[:, 1], ALU.mult)
            ee.put(eb, rr)
            qv, kv = qb.ap, kb.ap
        mask = bc(K("ident" if s == 0 else f"m{s}").rearrange("p (a n) -> p a n", a=1), [128, 2, 128])
        yield 1
        for t in range(2):
            dst = (acc[t] if s == 0 else mt[t]).rearrange("p (m a n) -> p m a n", m=2, a=2)
            for a in range(2):
                b = PS.get()
                for m in range(2):
                    seg = 2 * m + t
                    k = mm(b.ap[:, m * 128:m * 128 + 128], kv[64 * a:64 * a + 64, seg * 128:seg * 128 + 128],
                           qv[64 * a:64 * a + 64, seg * 128:seg * 128 + 128], True, True, rr, b.rel, inc=(m == 1))
                r = tt(V, dst[:, :, a, :], b.ap[:, 0:256].rearrange("p (m n) -> p m n", m=2), mask, ALU.mult, k,
                       None if s == 0 else acc_tok[t])
                PS.put(b, r)
            acc_tok[t] = r if s == 0 else tt(G, acc[t], acc[t], mt[t], ALU.add, r)
        if s:
            qs.put(qb, k)
            ks.put(kb, k)
        yield 1

    run([diff_unit(h, t) for h in range(4) for t in range(2)], 3,
        chained(*[gla_level(s) for s in (0, 1, 2, 4, 8, 16, 32, 64)]))
    A.wait(V.now())
    diff_norm(0)
    A.wait(V.now())
    diff_norm(1)
    Bq = Bc.rearrange("p (n t m) -> p n t m", n=2, t=2)
    r = act(qd, Bq[:, :, 1, :], ACT.Exp)
    tt(V, qd, qd, gl[:, 0:512].rearrange("p (n t m) -> p n t m", n=2, t=2)[:, :, 1, :], ALU.mult, r)
    r = tt(V, kdT, bc(Bq[:, :, 0, 127:128], [128, 2, 128]), Bq[:, :, 0, :], ALU.subtract)
    r = act(kdT, kdT, ACT.Exp, r)
    r = tt(V, kdT, kdT, gl[:, 512:1024].rearrange("p (n t m) -> p n t m", n=2, t=2)[:, :, 0, :], ALU.mult, r)
    b = PS.get()
    for m in range(2):
        k = tp(b.ap[:, m * 128:m * 128 + 128], kdT[:, m, :], r, b.rel, inc=(m == 1))
    r = cpy(V, kdt, b.ap[:, 0:256].rearrange("p (n m) -> p n m", n=2), k)
    PS.put(b, r)
    b = PS.get()
    for h in range(4):
        base = (h % 2) * 64
        k = mm(b.ap[base:base + 64, (h // 2) * 128:(h // 2) * 128 + 128], kdt[:, h // 2, base:base + 64],
               vd[:, 0, h * 128:h * 128 + 128], True, True, r, b.rel, row_tok, inc=(h == 3))
    r = cpy(V, Sg, b.ap[:, 0:256].rearrange("p (n m) -> p n m", n=2), k)
    PS.put(b, r)
    for h in range(4):
        base = (h % 2) * 64
        b = PS.get()
        mm(b.ap[:, 0:128], vd[:, 0, h * 128:h * 128 + 128], acc[0][:, h * 128:h * 128 + 128], True, True,
           acc_tok[0], acc_tok[1], b.rel, r)
        mm(b.ap[:, 128:256], vd[:, 1, h * 128:h * 128 + 128], acc[1][:, h * 128:h * 128 + 128], True, False)
        k = mm(b.ap[:, 128:256], Sg[base:base + 64, h // 2, :], qd[base:base + 64, h // 2, :], False, True, inc=True)
        r2 = cpy(V, oT[:, 4 + h, :], b.ap[:, 0:256], k)
        PS.put(b, r2)
    for n in range(2):
        r = rms_out(oTf[:, 1024 + n * 512:1536 + n * 512], rT.rearrange("p n m -> p (n m)")[:, n * 512:n * 512 + 512],
                    C("lnw"), 512, tmp, [V.now()])
    banks, k = down([ins["woo"][0], ins["woo"][1]], oT, r)
    lt = norm(banks, k, False)
    lt = ffn(1, 3, lt)

    def gate_row(i):
        g = take(1024).rearrange("p (k n) -> p k n", k=8)
        r = cpy(V, g, bc(mods[:, 24 * i + 16:24 * i + 24].rearrange("p (k a) -> p k a", a=1), [128, 8, 128]))
        for c in range(2):
            b = PS.get()
            for k in range(4):
                m = mm(b.ap[:, 128 * k:128 * k + 128], g[:, 4 * c + k, :], ident, True, True, r, b.rel, inc=(k == 3))
            m = cpy(V, gate[:, 512 * c:512 * c + 512], b.ap, m)
            PS.put(b, m)

    open_stage(17000, mark[0], False)
    xt = transposed(lt, after(3), rows_of[0])
    rows_of[0] = load_rows(4)
    qk = take(16 * 256).rearrange("p (n m) -> p n m", n=16)
    vs = take(2048).rearrange("p (t n) -> p t n", t=2)
    oT = take(2048).rearrange("p (n m) -> p n m", n=8)
    tables("natural_log_exp_and_others")
    pT = {}

    def evac_sb(c0):
        def f(c, ps, r):
            n = c0 + c
            r = ts(V, qk[:, n, :], ps, 0.125, None, ALU.mult, None, r) if n < 8 else cpy(A, qk[:, n, :], ps, r)
            pT[n] = r
            return r
        return f

    run([proj_T(ins["ws"][j], 4, xt, evac_sb(4 * j)) for j in range(4)], 1, adaln(2))
    row_tok = []
    run([proj_rows(ins["ws"][4 + j], 512, xt, evac_rows(vs, 512 * j, A if j else V)) for j in range(2)], 1)
    gate_row(0)
    az = Pool([take(384) for _ in range(5)])
    sp = Pool([take(384) for _ in range(5)])

    def diag(ap):
        return ap.rearrange("p (n m) -> p n m", n=3)[:, 0:3:2, :]

    def keep(ap, tok):
        return G(lambda e: e.affine_select(out=diag(ap), in_=diag(ap), compare_op=ALU.is_gt, fill=0.0, base=0,
                                           pattern=[[0, 2], [1, 128]], channel_multiplier=-1), tok)

    sb_tok = []

    def sb_unit(h):
        base, n = (h % 2) * 64, h // 2
        zb = PS.get()
        kk, qq = qk[base:base + 64, 8 + n, :], qk[base:base + 64, n, :]
        mm(zb.ap[:, 0:256], kk[:, 0:128], qq, True, False, zb.rel, pT[n], pT[8 + n])
        r = mm(zb.ap[:, 256:384], kk[:, 128:256], qq[:, 128:256], False, False, inc=True)
        a, s = az.get(), sp.get()
        z = zb.ap[:, 0:384]
        act(a.ap, z, ACT.Abs, r, a.rel)
        act(a.ap, a.ap, ACT.Exp, scale=-1.0)
        r = act(a.ap, a.ap, ACT.Ln, bias=1.0)
        r = stt(s.ap, z, 0.0, a.ap, ALU.max, ALU.add, r, s.rel)
        r = keep(s.ap, r)
        yield 1
        mm(zb.ap[:, 0:256], K("ntri"), s.ap[:, 0:256], False, False, r)
        mm(zb.ap[:, 128:256], neg1[:, :], s.ap[:, 256:384], False, False)
        k = mm(zb.ap[:, 256:384], K("ntri"), s.ap[:, 256:384], False, True, inc=True)
        sp.put(s, k)
        r = act(a.ap, zb.ap[:, 0:384], ACT.Exp, k)
        PS.put(zb, r)
        r = keep(a.ap, r)
        yield 1
        b = PS.get()
        o = b.ap[base:base + 64, :]
        mm(o[:, 0:256], vs[:, 0, h * 64:h * 64 + 64], a.ap[:, 0:256], True, False, r, b.rel, row_tok)
        k = mm(o[:, 128:256], vs[:, 1, h * 64:h * 64 + 64], a.ap[:, 256:384], False, True, inc=True)
        az.put(a, k)
        r = cpy(V, oT[base:base + 64, n, :], o[:, 0:256], k)
        PS.put(b, r)
        sb_tok.append(r)
        yield 1

    run([sb_unit(h) for h in range(16)], 4)
    banks, k = down([ins["wso"][0], ins["wso"][1]], oT, sb_tok)
    lt = norm(banks, k, True)

    def moe(l, i, tok, last=False):
        xsp = open_stage(8000, mark[0])
        hsp = stage[0].enter_context(nc.sbuf_tensor(f"hsplit{l}", [128, 2, 2, 4, 256], F32R))
        xt = transposed(tok, after(3 + i), rows_of[0], xsp)
        rows_of[0] = load_rows(4 + i)
        accv = take(2048).rearrange("p (t n) -> p t n", t=2)
        rw = C("rw").rearrange("p (k n) -> p k n", k=8)
        b = PS.get()
        for t in range(2):
            for k in range(8):
                r = mm(b.ap[:, 16 * t:16 * t + 16], xT[:, k, t * 128:t * 128 + 128], rw[:, k, :], k == 0, k == 7,
                       b.rel, xt, inc=(k == 7))

        def s32(n):
            return small[:, 220 + 32 * n:252 + 32 * n]

        def tv(ap):
            return ap.rearrange("p (t n) -> p t n", t=2)

        def t1(ap, n=16):
            return bc(ap.rearrange("p (t a) -> p t a", a=1), [128, 2, n])

        def g1(ap):
            return bc(ap.rearrange("p (g a) -> p g a", a=1), [128, 8, 4])

        def gv(ap):
            return ap.rearrange("p (g n) -> p g n", n=4)

        def red(o, i, op=ALU.max):
            return V(lambda e: e.tensor_reduce(o, i, X, op))

        L, Pn, Mk, O1, O2, W = (s32(n) for n in range(6))
        q = small[:, 412:560]
        r = tt(V, tv(L), b.ap[:, 0:32].rearrange("p (t n) -> p t n", t=2),
               bc(R("rtb").rearrange("p (a n) -> p a n", a=1), [128, 2, 16]), ALU.add, r)
        PS.put(b, r)
        red(q[:, 0:2], tv(L))
        r = tt(V, tv(Pn), tv(L), t1(q[:, 0:2]), ALU.subtract)
        r = act(Pn, Pn, ACT.Exp, r)
        V(lambda e: e.tensor_reduce(q[:, 2:4], tv(Pn), X, ALU.add), r)
        V(lambda e: e.reciprocal(q[:, 4:6], q[:, 2:4]))
        tt(V, tv(Pn), tv(Pn), t1(q[:, 4:6]), ALU.mult)
        prs = [(0, 1), (0, 2), (0, 3), (1, 2), (1, 3), (2, 3)]
        pr = q[:, 8:56].rearrange("p (g n) -> p g n", n=6)
        for n, (a1, b1) in enumerate(prs):
            tt(V, pr[:, :, n:n + 1], gv(Pn)[:, :, a1:a1 + 1], gv(Pn)[:, :, b1:b1 + 1], ALU.add)
        gsc = q[:, 56:64]
        red(gsc, pr)
        g2 = gsc.rearrange("p (t n) -> p t n", t=2)

        def first(dst, src, width, wts, mx):
            red(mx, src)
            tt(V, dst, src, t1(mx, width), ALU.is_equal)
            tt(V, dst, dst, wts, ALU.mult)
            red(q[:, 72:74], dst)
            return tt(V, dst, dst, t1(q[:, 72:74], width), ALU.is_equal)

        sel = q[:, 64:72]
        first(sel.rearrange("p (t n) -> p t n", t=2), g2, 4, K("g4").rearrange("p (t n) -> p t n", t=2), q[:, 74:76])
        ts(V, sel, sel, 1.0, 1e30, ALU.subtract, ALU.mult)
        tt(V, gv(Mk), gv(L), g1(sel), ALU.add)
        first(tv(O1), tv(Mk), 16, tv(K("e16")), q[:, 76:78])
        stt(Mk, O1, -1e32, Mk, ALU.mult, ALU.add)
        first(tv(O2), tv(Mk), 16, tv(K("e16")), q[:, 78:80])
        r = tt(V, q[:, 80:82], q[:, 78:80], q[:, 76:78], ALU.subtract)
        r = act(q[:, 80:82], q[:, 80:82], ACT.Exp, r)
        ts(V, q[:, 82:84], q[:, 80:82], 1.0, None, ALU.add, None, r)
        V(lambda e: e.reciprocal(q[:, 84:86], q[:, 82:84]))
        tt(V, q[:, 86:88], q[:, 80:82], q[:, 84:86], ALU.mult)
        tt(V, tv(O1), tv(O1), t1(q[:, 84:86]), ALU.mult)
        tt(V, tv(O2), tv(O2), t1(q[:, 86:88]), ALU.mult)
        tt(V, W, O1, O2, ALU.add)
        tables("silu_and_others")
        hp = Pool([hsp[:, n] for n in range(2)])
        sg = Pool([take(256) for _ in range(4)])
        out_tok = [None]

        def hidden(e):
            g, u = (tiles_of(ins[n][l * 16 + e], 4) for n in ("mg", "mu"))
            return g + u

        plan = hidden(0)
        for e in range(16):
            plan += (hidden(e + 1) if e < 15 else []) + rows_of_piece(ins["md"][l * 16 + e])
        get = stream(plan)

        def expert(e):
            hb = hp.get()
            hh, hl = hb.ap[:, 0], hb.ap[:, 1]
            s4 = [sg.get() for _ in range(4)]
            for f in range(4):
                b = PS.get()
                m = tile3(b.ap[:, 0:256], get, xsp, True, xt, b.rel)
                r = act(s4[f].ap, b.ap[:, 0:256], ACT.Silu, m, s4[f].rel)
                PS.put(b, r)
            for f in range(4):
                b = PS.get()
                m = tile3(b.ap[:, 0:256], get, xsp, True, xt, b.rel)
                y = s4[f].ap
                q = tt(V, y, y, b.ap[:, 0:256], ALU.mult, m, r)
                PS.put(b, q)
                q = cpy(A, hh[:, f, :], y, q, hb.rel)
                hk = tt(G, hl[:, f, :], y, hh[:, f, :].bitcast(F32), ALU.subtract, q, hb.rel)
                sg.put(s4[f], hk)
            yield 1
            banks = [PS.get() for _ in range(4)]
            for f in range(4):
                buf, hi, lo, r = get()
                for t in range(2):
                    for c in range(2):
                        b = banks[2 * t + c]
                        cc = slice(c * 512, c * 512 + 512)
                        for n, (a, w) in enumerate(((hh, hi), (hh, lo), (hl, hi))):
                            m = mm(b.ap, a[:, f, t * 128:t * 128 + 128], w[:, cc], f == 0 and n == 0, f == 3 and n == 2,
                                   r, hk, b.rel, inc=(n == 2))
                        if f == 3:
                            o = accv[:, t, cc]
                            w = W[:, 16 * t + e:16 * t + e + 1]
                            if e == 0:
                                v = ts(V, o, b.ap, w, None, ALU.mult, None, m)
                            else:
                                v = stt(o, b.ap, w, o, ALU.mult, ALU.add, m)
                            PS.put(b, v)
                stage[3].put(buf, m)
            out_tok[0] = v
            hp.put(hb, m)
            yield 1

        ex = [expert(e) for e in range(16)]
        next(ex[0])
        for e in range(16):
            if e < 15:
                next(ex[e + 1])
            next(ex[e])
        v = out_tok[0]
        gate_row(i)
        return norm(accv, [v, v], True, rows_of[0] if last else None)

    lt = moe(0, 1, lt)

    open_stage(24800, mark[0], False)
    xt = transposed(lt, after(5), rows_of[0])
    rows_of[0] = load_rows(6)
    tables("silu_and_others")
    qk = take(16 * 256).rearrange("p (n m) -> p n m", n=16)
    gTf = take(16 * 256)
    gT = gTf.rearrange("p (n m) -> p n m", n=16)
    vr = take(4096).rearrange("p (t n) -> p t n", t=2)
    dec = take(2048)
    cs_ = take(512)
    tmpr = Pool([take(512) for _ in range(3)])
    A.raw(lambda e: e.dma_start(dec, ins["dec"]).then_inc(s_dec, 16))
    A.raw(lambda e: e.dma_start(posi[:, :], ins["pos"].broadcast_to([128, 256])).then_inc(s_dec, 16))
    DEC = (s_dec, 32)
    cosT, sinT = cs_[:, 0:256], cs_[:, 256:512]
    tb = tmpr.get()
    ang, kq = tb.ap[:, 0:256], tb.ap[:, 256:512]
    cpy(V, ang, posi[:, :], DEC)
    ts(V, ang, ang, K("freq"), None, ALU.mult, None)
    ki = posi[:, :]
    C1, C2 = 6.28125, 2 * math.pi - 6.28125
    C2a = float(np.float32(np.round(C2 * 2 ** 20) / 2 ** 20))
    C2b = C2 - C2a
    for dst, shift in ((sinT, 0.0), (cosT, 0.25)):
        ts(V, kq, ang, 1.0 / (2 * math.pi), shift, ALU.mult, ALU.add)
        cpy(V, ki, kq)
        cpy(V, kq, ki)
        stt(dst, kq, -C1, ang, ALU.mult, ALU.add)
        stt(dst, kq, -C2a, dst, ALU.mult, ALU.add)
        stt(dst, kq, -C2b, dst, ALU.mult, ALU.add)
        if shift:
            ts(V, dst, dst, math.pi / 2, None, ALU.add, None)
        r = ts(V, dst, dst, math.pi, -math.pi, ALU.min, ALU.max)
        rc = act(dst, dst, ACT.Sin, r)
    tmpr.put(tb, V.now())
    qtok = {}

    def evac_ret(c0):
        def f(c, ps, r):
            n = c0 + c
            if n >= 16:
                r = act(gT[:, n - 16, :], ps, ACT.Silu, r)
                return r
            tb = tmpr.get()
            raw, t2 = tb.ap[:, 0:256], tb.ap[:, 256:512]
            rel = act(raw, ps, ACT.Copy, r, tb.rel, scale=1.0 if n < 8 else 128 ** -0.5)
            b = PS.get()
            k = mm(b.ap[:, 0:256], K("rot"), raw, True, True, rel, b.rel, inc=True)
            r1 = tt(V, t2, b.ap[:, 0:256], sinT, ALU.mult, k, rc)
            PS.put(b, r1)
            tt(V, raw, raw, cosT, ALU.mult)
            qtok[n] = tt(V, qk[:, n, :], raw, t2, ALU.add)
            tmpr.put(tb, qtok[n])
            return rel
        return f

    run([proj_T(ins["wr"][j], 4, xt, evac_ret(4 * j)) for j in range(8)], 1, adaln(3))
    row_tok = []
    run([proj_rows(ins["wrv"][j], 512, xt, evac_rows(vr, 512 * j, A if j % 2 else V)) for j in range(4)], 1)
    gate_row(2)
    tables("natural_log_exp_and_others")
    rtmp = Pool([take(384) for _ in range(3)])
    otmp = Pool([take(512) for _ in range(3)])
    gtok = A.now()
    ret_tok = []

    def ret_unit(h):
        b = PS.get()
        mm(b.ap[:, 0:256], qk[:, 8 + h, 0:128], qk[:, h, :], True, True, b.rel, qtok[h], qtok[8 + h])
        k = mm(b.ap[:, 256:384], qk[:, 8 + h, 128:256], qk[:, h, 128:256], True, True, inc=True)
        p = rtmp.get()
        tt(V, p.ap[:, 0:256], b.ap[:, 0:256], dec[:, h * 256:h * 256 + 256], ALU.mult, k, p.rel, DEC)
        r = tt(V, p.ap[:, 256:384], b.ap[:, 256:384], dec[:, h * 256:h * 256 + 128], ALU.mult)
        PS.put(b, r)
        yield 1
        b = PS.get()
        for d in range(2):
            c = h * 256 + d * 128
            mm(b.ap[:, d * 256:d * 256 + 256], vr[:, 0, c:c + 128], p.ap[:, 0:256], True, False, r, b.rel, row_tok)
            k = mm(b.ap[:, d * 256 + 128:d * 256 + 256], vr[:, 1, c:c + 128], p.ap[:, 256:384], False, True, inc=True)
        rtmp.put(p, k)
        o = otmp.get()
        r = cpy(A, o.ap, b.ap, k, o.rel)
        PS.put(b, r)
        yield 1
        b = PS.get()
        mm(b.ap[:, 0:256], ones[:, :], o.ap[:, 0:256], True, False, r, b.rel)
        k = mm(b.ap[:, 0:256], ones[:, :], o.ap[:, 256:512], False, True, inc=True)
        for d in range(2):
            r = stt(o.ap[:, d * 256:d * 256 + 256], b.ap[:, 0:256], -1.0 / 256, o.ap[:, d * 256:d * 256 + 256],
                    ALU.mult, ALU.add, k)
        PS.put(b, r)
        tb = tmpr.get()
        r = act(tb.ap, o.ap, ACT.Square, r, tb.rel)
        yield 1
        b = PS.get()
        mm(b.ap[:, 0:256], ones[:, :], tb.ap[:, 0:256], True, False, r, b.rel)
        k = mm(b.ap[:, 0:256], ones[:, :], tb.ap[:, 256:512], False, True, inc=True)
        r1, r2 = inv_sqrt(tb.ap[:, 0:256], b.ap[:, 0:256], 1.0 / 256, 1e-5, None, k)
        PS.put(b, r1)
        for d in range(2):
            od = o.ap[:, d * 256:d * 256 + 256]
            tt(V, od, od, tb.ap[:, 0:256], ALU.mult, r2)
            r = stt(gT[:, 2 * h + d, :], od, C("rgn", 2 * h + d, 2 * h + d + 1), gT[:, 2 * h + d, :],
                    ALU.mult, ALU.mult, gtok)
        tmpr.put(tb, r)
        otmp.put(o, r)
        ret_tok.append(r)
        yield 1

    run([ret_unit(h) for h in range(8)], 3)
    banks, k = down([ins["wro"][j] for j in range(4)], gT, ret_tok)
    lt = norm(banks, k, True)
    moe(1, 3, lt, True)
    A.wait((s_out, 32))
    A.wait(*[q.now() for q in (T, V, G)])

    stage[0].close()
    block = ctx.enter_context(nc.Block())

    @block.tensor
    def _(e):
        for f in T.ops:
            f(e)

    @block.vector
    def _(e):
        for f in V.ops:
            f(e)

    @block.scalar
    def _(e):
        for f in A.ops:
            f(e)

    @block.gpsimd
    def _(e):
        for f in G.ops:
            f(e)

    @block.sync
    def _(e):
        for f in S.ops:
            f(e)


def kernel(**inputs):
    import numpy as _np
    import concourse.bacc as _bacc
    from concourse import mybir as _mybir
    from concourse.bass_utils import run_bass_kernel_spmd as _run

    a = {k: _np.ascontiguousarray(v) for k, v in inputs.items()}

    def tiles(w, kt, cols):
        n = w.shape[1] // cols
        return w.reshape(kt, 128, n, cols).transpose(2, 1, 0, 3).reshape(n, 128, kt * cols)

    def rowtiles(w, kt):
        n = w.shape[0] // (kt * 128)
        return w.reshape(n, kt, 128, w.shape[1]).transpose(0, 2, 1, 3).reshape(n, 128, kt * w.shape[1])

    def col(v, n):
        v = v.reshape(-1, n, 128)
        return v.transpose(2, 1, 0).reshape(128, -1)

    def pad(v):
        return _np.concatenate([v, _np.zeros((128 - v.shape[0], v.shape[1]), v.dtype)])

    we, wo = a["w_in_even"][0], a["w_in_odd"][0]
    ins = {"x": a["x"][0]}
    ins["we"] = tiles(_np.concatenate([we[:, 0:3072], we[:, 3084:4620]], 1), 8, 512)
    ins["wev"] = tiles(we[:, 4620:5132], 8, 512)
    ins["wev2"] = tiles(we[:, 5132:5388], 8, 256)
    ins["woe"] = rowtiles(a["w_out_even"][0], 4)
    ins["woo"] = rowtiles(a["w_out_odd"][0], 4)
    ins["wo"] = tiles(_np.concatenate([wo[:, 0:1024], wo[:, 1536:2048], wo[:, 2560:3072]], 1), 8, 512)
    ins["wov"] = tiles(_np.concatenate([wo[:, 1024:1536], wo[:, 2048:2560]], 1), 8, 512)
    for l in range(2):
        u = a["ffn_w_up"][l].reshape(1024, 2, 11, 256).transpose(0, 2, 1, 3).reshape(1024, 5632)
        ins[f"wu{l}"] = tiles(u, 8, 512)
        d = a["ffn_w_down"][l]
        ins[f"wd{l}"] = rowtiles(d[0:2560], 4)
        ins[f"wdl{l}"] = rowtiles(d[2560:2816], 2)
    ins["ada"] = _np.concatenate([tiles(w, 8, 512) for w in a["ada_w_2"].reshape(4, 1024, 3072)])
    ins["ws"] = tiles(a["sb_w_in_2"][0], 8, 512)
    ins["wso"] = rowtiles(a["sb_w_out_2"][0], 4)
    wr = a["ret_w_in_2"][0]
    ins["wr"] = tiles(_np.concatenate([wr[:, 0:2048], wr[:, 4096:6144]], 1), 8, 512)
    ins["wrv"] = tiles(wr[:, 2048:4096], 8, 512)
    ins["wro"] = rowtiles(a["ret_w_out_2"][0], 4)
    ins["mg"] = _np.concatenate([tiles(w, 8, 512) for w in a["moe_w_gate_2"].reshape(32, 1024, 512)])
    ins["mu"] = _np.concatenate([tiles(w, 8, 512) for w in a["moe_w_up_2"].reshape(32, 1024, 512)])
    ins["md"] = _np.concatenate([rowtiles(w, 4) for w in a["moe_w_down_2"].reshape(32, 512, 1024)])
    adab = a["ada_b_2"].reshape(4, 3072)
    g1, b1 = a["ln_g"].reshape(4, 1024), a["ln_b"].reshape(4, 1024)
    g2, b2 = a["ln_g_2"].reshape(4, 1024), a["ln_b_2"].reshape(4, 1024)
    par = {
        "gconv": col(a["gdn_conv_w"][0], 18), "fw0": col(a["ffn_conv_w"][0], 44), "fb0": col(a["ffn_conv_b"][0], 44),
        "fw1": col(a["ffn_conv_w"][1], 44), "fb1": col(a["ffn_conv_b"][1], 44), "gnw": col(a["gdn_norm_w"][0], 1),
        "dnw": col(a["diff_norm_w"][0], 1), "lnw": col(a["gla_norm_w"][0], 1), "lbg": col(a["gla_b_gate"][0], 2),
        "rgn": col(a["ret_gn_g_2"][0], 16), "adab": _np.concatenate([col(b, 24) for b in adab], 1),
        "lng": _np.concatenate([col(v, 8) for v in _np.concatenate([g1, g2])], 1),
        "lnb": _np.concatenate([col(v, 8) for v in _np.concatenate([b1, b2])], 1),
        "c": col(a["c_2"][0], 8), "dl": pad(a["diff_lambda"][0].T), "rb": pad(a["rel_bias"]),
        "lwg": pad(a["gla_w_gate"][0]), "rw": tiles(a["router_w_2"], 8, 16)[0],
        "wba": tiles(we[:, 3072:3084], 8, 12)[0], "wgd": tiles(wo[:, 3072:3088], 8, 16)[0],
    }
    assert all(par[n].shape == (128, w) for n, w in PARAMS), {n: par[n].shape for n, _ in PARAMS}
    ins["cp"] = _np.concatenate([par[n] for n, _ in PARAMS], 1)
    ins["rp"] = _np.concatenate([a["gdn_a_log"][0], a["gdn_dt_bias"][0], a["router_b_2"]])[None, :]
    rows = []
    for g, b in zip(_np.concatenate([g1, g2]), _np.concatenate([b1, b2])):
        rows += [g, b]
    ins["rows"] = _np.stack(rows)
    ins["kc"], _, ins["dec"] = consts()
    ins["pos"] = a["positions_2"]

    nc = _bacc.Bacc("TRN2", target_bir_lowering=False, num_devices=1)
    arrays, args = {}, {}
    for name, v in ins.items():
        v = _np.ascontiguousarray(v)
        arrays[f"in_{name}"] = v
        args[name] = nc.dram_tensor(f"in_{name}", v.shape, _mybir.dt.from_np(v.dtype), kind="ExternalInput").ap()
    out = nc.dram_tensor("out_0", (256, 1024), _mybir.dt.float32, kind="ExternalOutput").ap()
    build(nc, args, out)
    r = _run(nc, [arrays], core_ids=[0])
    return r.results[0]["out_0"].reshape(1, 256, 1024)
```

```python
import math
from contextlib import ExitStack

import numpy as np
import concourse.bass as bass
from concourse import mybir

F32 = mybir.dt.float32
F32R = mybir.dt.float32r
I32 = mybir.dt.int32
ALU = mybir.AluOpType
ACT = mybir.ActivationFunctionType
X = mybir.AxisListType.X
ALPHA = 4 ** 0.25
LAM0 = 0.8 - 0.6 * math.exp(-0.3)
SLOTS = 3
NEG = -1e30


class Queue:

    def __init__(self, sem, link):
        self.sem, self.link, self.ops, self.n, self.seen = sem, link, [], 0, {}
        self.loose = False

    def wait(self, *toks):
        for tok in toks:
            if tok is None:
                continue
            if isinstance(tok, list):
                self.wait(*tok)
                continue
            sem, v = tok
            if self.seen.get(id(sem), 0) < v:
                self.seen[id(sem)] = v
                self.ops.append(lambda e, s=sem, v=v: e.wait_ge(s, v))

    def __call__(self, fn, *toks, inc=True):
        self.wait(*toks)
        if self.link and self.n and not self.loose:
            self.wait((self.sem, self.n))
        if inc:
            self.n += 1
            self.ops.append(lambda e: fn(e).then_inc(self.sem, 1))
            return (self.sem, self.n)
        self.ops.append(fn)
        return None

    def raw(self, fn):
        self.ops.append(fn)

    def now(self):
        return (self.sem, self.n) if self.n else None


class Buf:
    def __init__(self, ap):
        self.ap, self.rel = ap, []


class Pool:

    def __init__(self, aps):
        self.free = [Buf(a) for a in aps]

    def get(self):
        return self.free.pop(0)

    def put(self, buf, *toks):
        buf.rel = [t for t in toks if t is not None]
        self.free.append(buf)


def consts():
    f = np.float32
    p = np.arange(128)[:, None]
    i = np.arange(128)[None, :]
    out, at = [], {}

    def add(name, a):
        a = np.asarray(a, f)
        if a.shape[0] < 128:
            a = np.concatenate([a, np.zeros((128 - a.shape[0], a.shape[1]), f)])
        at[name] = (sum(x.shape[1] for x in out), a.shape[1])
        out.append(a)

    add("ident", p == i)
    add("exch", p + i == 127)
    rot = np.zeros((128, 128), f)
    for m in range(64):
        rot[m + 64, m] = -1.0
        rot[m, m + 64] = 1.0
    add("rot", rot)
    add("tri", p <= i)
    add("ntri", -(p >= i).astype(f))
    add("cmt", np.where(i < p, f(NEG), f(0)))
    for s in (1, 2, 4, 8, 16, 32, 64):
        add(f"m{s}", (p // (2 * s) == i // (2 * s)) & (p % (2 * s) < s) & (i % (2 * s) >= s))
    y = np.arange(256)[None, :]
    rel = p + 128 - y
    for n, d in enumerate((1, 4, 16)):
        ok = (rel >= 0) & (rel <= 128 * d) & (rel % d == 0)
        add(f"dm{n}", np.where(ok, f(0), f(NEG)))
    add("cm", np.where(rel >= 0, f(0), f(NEG)))
    dist = 255 - np.arange(384)
    d = np.maximum(dist, 1).astype(f)
    large = 16 + (np.log(d / f(16)) / f(math.log(128.0)) * f(16)).astype(np.int32)
    b = np.where(dist < 16, dist, np.minimum(large, 31))
    add("hot", (b[None, :] == np.arange(32)[:, None]) & (dist >= 0)[None, :])
    add("freq", np.tile((1.0 / (f(10000.0) ** (np.arange(0, 128, 2).astype(f) / f(128)))).astype(f), 2)[:, None])
    add("iota", np.broadcast_to(np.arange(128), (128, 128)))
    add("e16", np.broadcast_to(16.0 - (np.arange(32) % 16), (128, 32)))
    add("g4", np.broadcast_to(4.0 - (np.arange(8) % 4), (128, 8)))
    lg = np.log(f(1) - np.exp2(f(-5) - np.arange(8).astype(f))).astype(f)
    yy = np.arange(256)[None, :]
    dec = [np.where(yy >= p, np.exp(np.maximum(yy - p, 0).astype(f) * lg[h]), f(0)) for h in range(8)]
    return np.concatenate(out, 1).astype(f), at, np.concatenate(dec, 1).astype(f)


PARAMS = [("gconv", 72), ("fw0", 132), ("fb0", 44), ("fw1", 132), ("fb1", 44), ("gnw", 1), ("dnw", 1),
          ("lnw", 1), ("lbg", 2), ("rgn", 16), ("adab", 96), ("lng", 64), ("lnb", 64), ("c", 8), ("dl", 4), ("rb", 4),
          ("lwg", 256), ("rw", 128), ("wba", 96), ("wgd", 128)]
ROWS = [("alog", 6), ("dtb", 6), ("rtb", 16)]


def offsets(spec):
    at, n = {}, 0
    for name, w in spec:
        at[name] = (n, w)
        n += w
    return at, n


def build(nc, ins, out):
    ctx = ExitStack()
    with ctx:
        emit(nc, ctx, ins, out)


def emit(nc, ctx, ins, out):
    _, kat, _ = consts()
    pat, npar = offsets(PARAMS)
    rat, nrow = offsets(ROWS)
    ncon = ins["kc"].shape[1]

    def sb(name, cols, dt=F32):
        return ctx.enter_context(nc.sbuf_tensor(name, [128, cols], dt))

    def sem(name):
        return ctx.enter_context(nc.semaphore(name))

    ring = sb("ring", SLOTS * 4096)
    kc = sb("kc_sb", ncon)
    cp = sb("cp_sb", npar)
    rp = sb("rp_sb", nrow)
    ones = sb("ones", 128)
    neg1 = sb("neg1", 128)
    half = sb("half", 16)
    xs = sb("xs", 2048)
    xTs = sb("xTs", 2048)
    lnp = sb("lnp", 2048)
    gate = sb("gate", 1024)
    mods = sb("mods", 96)
    lnc = sb("lnc", 128)
    tmpn = sb("tmpn", 1024)
    TPs = sb("TPs", 1024)
    small = sb("small", 640)
    adacc = tmpn
    posi = sb("posi", 256, I32)
    psum = ctx.enter_context(nc.psum_tensor("ps", [128, 8, 512], F32))
    scratch = nc.dram_tensor("scratch", [4, 384], F32)

    T = Queue(sem("s_pe"), False)
    V = Queue(sem("s_dve"), True)
    A = Queue(sem("s_act"), True)
    G = Queue(sem("s_pool"), True)
    S = Queue(sem("s_sp"), False)
    s_par = sem("s_par")
    s_ring = [sem(f"s_ring{i}") for i in range(SLOTS)]
    s_row = sem("s_row")
    s_dec = sem("s_dec")
    s_scr = sem("s_scr")
    s_hank = sem("s_hank")
    s_out = sem("s_out")

    PS = Pool([psum[:, i, :] for i in range(8)])

    def K(name):
        o, w = kat[name]
        return kc[:, o:o + w]

    def C(name, a=0, b=None):
        o, w = pat[name]
        return cp[:, o + a:o + (w if b is None else b)]

    def R(name):
        o, w = rat[name]
        return rp[:, o:o + w]

    ident = K("ident")
    x = xs[:, :].rearrange("p (t n) -> p t n", t=2)
    xT = xTs[:, :].rearrange("p (k n) -> p k n", k=8)

    def mm(o, l, r, start, stop, *toks, inc=False):
        return T(lambda e: e.matmul(o, l, r, start=start, stop=stop, skip_group_check=True), *toks, inc=inc)

    def tp(o, i, *toks, inc=False):
        n = i.shape[0]
        return T(lambda e: e.transpose(o, i, ident[0:n, 0:n]), *toks, inc=inc)

    def act(o, i, f, *toks, **kw):
        return A(lambda e: e.activation(o, i, f, **kw), *toks)

    def tt(q, o, a, b, op, *toks):
        return q(lambda e: e.tensor_tensor(o, a, b, op), *toks)

    def ts(q, o, a, s1, s2, op0, op1, *toks):
        if s2 is None:
            return q(lambda e: e.tensor_scalar(o, a, s1, None, op0), *toks)
        return q(lambda e: e.tensor_scalar(o, a, s1, s2, op0, op1), *toks)

    def stt(o, a, s, b, op0, op1, *toks):
        return V(lambda e: e.scalar_tensor_tensor(out=o, in0=a, scalar=s, in1=b, op0=op0, op1=op1), *toks)

    def cpy(q, o, i, *toks):
        if q is A:
            return act(o, i, ACT.Copy, *toks)
        return q(lambda e: e.tensor_copy(o, i), *toks)

    def bc(ap, shape):
        return ap.broadcast_to(shape)

    def tables(name):
        A.raw(lambda e: e.preload_act_table_set(name))

    nload = [0]
    ring_rel = [[] for _ in range(SLOTS)]

    def load(src, kt):
        n = nload[0]
        nload[0] += 1
        s = n % SLOTS
        w = 4096 if callable(src) else src.shape[1]
        S.wait(*ring_rel[s], PAR if n == 1 else None)
        dst = ring[:, s * 4096:s * 4096 + w]
        S.raw(lambda e: e.dma_start(dst, src() if callable(src) else src).then_inc(s_ring[s], 16))
        view = dst.rearrange("p (k n) -> p k n", k=kt)
        return view, (s_ring[s], 16 * (n // SLOTS + 1)), s

    def done(s, tok):
        ring_rel[s] = [tok]

    top = [0]
    stage = [None, None, 0, None]

    def open_stage(cols, toks, split=True):
        if stage[0] is not None:
            stage[0].close()
        stage[0] = ExitStack()
        stage[2] = cols
        n = nstage[0]
        nstage[0] += 1
        stage[1] = stage[0].enter_context(nc.sbuf_tensor(f"arena{n}", [128, cols], F32))
        top[0] = 0
        for q in (V, A, G):
            q.wait(*toks)
        if not split:
            return None
        w = stage[0].enter_context(nc.sbuf_tensor(f"wsplit{n}", [128, 4, 2, 1024], F32R))
        xsp = stage[0].enter_context(nc.sbuf_tensor(f"xsplit{n}", [128, 2, 8, 256], F32R))
        stage[3] = Pool([w[:, i, :, :] for i in range(4)])
        return xsp

    def take(cols):
        a = top[0]
        top[0] += cols
        assert top[0] <= stage[2], (top[0], stage[2])
        return stage[1][:, a:a + cols]

    nstage = [0]

    def when(flag, fill):
        queues = (T, V, A, G, S)
        before = [(len(q.ops), q.n, dict(q.seen)) for q in queues]
        loads = nload[0]
        fill()
        for q, (k, n, seen) in zip(queues, before):
            body = q.ops[k:]
            if not body:
                continue
            del q.ops[k:]
            q.seen = seen
            if q is S:
                skip = []
                for i in range(SLOTS):
                    c0, c1 = (len(range(i, m, SLOTS)) for m in (loads, nload[0]))
                    skip.append((s_ring[i], 16 * c0, 16 * (c1 - c0)))
            else:
                skip = [(q.sem, n, q.n - n)]

            def op(e, body=body, skip=skip, r=flag[q]):
                with e.If(r[0] > 0):
                    for f in body:
                        f(e)
                with e.Else():
                    for sem_, have, add in skip:
                        e.wait_ge(sem_, have)
                        e.sem_inc(sem_, add)

            q.ops.append(op)

    def snap():
        return [q.now() for q in (T, V, A, G)]

    def run(gens, width, fill=None):
        gens, live = list(gens), []
        while gens or live:
            while gens and len(live) < width:
                live.append(gens.pop(0))
            for g in list(live):
                if next(g, 0) == 0:
                    live.remove(g)
            if fill is not None and next(fill, 0) == 0:
                fill = None
        for _ in fill or ():
            pass

    A.raw(lambda e: e.dma_start(kc[:, :], ins["kc"]).then_inc(s_par, 16))
    A.raw(lambda e: e.dma_start(cp[:, :], ins["cp"]).then_inc(s_par, 16))
    A.raw(lambda e: e.dma_start(rp[:, :], ins["rp"].broadcast_to([128, nrow])).then_inc(s_par, 16))
    A.raw(lambda e: e.dma_start(x[:, 0, :], ins["x"][0:128, :]).then_inc(s_par, 16))
    A.raw(lambda e: e.dma_start(x[:, 1, :], ins["x"][128:256, :]).then_inc(s_par, 16))
    PAR = (s_par, 80)
    m1 = G(lambda e: e.memset(ones[:, :], 1.0))
    m2 = G(lambda e: e.memset(neg1[:, :], -1.0))
    m3 = G(lambda e: e.memset(half[:, :], -0.5))
    for q in (T, V, A, G):
        q.wait(PAR, m3)
    gxt = [None]
    nrows = [0]

    def load_rows(i):
        G.wait(G.now())
        for c in range(2):
            dst = lnp[:, 1024 * c:1024 * c + 1024]
            r = 2 * i + c
            G.raw(lambda e, dst=dst, r=r: e.dma_start(dst, ins["rows"][r:r + 1, :].broadcast_to([128, 1024]))
                  .then_inc(s_row, 16))
            nrows[0] += 1
        return (s_row, 16 * nrows[0])

    open_stage(24800, [], False)
    top[0] = 23000
    hrow = take(384)
    hank = take(1024)
    b = PS.get()
    t = mm(b.ap[0:4, 0:384], C("rb")[0:32, :], K("hot")[0:32, :], True, True, inc=True)
    t = cpy(V, hrow[0:4, :], b.ap[0:4, 0:384], t)
    PS.put(b, t)
    A.wait(t)
    A.raw(lambda e: e.dma_start(scratch[:, :], hrow[0:4, :]).then_inc(s_scr, 16))
    A.wait((s_scr, 16))
    hsrc = bass.AP(tensor=scratch[:, :].tensor, offset=0, ap=[[1, 128], [384, 4], [1, 256]])
    A.raw(lambda e: e.dma_start(hank.rearrange("p (h n) -> p h n", h=4), hsrc).then_inc(s_hank, 16))
    def transposed(toks, cols=None, rows=None, split=None):
        last = []
        for t in range(2):
            for kp in range(2):
                b = PS.get()
                for k in range(4):
                    f = 4 * kp + k
                    r = tp(b.ap[:, 128 * k:128 * k + 128], x[:, t, f * 128:f * 128 + 128], toks[t], b.rel, inc=(k == 3))
                w = b.ap.rearrange("p (k n) -> p k n", k=4)
                dst = xT[:, 4 * kp:4 * kp + 4, t * 128:t * 128 + 128]
                if cols is None:
                    e = [cpy(A if kp % 2 else V, dst, w, r)]
                else:
                    g, b2 = cols
                    e = []
                    onv = t == 1 and kp == 0
                    for k in range(4):
                        f = 4 * kp + k
                        if onv:
                            q = ts(V, dst[:, k, :], w[:, k, :], g[:, f:f + 1], b2[:, f:f + 1], ALU.mult, ALU.add, r)
                        else:
                            q = act(dst[:, k, :], w[:, k, :], ACT.Identity, r, scale=g[:, f:f + 1], bias=b2[:, f:f + 1])
                    e = [q]
                PS.put(b, *e)
                if split is not None:
                    hi = split[:, 0, 4 * kp:4 * kp + 4, t * 128:t * 128 + 128]
                    lo = split[:, 1, 4 * kp:4 * kp + 4, t * 128:t * 128 + 128]
                    q = cpy(A, hi, dst, e)
                    e = [tt(V, lo, dst, hi.bitcast(F32), ALU.subtract, q, e)]
                last += e
            if rows is not None:
                tt(G, x[:, t, :], x[:, t, :], lnp[:, 0:1024], ALU.mult, rows, r)
                gxt[0] = tt(G, x[:, t, :], x[:, t, :], lnp[:, 1024:2048], ALU.add)
        return last

    def proj_T(src, ntile, tok, evac, kt=8, act_in=None):
        a = xT if act_in is None else act_in
        view, arrived, slot = load(src, kt)
        for c in range(ntile):
            b = PS.get()
            for k in range(kt):
                r = mm(b.ap[:, 0:256], view[:, k, c * 128:c * 128 + 128], a[:, k, :], k == 0, k == kt - 1,
                       arrived, tok, b.rel, inc=(k == kt - 1))
            if c == ntile - 1:
                done(slot, r)
            PS.put(b, evac(c, b.ap[:, 0:256], r))
            yield 1

    def tiles_of(src, n):
        return [(src, 8, "cols", c, c == n - 1) for c in range(n)]

    def rows_of_piece(src):
        k = 4 if callable(src) else src.shape[1] // 1024
        return [(src, k, "row", c, c == k - 1) for c in range(k)]

    def stream(chunks):
        it, ready, view = iter(chunks), [], [None]

        def get():
            while len(ready) < 4 and (stage[3].free or not ready):
                c = next(it, None)
                if c is None:
                    break
                src, kt, how, i, last = c
                if i == 0:
                    view[0] = load(src, kt)
                v, arrived, slot = view[0]
                buf = stage[3].get()
                if how == "pair":
                    part = v[:, 2 * i:2 * i + 2, :]
                    hi, lo = (buf.ap[:, j, :].rearrange("p (k n) -> p k n", k=2) for j in range(2))
                elif how == "cols":
                    part = v[:, :, i * 128:i * 128 + 128]
                    hi, lo = (buf.ap[:, j, :].rearrange("p (k n) -> p k n", k=8) for j in range(2))
                else:
                    part = v[:, i, :]
                    hi, lo = buf.ap[:, 0, :], buf.ap[:, 1, :]
                was, V.loose, A.loose = (V.loose, A.loose), True, True
                r = cpy(A, hi, part, arrived, buf.rel)
                r = tt(V, lo, part, hi.bitcast(F32), ALU.subtract, r, arrived)
                V.loose, A.loose = was
                if last:
                    done(slot, r)
                ready.append((buf, hi, lo, r))
            return ready.pop(0)

        return get

    def tile3(o, get, xsp, start, tok, rel):
        buf, hi, lo, r = get()
        for k in range(8):
            for n, (w, j) in enumerate(((hi, 0), (hi, 1), (lo, 0))):
                m = mm(o, w[:, k, :], xsp[:, j, k, :], k == 0 and n == 0, k == 7 and n == 2, r, tok, rel,
                       inc=(k == 7 and n == 2))
        stage[3].put(buf, m)
        return m

    def proj_S(get, ntile, xsp, tok, evac):
        for c in range(ntile):
            b = PS.get()
            m = tile3(b.ap[:, 0:256], get, xsp, True, tok, b.rel)
            PS.put(b, evac(c, b.ap[:, 0:256], m))
            yield 1

    def down3(get, total, lhs, tok):
        banks = [PS.get() for _ in range(4)]
        tail = []
        for f in range(total):
            c4 = get()
            if f < total - 2:
                tail.append([(f, c4, t) for t in range(2)])
            elif f == total - 2:
                last = c4
            else:
                tail.append([(f - 1, last, 0), (f, c4, 0), (f - 1, last, 1), (f, c4, 1)])
            if f == total - 2:
                continue
            for f1, (buf, hi, lo, r), t in tail.pop():
                tk = slice(t * 128, t * 128 + 128)
                for c in range(2):
                    b = banks[2 * t + c]
                    cc = slice(c * 512, c * 512 + 512)
                    for n, (a, w) in enumerate(((0, hi), (0, lo), (1, hi))):
                        m = mm(b.ap, lhs[a][:, f1, tk], w[:, cc], f1 == 0 and n == 0, f1 == total - 1 and n == 2, r, tok,
                               b.rel, inc=(n == 2 and c == 1))
                if t == 0:
                    m0 = m
                if t == 1:
                    stage[3].put(buf, m)
        return banks, [m0, m]

    def proj_rows(src, cols, tok, evac):
        view, arrived, slot = load(src, 8)
        for t in range(2):
            b = PS.get()
            for k in range(8):
                r = mm(b.ap[:, 0:cols], xT[:, k, t * 128:t * 128 + 128], view[:, k, :], k == 0, k == 7,
                       arrived, tok, b.rel, inc=(k == 7))
            if t == 1:
                done(slot, r)
            PS.put(b, evac(t, b.ap[:, 0:cols], r))
            yield 1

    def down(srcs, lhs, tok):
        banks = [PS.get() for _ in range(4)]
        total = sum(s.shape[1] // 1024 for s in srcs)
        k0 = 0
        fin = [None, None]
        for src in srcs:
            kt = src.shape[1] // 1024
            view, arrived, slot = load(src, kt)
            end = k0 + kt == total
            order = [(k, t) for t in range(2) for k in range(kt)] if end else [(k, t) for k in range(kt) for t in range(2)]
            for k, t in order:
                f = k0 + k
                for c in range(2):
                    r = mm(banks[2 * t + c].ap, lhs[:, f, t * 128:t * 128 + 128], view[:, k, c * 512:c * 512 + 512],
                           f == 0, f == total - 1, arrived, tok, banks[2 * t + c].rel,
                           inc=(k == kt - 1 and c == 1))
                if end and k == kt - 1:
                    fin[t] = r
            done(slot, r)
            k0 += kt
        return banks, fin

    mark = [None]

    def norm(src, stok, gated, last=None):
        toks = []
        st = small[:, 600:624]
        mark[0] = snap()
        for t in range(2):
            for c in range(2):
                xx = x[:, t, c * 512:c * 512 + 512]
                bank = isinstance(src, list)
                s = src[2 * t + c].ap if bank else src[:, t, c * 512:c * 512 + 512]
                if gated:
                    d = tmpn[:, c * 512:c * 512 + 512]
                    r = tt(V, d, s, gate[:, c * 512:c * 512 + 512], ALU.mult, stok[t])
                    if bank:
                        PS.put(src[2 * t + c], r)
                    s = d
                r = stt(xx, xx, ALPHA, s, ALU.mult, ALU.add, stok[t], gxt[0])
                if bank and not gated:
                    PS.put(src[2 * t + c], r)
                V(lambda e, c=c, xx=xx, t=t: e.bn_stats(small[:, 560 + 12 * t + 6 * c:566 + 12 * t + 6 * c], xx))
            mv = st[:, 4 * t:4 * t + 2]
            V(lambda e, mv=mv, t=t: e.bn_aggr(mv, small[:, 560 + 12 * t:572 + 12 * t]))
            r = ts(V, st[:, 4 * t + 2:4 * t + 3], mv[:, 1:2], 1e-5, None, ALU.add, None)
            r = tt(G, st[:, 4 * t + 3:4 * t + 4], st[:, 4 * t + 2:4 * t + 3], half[:, 0:1], ALU.pow, r)
            r = ts(V, x[:, t, :], x[:, t, :], mv[:, 0:1], st[:, 4 * t + 3:4 * t + 4], ALU.subtract, ALU.mult, r)
            if last is not None:
                tt(V, x[:, t, :], x[:, t, :], lnp[:, 0:1024], ALU.mult, last)
                r = tt(V, x[:, t, :], x[:, t, :], lnp[:, 1024:2048], ALU.add)
                A.wait(r)
                A.raw(lambda e, t=t: e.dma_start(out[t * 128:t * 128 + 128, :], x[:, t, :]).then_inc(s_out, 16))
            toks.append(r)
        return toks

    def inv_sqrt(dst, sums, scale, eps, add, tok):
        epsc[eps]
        r = act(dst, sums, ACT.Ln, tok, scale=scale, bias=epsc[eps])
        if add:
            return r, act(dst, dst, ACT.Exp, scale=-0.5, bias=epsc[add])
        return r, act(dst, dst, ACT.Exp, scale=-0.5)

    epsc = {}
    for n, v in enumerate((1e-6, 1e-5, math.log(128 ** -0.5), math.pi / 2)):
        epsc[v] = small[:, 624 + n:625 + n]
        r = V(lambda e, n=n, v=v: e.memset(small[:, 624 + n:625 + n], v))
    A.wait(r)
    LQ = math.log(128 ** -0.5)

    scc = small[:, 210:218]
    tables("silu_and_others")
    sc_tok = act(scc, C("c"), ACT.Silu)
    ada_buf = Pool([adacc[:, 0:512], adacc[:, 512:1024]])

    def adaln(i):
        for j in range(6):
            view, arrived, slot = load(ins["ada"][6 * i + j], 8)
            a = ada_buf.get()
            for k in range(8):
                if k == 0:
                    r = ts(V, a.ap, view[:, k, :], scc[:, k:k + 1], None, ALU.mult, None, arrived, sc_tok, a.rel)
                else:
                    r = stt(a.ap, view[:, k, :], scc[:, k:k + 1], a.ap, ALU.mult, ALU.add)
                if k % 4 == 3:
                    if k == 7:
                        done(slot, r)
                    yield 1
            b = PS.get()
            for c in range(4):
                m = mm(b.ap[:, c:c + 1], a.ap[:, 128 * c:128 * c + 128], ones[:, 0:1], True, True, r, b.rel, inc=(c == 3))
            ada_buf.put(a, m)
            o = 24 * i + 4 * j
            m = stt(mods[:, o:o + 4], b.ap[:, 0:4], 0.0 if j < 2 else 1.0, C("adab", o, o + 4), ALU.add, ALU.add, m)
            PS.put(b, m)
        sh, sc = mods[:, 24 * i:24 * i + 8], mods[:, 24 * i + 8:24 * i + 16]
        o = 8 * (3 + i)
        tt(V, lnc[:, o:o + 8], C("lng", o, o + 8), sc, ALU.mult)
        tt(V, lnc[:, 64 + o:72 + o], C("lnb", o, o + 8), sc, ALU.mult)
        tt(V, lnc[:, 64 + o:72 + o], lnc[:, 64 + o:72 + o], sh, ALU.add)

    def chained(*gens):
        for g in gens:
            yield from g

    def after(i):
        if i < 3:
            return C("lng", 8 * i, 8 * i + 8), C("lnb", 8 * i, 8 * i + 8)
        return lnc[:, 8 * i:8 * i + 8], lnc[:, 64 + 8 * i:72 + 8 * i]

    rows = load_rows(0)
    xt = transposed([None, None])
    top[0] = 0
    qkvz = take(24 * 256)
    QT = qkvz.rearrange("p (n m) -> p n m", n=24)
    oTf = take(2048)
    oT = oTf.rearrange("p (n m) -> p n m", n=8)
    top_gdn = top[0]
    qbk = take(12 * 256).rearrange("p (n m) -> p n m", n=12)
    vbt = take(1536).rearrange("p (t n) -> p t n", t=2)
    temp0 = top[0]

    conv_tok = {}

    def evac_even(c0):
        def f(c, ps, r):
            n = c0 + c
            y = QT[:, n, :]
            if n < 18:
                w = C("gconv")
                r1 = act(y, ps, ACT.Copy, r, scale=w[:, 4 * n + 3:4 * n + 4])
                for s in (1, 2, 3):
                    r1 = stt(y[:, s:256], ps[:, 0:256 - s], w[:, 4 * n + 3 - s:4 * n + 4 - s], y[:, s:256],
                             ALU.mult, ALU.add, r1)
            else:
                r1 = cpy(A, y, ps, r)
            conv_tok[n] = r1
            return r1
        return f

    def evac_b(c0):
        def f(c, ps, r):
            n = c0 + c
            if n < 6:
                r = ts(V, qbk[:, n, :], ps, 0.125, None, ALU.mult, None, r)
            else:
                r = cpy(V if n % 2 else A, qbk[:, n, :], ps, r)
            b_tok[n] = r
            return r
        return f

    b_tok = {}
    tables("natural_log_exp_and_others")

    def evac_rows(dst, c0, q):
        def f(t, ps, r):
            r = cpy(q, dst[:, t, c0:c0 + ps.shape[1]], ps, r)
            row_tok.append(r)
            return r
        return f

    row_tok = []
    run([proj_T(ins["we"][6 + j], 4, xt, evac_b(4 * j)) for j in range(3)]
        + [proj_rows(ins["wev"][0], 512, xt, evac_rows(vbt, 0, V)),
           proj_rows(ins["wev2"][0], 256, xt, evac_rows(vbt, 512, A))], 1)
    b = PS.get()
    wba = C("wba").rearrange("p (k n) -> p k n", k=8)
    for t in range(2):
        for k in range(8):
            r = mm(b.ap[:, 12 * t:12 * t + 12], xT[:, k, t * 128:t * 128 + 128], wba[:, k, :], k == 0, k == 7,
                   b.rel, inc=(k == 7))
    ba = small[:, 0:24].rearrange("p (t n) -> p t n", t=2)
    r = cpy(V, small[:, 0:24], b.ap[:, 0:24], r)
    PS.put(b, r)

    def softplus(dst, src, tmp, tok):
        act(tmp, src, ACT.Abs, tok)
        act(tmp, tmp, ACT.Exp, scale=-1.0)
        r = act(tmp, tmp, ACT.Ln, bias=1.0)
        return stt(dst, src, 0.0, tmp, ALU.max, ALU.add, r)

    def cols(a):
        return small[:, a:a + 12]

    def two(ap):
        return ap.rearrange("p (t n) -> p t n", t=2)

    r = act(two(cols(24)), ba[:, :, 0:6], ACT.Exp, r, scale=-1.0)
    r = ts(V, cols(24), cols(24), 1.0, None, ALU.add, None, r)
    r = V(lambda e: e.reciprocal(cols(24), cols(24)))
    r = tt(V, two(cols(96)), ba[:, :, 6:12], bc(R("dtb").rearrange("p (a n) -> p a n", a=1), [128, 2, 6]), ALU.add)
    r = softplus(cols(96), cols(96), cols(108), r)
    e1 = act(small[:, 120:126], R("alog"), ACT.Exp)
    r = stt(two(cols(36)), two(cols(96)), -1.0,
            bc(small[:, 120:126].rearrange("p (a n) -> p a n", a=1), [128, 2, 6]), ALU.mult, ALU.mult, e1)
    b = PS.get()
    mm(b.ap[:, 0:12], K("tri"), cols(36), True, True, r, b.rel)
    rg = mm(b.ap[:, 12:24], ones[:, :], cols(36), True, True, inc=True)
    cpy(V, small[:, 130:154], b.ap[:, 0:24], rg)
    r = cpy(V, cols(48), b.ap[:, 0:12])
    PS.put(b, r)
    ts(V, cols(84), cols(48), -1.0, None, ALU.mult, None)
    r = tt(V, cols(72), small[:, 142:154], cols(48), ALU.subtract)
    act(cols(72), cols(72), ACT.Exp, r)
    r = act(cols(60), cols(48), ACT.Exp)
    gates = tt(V, cols(60), cols(60), cols(24), ALU.mult, r)

    TP = TPs[:, :].rearrange("p (h n) -> p h n", h=4)
    for c in range(2):
        b = PS.get()
        t = mm(b.ap, K("exch"), hank[:, 512 * c:512 * c + 512], True, True, (s_hank, 16), b.rel, inc=True)
        t = cpy(V, TPs[:, 512 * c:512 * c + 512], b.ap, t)
        PS.put(b, t)
    TPt = t

    top[0] = temp0
    sS = Pool([take(768) for _ in range(4)])
    sP = Pool([take(768) for _ in range(4)])
    stat = Pool([small[:, 160 + 4 * i:164 + 4 * i] for i in range(6)])
    DM = kc[:, kat["dm0"][0]:kat["dm0"][0] + 768].rearrange("p (g n) -> p g n", g=3)
    o_tok = []

    def swa_unit(h, t):
        base = (h % 2) * 64
        nk = 128 * (t + 1)
        off = 256 - nk
        s = sS.get()
        sv = s.ap[:, 0:3 * nk].rearrange("p (g n) -> p g n", g=3)
        for g0, g1 in ([(0, 3)] if t == 0 else [(0, 2), (2, 3)]):
            b = PS.get()
            for g in range(g0, g1):
                n = g * 2 + h // 2
                r = mm(b.ap[:, (g - g0) * nk:(g - g0) * nk + nk], qbk[base:base + 64, n, t * 128:t * 128 + 128],
                       qbk[base:base + 64, 6 + n, 0:nk], True, True, b.rel, b_tok[n], b_tok[6 + n], inc=(g == g1 - 1))
            r = tt(V, sv[:, g0:g1, :], b.ap[:, 0:(g1 - g0) * nk].rearrange("p (g n) -> p g n", g=g1 - g0),
                   bc(TP[:, h:h + 1, off:256], [128, g1 - g0, nk]), ALU.add, r, s.rel, TPt)
            PS.put(b, r)
        r = tt(V, sv, sv, DM[:, :, off:256], ALU.add)
        sm = stat.get()
        r = V(lambda e: e.tensor_reduce(sm.ap[:, 0:1], s.ap[:, 0:3 * nk], X, ALU.max, negate=True), sm.rel)
        r = act(s.ap[:, 0:3 * nk], s.ap[:, 0:3 * nk], ACT.Exp, r, bias=sm.ap[:, 0:1], accum_out=sm.ap[:, 1:2])
        yield 1
        V(lambda e: e.reciprocal(sm.ap[:, 2:3], sm.ap[:, 1:2]), r)
        r = ts(V, s.ap[:, 0:3 * nk], s.ap[:, 0:3 * nk], sm.ap[:, 2:3], None, ALU.mult, None)
        stat.put(sm, r)
        yield 1
        p = sP.get()
        nt = 3 * (t + 1)
        pt = []
        for c0 in range(0, nt, 4):
            c1 = min(c0 + 4, nt)
            b = PS.get()
            for c in range(c0, c1):
                r2 = tp(b.ap[:, (c - c0) * 128:(c - c0) * 128 + 128], s.ap[:, c * 128:c * 128 + 128], r, b.rel,
                        inc=(c == c1 - 1))
            r3 = cpy(A if c0 else V, p.ap[:, c0 * 128:c1 * 128], b.ap[:, 0:(c1 - c0) * 128], r2, p.rel)
            pt.append(r3)
            PS.put(b, r3)
        sS.put(s, r2)
        yield 1
        ob = PS.get()
        for c in range(nt):
            g, jt = c // (t + 1), c % (t + 1)
            r = mm(ob.ap[base:base + 64, 0:128], vbt[:, jt, g * 256 + h * 64:g * 256 + h * 64 + 64],
                   p.ap[:, c * 128:c * 128 + 128], c == 0, c == nt - 1, pt, ob.rel, row_tok, inc=(c == nt - 1))
        sP.put(p, r)
        r = cpy(A, oT[base:base + 64, 6 + h // 2, t * 128:t * 128 + 128], ob.ap[base:base + 64, 0:128], r)
        o_tok.append(r)
        PS.put(ob, r)
        yield 1

    def projections():
        for j in range(6):
            yield from proj_T(ins["we"][j], 4, xt, evac_even(4 * j))

    run([swa_unit(h, t) for h in range(4) for t in range(2)], 3, projections())
    tables("silu_and_others")
    for n in range(6):
        silu_tok = act(qkvz[:, 1024 * n:1024 * n + 1024], qkvz[:, 1024 * n:1024 * n + 1024], ACT.Silu,
                       [conv_tok[4 * n + i] for i in range(4)])
    tables("natural_log_exp_and_others")

    for q in (V, A, G):
        q.wait(*snap())
    top[0] = top_gdn
    take(768)
    sq = Pool([take(512) for _ in range(3)])
    l2 = {}

    def l2_unit(n):
        pair = qkvz[:, n * 256:n * 256 + 512]
        s = sq.get()
        r = act(s.ap, pair, ACT.Square, s.rel, silu_tok)
        yield 1
        b = PS.get()
        r = mm(b.ap, ones[:, :], s.ap, True, True, r, b.rel, inc=True)
        r1, r2 = inv_sqrt(s.ap, b.ap, 1.0, 1e-6, LQ if n < 6 else None, r)
        PS.put(b, r1)
        r = tt(V, pair, pair, s.ap, ALU.mult, r2)
        l2[n] = l2[n + 1] = r
        sq.put(s, r)
        yield 1

    run([l2_unit(n) for n in range(0, 12, 2)], 3)
    top[0] = top_gdn
    Sst = take(768)
    for q in (V, A, G):
        q.wait(*snap())
    NAMES = ("a", "b", "DT", "EG", "LT", "QK", "E", "D", "kbe", "vb")
    sets = Pool([{k: take(384) for k in NAMES} for _ in range(4)])
    M3 = [128, 3, 128]

    def v3(ap):
        return ap.rearrange("p (h n) -> p h n", h=3)

    def k3(name):
        return bc(K(name).rearrange("p (a n) -> p a n", a=1), M3)

    def col3(a, n):
        return bc(small[:, a + n:a + n + 3].rearrange("p (n a) -> p n a", a=1), M3)

    def cs(ap):
        return lambda i: ap[:, i * 128:i * 128 + 128]

    def three(l, r, toks, acc=None):
        b = PS.get()
        for i in range(3):
            k = mm(b.ap[:, i * 128:i * 128 + 128], l(i), r(i), True, acc is None, toks, b.rel,
                   inc=(i == 2 and acc is None))
            if acc is not None:
                k = mm(b.ap[:, i * 128:i * 128 + 128], acc[0](i), acc[1](i), False, True, toks, inc=(i == 2))
        return b, k

    def flip(src, toks):
        b = PS.get()
        for i in range(3):
            k = tp(b.ap[:, i * 128:i * 128 + 128], src(i), toks, b.rel, inc=(i == 2))
        return b, k

    S_tok, gdn_tok = {}, []
    T.wait(silu_tok, l2[11])

    def gdn_unit(t, hg):
        ub = sets.get()
        u = ub.ap
        n0 = 6 * t + 3 * hg
        tk = slice(t * 128, t * 128 + 128)

        def head(j):
            return lambda i: QT[:, j + 3 * hg + i, tk]

        cpy(V, v3(u["a"]), col3(36, n0), ub.rel)
        r = cpy(V, v3(u["b"]), col3(24, n0))
        b, k = three(cs(u["a"]), lambda i: K("tri"), r)
        b2, k2 = three(cs(u["b"]), lambda i: ident, r)
        B = b.ap[:, 0:384]
        r = tt(V, v3(u["DT"]), v3(B), k3("cmt"), ALU.add, k)
        re = act(u["EG"], B, ACT.Exp, r)
        PS.put(b, re)
        for i in range(3):
            r = act(u["DT"][:, i * 128:i * 128 + 128], u["DT"][:, i * 128:i * 128 + 128], ACT.Exp,
                    bias=small[:, 84 + n0 + i:85 + n0 + i])
        r2 = tt(V, u["LT"], u["DT"], b2.ap[:, 0:384], ALU.mult, r, k2)
        PS.put(b2, r2)
        yield 1
        b, k = three(head(6), head(6), None)
        b2, k2 = three(head(6), head(0), None)
        r = tt(V, u["LT"], u["LT"], b.ap[:, 0:384], ALU.mult, k)
        PS.put(b, r)
        r = tt(V, u["QK"], u["DT"], b2.ap[:, 0:384], ALU.mult, k2)
        PS.put(b2, r)
        tt(V, v3(u["E"]), v3(u["LT"]), k3("m1"), ALU.mult)
        r = tt(V, v3(u["E"]), k3("ident"), v3(u["E"]), ALU.subtract)
        rL = tt(V, v3(u["DT"]), v3(u["LT"]), k3("m2"), ALU.mult)
        yield 1
        b, k = flip(cs(u["E"]), r)
        rD = cpy(A, u["D"], b.ap[:, 0:384], k)
        PS.put(b, rD)
        b, k = flip(head(6), None)
        if t == 0:
            r1 = tt(V, v3(u["EG"]), v3(b.ap[:, 0:384]), col3(72, n0), ALU.mult, k, re)
        else:
            r1 = tt(V, v3(u["kbe"]), v3(b.ap[:, 0:384]), col3(60, n0), ALU.mult, k)
        PS.put(b, r1)
        if t == 1:
            tt(V, v3(u["EG"]), v3(u["EG"]), QT[:, 3 * hg:3 * hg + 3, tk], ALU.mult, re)
        b, k = flip(head(12), None)
        rv = tt(V, v3(u["vb"]), v3(b.ap[:, 0:384]), col3(24, n0), ALU.mult, k)
        PS.put(b, rv)
        L = u["DT"]
        rE = rv
        for s in (2, 4, 8, 16, 32, 64):
            b, k = three(cs(L), cs(u["D"]), [rL, rD])
            ra = cpy(A, u["a"], b.ap[:, 0:384], k)
            PS.put(b, ra)
            if s < 64:
                rL = tt(V, v3(L), v3(u["LT"]), k3(f"m{2 * s}"), ALU.mult, k)
            yield 1
            b2, k2 = three(cs(u["a"]), cs(u["E"]), [ra, rE])
            if s < 64:
                b, k = three(cs(u["E"]), cs(u["a"]), None)
            else:
                k = k2
            rE = tt(V, u["E"], u["E"], b2.ap[:, 0:384], ALU.subtract, k)
            PS.put(b2, rE)
            if s < 64:
                rD = tt(V, u["D"], u["D"], b.ap[:, 0:384], ALU.subtract, k)
                PS.put(b, rD)
            yield 1
        E = u["E"]
        Sg = Sst[:, hg * 384:hg * 384 + 384]
        if t == 0:
            b, k = three(cs(E), cs(u["vb"]), rE)
            r = cpy(V, u["a"], b.ap[:, 0:384], k)
            PS.put(b, r)
            yield 1
            b, k = three(cs(u["EG"]), cs(u["a"]), r)
            S_tok[hg] = cpy(A, Sg, b.ap[:, 0:384], k)
            PS.put(b, S_tok[hg])
            b, k = three(cs(u["a"]), cs(u["QK"]), r)
        else:
            b, k = three(cs(u["kbe"]), cs(E), rE)
            r = ts(V, u["b"], b.ap[:, 0:384], -1.0, None, ALU.mult, None, k)
            PS.put(b, r)
            yield 1
            b, k = three(cs(E), cs(u["vb"]), [r, S_tok[hg]], (cs(u["b"]), cs(Sg)))
            r = cpy(V, u["a"], b.ap[:, 0:384], k)
            PS.put(b, r)
            yield 1
            b, k = three(cs(u["a"]), cs(u["QK"]), r, (cs(Sg), cs(u["EG"])))
        r = cpy(V, oT[:, 3 * hg:3 * hg + 3, tk], v3(b.ap[:, 0:384]), k)
        PS.put(b, r)
        sets.put(ub, r, k)
        gdn_tok.append(r)
        yield 1

    run([gdn_unit(t, hg) for t in range(2) for hg in range(2)], 4, adaln(0))

    def rms_out(o, g, w, sz, tmp, tok):
        r = act(tmp[:, 0:sz], o, ACT.Square, tok)
        b = PS.get()
        r = mm(b.ap[:, 0:sz], ones[:, :], tmp[:, 0:sz], True, True, r, b.rel, inc=True)
        r1, r2 = inv_sqrt(tmp[:, 0:sz], b.ap[:, 0:sz], 1.0 / 128, 1e-6, None, r)
        PS.put(b, r1)
        tt(V, o, o, tmp[:, 0:sz], ALU.mult, r2)
        return stt(o, o, w, g, ALU.mult, ALU.mult)

    tmp3 = [sets.free[0].ap[k] for k in ("a", "DT", "LT")] + [sets.free[1].ap[k] for k in ("a", "DT", "LT")]
    for n in range(6):
        r = rms_out(oT[:, n, :], QT[:, 18 + n, :], C("gnw"), 256, tmp3[n][:, 0:256], gdn_tok + [T.now()])
    banks, k = down([ins["woe"][0], ins["woe"][1]], oT, [r] + o_tok)
    lt = norm(banks, k, False)

    def ffn(l, ln_i, tok):
        xsp = open_stage(2048, mark[0])
        gsp = stage[0].enter_context(nc.sbuf_tensor(f"gsplit{l}", [128, 2, 22, 256], F32R))
        xt = transposed(tok, after(ln_i - 1), rows_of[0], xsp)
        rows_of[0] = load_rows(ln_i)
        tables("silu_and_others")
        yg = Pool([take(512) for _ in range(4)])
        wv = C(f"fw{l}")
        bv = C(f"fb{l}")
        last, later, silu_of = [None], [], {}
        up = [c for j in range(11) for c in tiles_of(ins[f"wu{l}"][j], 4)]
        dn = [c for i in range(5) for c in rows_of_piece(ins[f"wd{l}"][i])] + rows_of_piece(ins[f"wdl{l}"][0])
        get = stream(up + dn)
        for j in range(11):
            ys = []

            def f(c, ps, r, j=j, ys=ys):
                n = 2 * j + c if c < 2 else 22 + 2 * j + c - 2
                if c < 2:
                    buf = yg.get()
                    ys.append(buf)
                    y = buf.ap[:, 0:256]
                else:
                    buf = ys[c - 2]
                    y = buf.ap[:, 256:512]
                for g in later:
                    g()
                later.clear()
                r = act(y, ps, ACT.Identity, r, buf.rel, scale=wv[:, 3 * n + 2:3 * n + 3], bias=bv[:, n:n + 1])
                for s in (1, 2):
                    r = stt(y[:, s:256], ps[:, 0:256 - s], wv[:, 3 * n + 2 - s:3 * n + 3 - s], y[:, s:256],
                            ALU.mult, ALU.add, r)
                if c < 2:
                    def silu():
                        silu_of[n] = act(y, y, ACT.Silu, r)
                    later.append(silu)
                else:
                    g = 2 * j + c - 2
                    q = tt(G, y, buf.ap[:, 0:256], y, ALU.mult, r, silu_of.get(g) or r)

                    def split():
                        k = cpy(A, gsp[:, 0, g, :], y, q)
                        last[0] = tt(G, gsp[:, 1, g, :], y, gsp[:, 0, g, :].bitcast(F32), ALU.subtract, k)
                        yg.put(buf, last[0])
                    later.append(split)
                return r

            run([proj_S(get, 4, xsp, xt, f)], 1)
        for g in later:
            g()
        banks, k = down3(get, 22, (gsp[:, 0], gsp[:, 1]), last[0])
        return norm(banks, k, False)

    rows_of = [rows]
    lt = ffn(0, 1, lt)

    open_stage(21000, mark[0], False)
    xt = transposed(lt, after(1), rows_of[0])
    rows_of[0] = load_rows(2)
    tables("silu_and_others")
    qc = take(2048).rearrange("p (n m) -> p n m", n=8)
    gl = take(1024)
    glv = gl.rearrange("p (n m) -> p n m", n=4)
    rT = take(1024).rearrange("p (n m) -> p n m", n=4)
    vc = take(1024).rearrange("p (t n) -> p t n", t=2)
    vd = take(1024).rearrange("p (t n) -> p t n", t=2)
    oTf = take(2048)
    oT = oTf.rearrange("p (n m) -> p n m", n=8)
    TC = take(1024).rearrange("p (h n) -> p h n", h=4)
    gdT = take(256)
    la = take(512)
    Bc = take(512)
    pT = {}

    def evac_odd(c0):
        def f(c, ps, r):
            n = c0 + c
            if n < 8:
                r = ts(V, qc[:, n, :], ps, 0.125, None, ALU.mult, None, r) if n < 4 else cpy(A, qc[:, n, :], ps, r)
            elif n < 12:
                m = n - 8
                r = ts(V, glv[:, m, :], ps, 0.125, None, ALU.mult, None, r) if m < 2 else cpy(A, glv[:, m, :], ps, r)
            else:
                r = act(rT[:, n - 12, :], ps, ACT.Silu, r)
            pT[n] = r
            return r
        return f

    run([proj_T(ins["wo"][j], 4, xt, evac_odd(4 * j)) for j in range(4)], 1, adaln(1))
    tables("natural_log_exp_and_others")
    row_tok = []
    run([proj_rows(ins["wov"][0], 512, xt, evac_rows(vc, 0, V)),
         proj_rows(ins["wov"][1], 512, xt, evac_rows(vd, 0, A))], 1)
    wgd = C("wgd").rearrange("p (k n) -> p k n", k=8)
    b = PS.get()
    for k in range(8):
        r = mm(b.ap[0:16, 0:256], wgd[:, k, :], xT[:, k, :], k == 0, k == 7, b.rel, xt, inc=(k == 7))
    r = cpy(V, gdT[0:16, :], b.ap[0:16, 0:256], r)
    PS.put(b, r)
    lwg = C("lwg")
    b = PS.get()
    for m in range(2):
        k = mm(b.ap[:, m * 256:m * 256 + 256], lwg[0:16, m * 128:m * 128 + 128], gdT[0:16, :], True, True, r, b.rel,
               inc=(m == 1))
    for m in range(2):
        r = ts(V, la[:, m * 256:m * 256 + 256], b.ap[:, m * 256:m * 256 + 256], C("lbg", m, m + 1), -1.0,
               ALU.add, ALU.mult, k)
    PS.put(b, r)
    r = softplus(la, la, Bc, r)
    r = ts(V, la, la, -1.0 / 16, None, ALU.mult, None)
    for i in range(4):
        s = slice(i * 128, i * 128 + 128)
        V(lambda e, s=s: e.tensor_tensor_scan(Bc[:, s], ones[:, :], la[:, s], 0.0, ALU.mult, ALU.add))
    tt(V, small[0:64, 200:202], C("dl")[0:64, 0:4:2], C("dl")[0:64, 1:4:2], ALU.mult)
    b = PS.get()
    r = mm(b.ap[:, 0:2], ones[0:64, :], small[0:64, 200:202], True, True, V.now(), b.rel, inc=True)
    r = act(small[:, 202:204], b.ap[:, 0:2], ACT.Exp, r)
    PS.put(b, r)
    tt(V, small[:, 204:205], small[:, 203:204], small[:, 202:203], ALU.subtract, r)
    ts(V, small[:, 205:206], small[:, 204:205], -LAM0, None, ALU.add, None)
    ts(V, small[:, 206:207], C("dnw"), 1.0 - LAM0, None, ALU.mult, None)
    r = tt(V, TC, TP, bc(K("cm").rearrange("p (a n) -> p a n", a=1), [128, 4, 256]), ALU.add)
    temp1 = top[0]
    sS = Pool([take(512) for _ in range(4)])
    sP = Pool([take(256) for _ in range(4)])
    stat = Pool([small[:, 160 + 6 * i:166 + 6 * i] for i in range(5)])

    def diff_unit(h, t):
        nk = 128 * (t + 1)
        off = 256 - nk
        s = sS.get()
        sv = s.ap[:, 0:2 * nk].rearrange("p (c n) -> p c n", c=2)
        pair = [PS.get(), PS.get()]
        for c in range(2):
            b = pair[c]
            r = mm(b.ap[:, 0:nk], qc[c * 64:c * 64 + 64, h, t * 128:t * 128 + 128],
                   qc[c * 64:c * 64 + 64, 4 + h, 0:nk], True, True, b.rel, pT[h], pT[4 + h], inc=True)
            r = tt(V, sv[:, c, :], b.ap[:, 0:nk], TC[:, h, off:256], ALU.add, r, s.rel)
            PS.put(b, r)
        sm = stat.get()
        r = V(lambda e: e.tensor_reduce(sm.ap[:, 0:2], sv, X, ALU.max, negate=True), sm.rel)
        for c in range(2):
            r = act(s.ap[:, c * nk:c * nk + nk], s.ap[:, c * nk:c * nk + nk], ACT.Exp, r,
                    bias=sm.ap[:, c:c + 1], accum_out=sm.ap[:, 2 + c:3 + c])
        yield 1
        V(lambda e: e.reciprocal(sm.ap[:, 4:6], sm.ap[:, 2:4]), r)
        ts(V, sm.ap[:, 5:6], sm.ap[:, 5:6], small[:, 205:206], None, ALU.mult, None)
        ts(V, s.ap[:, 0:nk], s.ap[:, 0:nk], sm.ap[:, 4:5], None, ALU.mult, None)
        r = stt(s.ap[:, 0:nk], s.ap[:, nk:2 * nk], sm.ap[:, 5:6], s.ap[:, 0:nk], ALU.mult, ALU.add)
        stat.put(sm, r)
        yield 1
        b = PS.get()
        for j in range(t + 1):
            r2 = tp(b.ap[:, j * 128:j * 128 + 128], s.ap[:, j * 128:j * 128 + 128], r, b.rel, inc=(j == t))
        sS.put(s, r2)
        p = sP.get()
        r3 = cpy(A, p.ap[:, 0:nk], b.ap[:, 0:nk], r2, p.rel)
        PS.put(b, r3)
        yield 1
        ob = PS.get()
        for j in range(t + 1):
            r = mm(ob.ap[:, 0:128], vc[:, j, h * 128:h * 128 + 128], p.ap[:, j * 128:j * 128 + 128],
                   j == 0, j == t, r3, ob.rel, row_tok, inc=(j == t))
        sP.put(p, r)
        r = cpy(A, oT[:, h, t * 128:t * 128 + 128], ob.ap[:, 0:128], r)
        PS.put(ob, r)
        dtok.append(r)
        yield 1

    dtok = []
    tmp = take(512)

    def diff_norm(n):
        o = oTf[:, n * 512:n * 512 + 512]
        r = act(tmp, o, ACT.Square)
        b = PS.get()
        r = mm(b.ap, ones[:, :], tmp, True, True, r, b.rel, inc=True)
        r1, r2 = inv_sqrt(tmp, b.ap, 1.0 / 128, 1e-6, None, r)
        PS.put(b, r1)
        stt(o, o, small[:, 206:207], tmp, ALU.mult, ALU.mult, r2)

    qs = Pool([take(512) for _ in range(2)])
    ks = Pool([take(512) for _ in range(2)])
    ee = Pool([take(512) for _ in range(2)])
    acc = [take(512) for _ in range(2)]
    mt = [take(512) for _ in range(2)]
    qd = take(256).rearrange("p (n m) -> p n m", n=2)
    kdT = take(256).rearrange("p (n m) -> p n m", n=2)
    kdt = take(256).rearrange("p (n m) -> p n m", n=2)
    Sg = take(256).rearrange("p (n m) -> p n m", n=2)
    q4 = gl[:, 0:512]
    k4 = gl[:, 512:1024]
    B4 = Bc.rearrange("p (n m) -> p n m", n=4)
    Btok = V.now()
    A.wait(Btok)
    acc_tok = [None, None]
    def gla_level(s):
        if s == 0:
            qv, kv, rr = q4, k4, [pT[8], pT[9], pT[10], pT[11]]
        else:
            qb, kb, eb = qs.get(), ks.get(), ee.get()
            z1 = G(lambda e, qb=qb: e.memset(qb.ap, 0.0), qb.rel)
            z2 = G(lambda e, kb=kb: e.memset(kb.ap, 0.0), kb.rel)
            nb = 256 // s

            def blocks(ap):
                return ap.rearrange("p (b n) -> p b n", n=2 * s)

            ref = blocks(Bc)[:, :, s - 1:s]
            ev = eb.ap.rearrange("p (w b n) -> p w b n", w=2, n=s)
            tt(V, ev[:, 0], blocks(Bc)[:, :, s:2 * s], bc(ref, [128, nb, s]), ALU.subtract, eb.rel)
            r = tt(V, ev[:, 1], bc(ref, [128, nb, s]), blocks(Bc)[:, :, 0:s], ALU.subtract)
            r = act(eb.ap, eb.ap, ACT.Exp, r)
            tt(V, blocks(qb.ap)[:, :, s:2 * s], blocks(q4)[:, :, s:2 * s], ev[:, 0], ALU.mult, r, z1, z2)
            rr = tt(V, blocks(kb.ap)[:, :, 0:s], blocks(k4)[:, :, 0:s], ev[:, 1], ALU.mult)
            ee.put(eb, rr)
            qv, kv = qb.ap, kb.ap
        mask = bc(K("ident" if s == 0 else f"m{s}").rearrange("p (a n) -> p a n", a=1), [128, 2, 128])
        yield 1
        for t in range(2):
            dst = (acc[t] if s == 0 else mt[t]).rearrange("p (m a n) -> p m a n", m=2, a=2)
            for a in range(2):
                b = PS.get()
                for m in range(2):
                    seg = 2 * m + t
                    k = mm(b.ap[:, m * 128:m * 128 + 128], kv[64 * a:64 * a + 64, seg * 128:seg * 128 + 128],
                           qv[64 * a:64 * a + 64, seg * 128:seg * 128 + 128], True, True, rr, b.rel, inc=(m == 1))
                r = tt(V, dst[:, :, a, :], b.ap[:, 0:256].rearrange("p (m n) -> p m n", m=2), mask, ALU.mult, k,
                       None if s == 0 else acc_tok[t])
                PS.put(b, r)
            acc_tok[t] = r if s == 0 else tt(G, acc[t], acc[t], mt[t], ALU.add, r)
        if s:
            qs.put(qb, k)
            ks.put(kb, k)
        yield 1

    run([diff_unit(h, t) for h in range(4) for t in range(2)], 3,
        chained(*[gla_level(s) for s in (0, 1, 2, 4, 8, 16, 32, 64)]))
    A.wait(V.now())
    diff_norm(0)
    A.wait(V.now())
    diff_norm(1)
    Bq = Bc.rearrange("p (n t m) -> p n t m", n=2, t=2)
    r = act(qd, Bq[:, :, 1, :], ACT.Exp)
    tt(V, qd, qd, gl[:, 0:512].rearrange("p (n t m) -> p n t m", n=2, t=2)[:, :, 1, :], ALU.mult, r)
    r = tt(V, kdT, bc(Bq[:, :, 0, 127:128], [128, 2, 128]), Bq[:, :, 0, :], ALU.subtract)
    r = act(kdT, kdT, ACT.Exp, r)
    r = tt(V, kdT, kdT, gl[:, 512:1024].rearrange("p (n t m) -> p n t m", n=2, t=2)[:, :, 0, :], ALU.mult, r)
    b = PS.get()
    for m in range(2):
        k = tp(b.ap[:, m * 128:m * 128 + 128], kdT[:, m, :], r, b.rel, inc=(m == 1))
    r = cpy(V, kdt, b.ap[:, 0:256].rearrange("p (n m) -> p n m", n=2), k)
    PS.put(b, r)
    b = PS.get()
    for h in range(4):
        base = (h % 2) * 64
        k = mm(b.ap[base:base + 64, (h // 2) * 128:(h // 2) * 128 + 128], kdt[:, h // 2, base:base + 64],
               vd[:, 0, h * 128:h * 128 + 128], True, True, r, b.rel, row_tok, inc=(h == 3))
    r = cpy(V, Sg, b.ap[:, 0:256].rearrange("p (n m) -> p n m", n=2), k)
    PS.put(b, r)
    for h in range(4):
        base = (h % 2) * 64
        b = PS.get()
        mm(b.ap[:, 0:128], vd[:, 0, h * 128:h * 128 + 128], acc[0][:, h * 128:h * 128 + 128], True, True,
           acc_tok[0], acc_tok[1], b.rel, r)
        mm(b.ap[:, 128:256], vd[:, 1, h * 128:h * 128 + 128], acc[1][:, h * 128:h * 128 + 128], True, False)
        k = mm(b.ap[:, 128:256], Sg[base:base + 64, h // 2, :], qd[base:base + 64, h // 2, :], False, True, inc=True)
        r2 = cpy(V, oT[:, 4 + h, :], b.ap[:, 0:256], k)
        PS.put(b, r2)
    for n in range(2):
        r = rms_out(oTf[:, 1024 + n * 512:1536 + n * 512], rT.rearrange("p n m -> p (n m)")[:, n * 512:n * 512 + 512],
                    C("lnw"), 512, tmp, [V.now()])
    banks, k = down([ins["woo"][0], ins["woo"][1]], oT, r)
    lt = norm(banks, k, False)
    lt = ffn(1, 3, lt)

    def gate_row(i):
        g = take(1024).rearrange("p (k n) -> p k n", k=8)
        r = cpy(V, g, bc(mods[:, 24 * i + 16:24 * i + 24].rearrange("p (k a) -> p k a", a=1), [128, 8, 128]))
        for c in range(2):
            b = PS.get()
            for k in range(4):
                m = mm(b.ap[:, 128 * k:128 * k + 128], g[:, 4 * c + k, :], ident, True, True, r, b.rel, inc=(k == 3))
            m = cpy(V, gate[:, 512 * c:512 * c + 512], b.ap, m)
            PS.put(b, m)

    open_stage(17000, mark[0], False)
    xt = transposed(lt, after(3), rows_of[0])
    rows_of[0] = load_rows(4)
    qk = take(16 * 256).rearrange("p (n m) -> p n m", n=16)
    vs = take(2048).rearrange("p (t n) -> p t n", t=2)
    oT = take(2048).rearrange("p (n m) -> p n m", n=8)
    tables("natural_log_exp_and_others")
    pT = {}

    def evac_sb(c0):
        def f(c, ps, r):
            n = c0 + c
            r = ts(V, qk[:, n, :], ps, 0.125, None, ALU.mult, None, r) if n < 8 else cpy(A, qk[:, n, :], ps, r)
            pT[n] = r
            return r
        return f

    run([proj_T(ins["ws"][j], 4, xt, evac_sb(4 * j)) for j in range(4)], 1)
    row_tok = []
    run([proj_rows(ins["ws"][4 + j], 512, xt, evac_rows(vs, 512 * j, A if j else V)) for j in range(2)], 1)
    gate_row(0)
    az = Pool([take(384) for _ in range(5)])
    sp = Pool([take(384) for _ in range(5)])

    def diag(ap):
        return ap.rearrange("p (n m) -> p n m", n=3)[:, 0:3:2, :]

    def keep(ap, tok):
        return G(lambda e: e.affine_select(out=diag(ap), in_=diag(ap), compare_op=ALU.is_gt, fill=0.0, base=0,
                                           pattern=[[0, 2], [1, 128]], channel_multiplier=-1), tok)

    sb_tok = []

    def sb_unit(h):
        base, n = (h % 2) * 64, h // 2
        zb = PS.get()
        kk, qq = qk[base:base + 64, 8 + n, :], qk[base:base + 64, n, :]
        mm(zb.ap[:, 0:256], kk[:, 0:128], qq, True, False, zb.rel, pT[n], pT[8 + n])
        r = mm(zb.ap[:, 256:384], kk[:, 128:256], qq[:, 128:256], False, False, inc=True)
        a, s = az.get(), sp.get()
        z = zb.ap[:, 0:384]
        act(a.ap, z, ACT.Abs, r, a.rel)
        act(a.ap, a.ap, ACT.Exp, scale=-1.0)
        r = act(a.ap, a.ap, ACT.Ln, bias=1.0)
        r = stt(s.ap, z, 0.0, a.ap, ALU.max, ALU.add, r, s.rel)
        r = keep(s.ap, r)
        yield 1
        mm(zb.ap[:, 0:256], K("ntri"), s.ap[:, 0:256], False, False, r)
        mm(zb.ap[:, 128:256], neg1[:, :], s.ap[:, 256:384], False, False)
        k = mm(zb.ap[:, 256:384], K("ntri"), s.ap[:, 256:384], False, True, inc=True)
        sp.put(s, k)
        r = act(a.ap, zb.ap[:, 0:384], ACT.Exp, k)
        PS.put(zb, r)
        r = keep(a.ap, r)
        yield 1
        b = PS.get()
        o = b.ap[base:base + 64, :]
        mm(o[:, 0:256], vs[:, 0, h * 64:h * 64 + 64], a.ap[:, 0:256], True, False, r, b.rel, row_tok)
        k = mm(o[:, 128:256], vs[:, 1, h * 64:h * 64 + 64], a.ap[:, 256:384], False, True, inc=True)
        az.put(a, k)
        r = cpy(V, oT[base:base + 64, n, :], o[:, 0:256], k)
        PS.put(b, r)
        sb_tok.append(r)
        yield 1

    run([sb_unit(h) for h in range(16)], 4, adaln(2))
    banks, k = down([ins["wso"][0], ins["wso"][1]], oT, sb_tok)
    lt = norm(banks, k, True)

    def moe(l, i, tok, last=False):
        xsp = open_stage(2328, mark[0])

        def fr(name, *dims):
            return stage[0].enter_context(nc.sbuf_tensor(f"{name}{l}", [128, *dims], F32R))

        eids = stage[0].enter_context(nc.sbuf_tensor(f"eids{l}", [128, 4], I32))
        hs, ysp = fr("hs", 2, 2, 1024), fr("ysp", 2, 1024)
        pm, pts, hts = fr("pm", 2, 256), fr("pt", 4, 256), fr("ht", 2, 2, 4, 128)
        xt = transposed(tok, after(3 + i), rows_of[0])
        rows_of[0] = load_rows(4 + i)
        rw = C("rw").rearrange("p (k n) -> p k n", k=8)
        b = PS.get()
        for t in range(2):
            for k in range(8):
                r = mm(b.ap[:, 16 * t:16 * t + 16], xT[:, k, t * 128:t * 128 + 128], rw[:, k, :], k == 0, k == 7,
                       b.rel, xt, inc=(k == 7))

        def s32(n):
            return small[:, 220 + 32 * n:252 + 32 * n]

        def tv(ap):
            return ap.rearrange("p (t n) -> p t n", t=2)

        def t1(ap, n=16):
            return bc(ap.rearrange("p (t a) -> p t a", a=1), [128, 2, n])

        def g1(ap):
            return bc(ap.rearrange("p (g a) -> p g a", a=1), [128, 8, 4])

        def gv(ap):
            return ap.rearrange("p (g n) -> p g n", n=4)

        def red(o, i, op=ALU.max):
            return V(lambda e: e.tensor_reduce(o, i, X, op))

        L, Pn, Mk, O1, O2 = (s32(n) for n in range(5))
        q = small[:, 412:560]
        r = tt(V, tv(L), b.ap[:, 0:32].rearrange("p (t n) -> p t n", t=2),
               bc(R("rtb").rearrange("p (a n) -> p a n", a=1), [128, 2, 16]), ALU.add, r)
        PS.put(b, r)
        red(q[:, 0:2], tv(L))
        r = tt(V, tv(Pn), tv(L), t1(q[:, 0:2]), ALU.subtract)
        r = act(Pn, Pn, ACT.Exp, r)
        V(lambda e: e.tensor_reduce(q[:, 2:4], tv(Pn), X, ALU.add), r)
        V(lambda e: e.reciprocal(q[:, 4:6], q[:, 2:4]))
        tt(V, tv(Pn), tv(Pn), t1(q[:, 4:6]), ALU.mult)
        prs = [(0, 1), (0, 2), (0, 3), (1, 2), (1, 3), (2, 3)]
        pr = q[:, 8:56].rearrange("p (g n) -> p g n", n=6)
        for n, (a1, b1) in enumerate(prs):
            tt(V, pr[:, :, n:n + 1], gv(Pn)[:, :, a1:a1 + 1], gv(Pn)[:, :, b1:b1 + 1], ALU.add)
        gsc = q[:, 56:64]
        red(gsc, pr)
        g2 = gsc.rearrange("p (t n) -> p t n", t=2)

        def first(dst, src, width, wts, mx):
            red(mx, src)
            tt(V, dst, src, t1(mx, width), ALU.is_equal)
            tt(V, dst, dst, wts, ALU.mult)
            red(q[:, 72:74], dst)
            return tt(V, dst, dst, t1(q[:, 72:74], width), ALU.is_equal)

        sel = q[:, 64:72]
        first(sel.rearrange("p (t n) -> p t n", t=2), g2, 4, K("g4").rearrange("p (t n) -> p t n", t=2), q[:, 74:76])
        ts(V, sel, sel, 1.0, 1e30, ALU.subtract, ALU.mult)
        tt(V, gv(Mk), gv(L), g1(sel), ALU.add)
        first(tv(O1), tv(Mk), 16, tv(K("e16")), q[:, 76:78])
        stt(Mk, O1, -1e32, Mk, ALU.mult, ALU.add)
        first(tv(O2), tv(Mk), 16, tv(K("e16")), q[:, 78:80])
        r = tt(V, q[:, 80:82], q[:, 78:80], q[:, 76:78], ALU.subtract)
        r = act(q[:, 80:82], q[:, 80:82], ACT.Exp, r)
        ts(V, q[:, 82:84], q[:, 80:82], 1.0, None, ALU.add, None, r)
        V(lambda e: e.reciprocal(q[:, 84:86], q[:, 82:84]))
        tt(V, q[:, 86:88], q[:, 80:82], q[:, 84:86], ALU.mult)
        qs = take(96)
        sl, rk, W = qs[:, 0:32], qs[:, 32:64], qs[:, 64:96]
        r = tt(V, sl, O1, O2, ALU.add)
        b = PS.get()
        mm(b.ap[:, 0:16], K("tri"), sl[:, 0:16], True, True, r, b.rel)
        mm(b.ap[:, 16:32], K("tri"), sl[:, 16:32], True, False)
        mm(b.ap[:, 16:32], ones[:, :], sl[:, 0:16], False, True)
        mm(b.ap[:, 32:48], ones[:, :], sl[:, 0:16], True, False)
        cnt = mm(b.ap[:, 32:48], ones[:, :], sl[:, 16:32], False, True, inc=True)
        tt(V, tv(O1), tv(O1), t1(q[:, 84:86]), ALU.mult)
        tt(V, tv(O2), tv(O2), t1(q[:, 86:88]), ALU.mult)
        tt(V, W, O1, O2, ALU.add)
        ts(V, rk, b.ap[:, 0:32], 1.0, None, ALU.subtract, None, cnt)
        co = take(48)
        ov, wv, hot = (co[:, 16 * n:16 * n + 16] for n in range(3))
        r = ts(V, ov, b.ap[:, 32:48], 128.5, None, ALU.is_gt, None)
        PS.put(b, r)
        tables("silu_and_others")

        for t in range(2):
            for c in range(2):
                b = PS.get()
                for k in range(4):
                    m = tp(b.ap[:, 128 * k:128 * k + 128], xT[:, 4 * c + k, t * 128:t * 128 + 128], xt, b.rel, inc=(k == 3))
                hi, lo = (hs[:, j, t, c * 512:c * 512 + 512] for j in range(2))
                m = cpy(A, hi, b.ap, m)
                hst = tt(V, lo, b.ap, hi.bitcast(F32), ALU.subtract, m)
                PS.put(b, hst)

        col3, eid, regs = take(18), eids, []

        def spill():
            red(q[:, 90:91], ov, ALU.add)
            cpy(V, eids[:, 3:4], q[:, 90:91])
            tt(V, wv, ov, K("e16")[:, 0:16], ALU.mult)
            for j in range(3):
                mx = q[:, 90:91]
                red(mx, wv)
                ts(V, hot, wv, mx, None, ALU.is_equal, None)
                tt(V, hot, hot, ov, ALU.mult)
                d = q[:, 92:108]
                tt(V, d, wv, hot, ALU.mult)
                tt(V, wv, wv, d, ALU.subtract)
                tt(V, ov, ov, hot, ALU.subtract)
                ts(V, mx, mx, -1.0, 16.0, ALU.mult, ALU.add)
                ts(V, mx, mx, 15.0, None, ALU.min, None)
                r = cpy(V, eid[:, j:j + 1], mx)
                pr = spt.rearrange("p (a n) -> p a n", a=6)
                tt(V, pr, qs.rearrange("p (a n) -> p a n", a=6),
                   bc(hot.rearrange("p (a n) -> p a n", a=1), [128, 6, 16]), ALU.mult)
                red(col3[:, 6 * j:6 * j + 6], pr, ALU.add)
                ts(V, col3[:, 6 * j + 2:6 * j + 4], col3[:, 6 * j + 2:6 * j + 4], 128.0, None, ALU.subtract, None)
            return V.now()

        flag = {q_: [] for q_ in (T, V, A, S)}

        def read_flag(tok):
            for q_, f in flag.items():
                q_.wait(tok)
                q_.raw(lambda e, f=f: f.append(e.value_load(eids[0:1, 3:4], min_val=0, max_val=3)))
            for j in range(3):
                S.raw(lambda e, j=j: regs.append(e.value_load(eids[0:1, j:j + 1], min_val=0, max_val=15)))

        spt = take(96)
        cw = take(20)

        def where(p, t):
            if p < 16:
                return [a[:, 16 * t + p:16 * t + p + 1] for a in (sl, rk, W)]
            return [col3[:, 6 * (p - 16) + 2 * a + t:6 * (p - 16) + 2 * a + t + 1] for a in range(3)]

        places = 19
        piece = {}
        for n in ("mg", "mu", "md"):
            for p in range(16):
                piece[n, p] = ins[n][l * 16 + p]
            for j in range(3):
                piece[n, 16 + j] = lambda n=n, j=j: ins[n][bass.ds(regs[j] + l * 16, 1)].rearrange("a p n -> (a p) n")

        def up_of(p):
            return [(piece[n, p], 8, "pair", c, c == 3) for n in ("mg", "mu") for c in range(4)]

        def plan(lo, hi):
            yield from up_of(lo)
            for p in range(lo, hi):
                yield from (up_of(p + 1) if p + 1 < hi else [])
                yield from rows_of_piece(piece["md", p])

        hd = Pool([take(512) for _ in range(2)])
        htp = Pool([hts[:, n] for n in range(2)])
        ptp = Pool([pts[:, n] for n in range(4)])
        acc, get = [], [None]
        pfree, xfree, yfree = [None], [None], [None]
        PT, CW, XG, H, HT, Y = {}, {}, {}, {}, {}, {}

        def select(p0):
            for n in range(2):
                if p0 + n < places:
                    for t in range(2):
                        s_, r_, _ = where(p0 + n, t)
                        r = ts(V, pm[:, t, 128 * n:128 * n + 128], K("iota"), r_, s_, ALU.is_equal, ALU.mult, pfree[0])
            return r

        def gather(p0, r):
            w = 256 if p0 + 1 < places else 128
            toks = []
            for c in range(4):
                b = PS.get()
                for k in range(2):
                    o = b.ap[:, 256 * k:256 * k + w]
                    f = 2 * c + k
                    for n, (j, t) in enumerate(((0, 0), (0, 1), (1, 0), (1, 1))):
                        m = mm(o, hs[:, j, t, 128 * f:128 * f + 128], pm[:, t, 0:w], n == 0, n == 3, r, hst, b.rel,
                               inc=(k == 1 and n == 3))
                v = b.ap.rearrange("p (k n) -> p k n", k=2)[:, :, 0:w]
                hi, lo = (xsp[:, j, 2 * c:2 * c + 2, 0:w] for j in range(2))
                q1 = cpy(A, hi, v, m, xfree[0])
                q2 = tt(V, lo, v, hi.bitcast(F32), ALU.subtract, q1, m)
                PS.put(b, q2)
                toks.append(q2)
            XG[p0] = XG[p0 + 1] = toks
            n2 = w // 128
            b = PS.get()
            for n in range(n2):
                for t in range(2):
                    m = tp(b.ap[:, 256 * n + 128 * t:256 * n + 128 * t + 128], pm[:, t, 128 * n:128 * n + 128].bitcast(F32), r,
                           b.rel, inc=(n == n2 - 1 and t == 1))
            for n in range(n2):
                pt = ptp.get()
                v = cpy(A, pt.ap, b.ap[:, 256 * n:256 * n + 256], m, pt.rel)
                PT[p0 + n] = (pt, v)
            PS.put(b, v)
            b = PS.get()
            for n in range(n2):
                for t in range(2):
                    m = mm(b.ap[:, n:n + 1], pm[:, t, 128 * n:128 * n + 128].bitcast(F32), where(p0 + n, t)[2], t == 0, t == 1,
                           b.rel, inc=(n == n2 - 1 and t == 1))
            v = cpy(V, cw[:, p0:p0 + n2], b.ap[:, 0:n2], m)
            PS.put(b, v)
            CW[p0] = CW[p0 + 1] = v
            pfree[0] = m

        def gate_up(p):
            seat = slice(128 * (p % 2), 128 * (p % 2) + 128)
            h = hd.get()
            for u in range(2):
                b = PS.get()
                for c in range(4):
                    buf, hi, lo, r = get[0]()
                    for k in range(2):
                        f = 2 * c + k
                        for n, (j, w) in enumerate(((0, hi), (0, lo), (1, hi))):
                            m = mm(b.ap, xsp[:, j, f, seat], w[:, k, :], f == 0 and n == 0, f == 7 and n == 2,
                                   r, XG[p][f // 2], b.rel, inc=(n == 2 and k == 1))
                    stage[3].put(buf, m)
                if u == 0:
                    r = act(h.ap, b.ap, ACT.Silu, m, h.rel)
                else:
                    r = tt(V, h.ap, h.ap, b.ap, ALU.mult, m, r)
                PS.put(b, r)
            xfree[0] = m
            H[p] = (h, r)

        def turn(p):
            h, r = H.pop(p)
            b = PS.get()
            for f in range(4):
                m = tp(b.ap[:, 128 * f:128 * f + 128], h.ap[:, 128 * f:128 * f + 128], r, b.rel, inc=(f == 3))
            hd.put(h, m)
            ht = htp.get()
            v = b.ap.rearrange("p (k n) -> p k n", k=4)
            hi, lo = ht.ap[:, 0], ht.ap[:, 1]
            q1 = cpy(A, hi, v, m, ht.rel)
            q2 = tt(V, lo, v, hi.bitcast(F32), ALU.subtract, q1, m)
            PS.put(b, q2)
            HT[p] = (ht, q2)

        def down_p(p):
            ht, tk = HT.pop(p)
            hh, hl = ht.ap[:, 0], ht.ap[:, 1]
            banks = [PS.get() for _ in range(2)]
            for f in range(4):
                buf, hi, lo, r = get[0]()
                for c in range(2):
                    b = banks[c]
                    cc = slice(c * 512, c * 512 + 512)
                    for n, (a, w) in enumerate(((hh, hi), (hh, lo), (hl, hi))):
                        m = mm(b.ap, a[:, f, :], w[:, cc], f == 0 and n == 0, f == 3 and n == 2, r, tk, b.rel, inc=(n == 2))
                    if f == 3:
                        s_ = cw[:, p:p + 1]
                        hi_, lo_ = ysp[:, 0, cc], ysp[:, 1, cc]
                        q1 = act(hi_, b.ap, ACT.Copy, m, CW[p], yfree[0], scale=s_)
                        q2 = V(lambda e, b=b, s_=s_, hi_=hi_, lo_=lo_: e.scalar_tensor_tensor(
                            out=lo_, in0=b.ap, scalar=s_, in1=hi_.bitcast(F32), op0=ALU.mult, op1=ALU.subtract), q1, m)
                        PS.put(b, q2)
                stage[3].put(buf, m)
            htp.put(ht, m)
            Y[p] = q2

        def scatter(p):
            y = Y.pop(p)
            pt, v = PT.pop(p)
            if not acc:
                acc.extend(PS.get() for _ in range(4))
            for t in range(2):
                for c in range(2):
                    for j in range(2):
                        m = mm(acc[2 * t + c].ap, pt.ap[:, 128 * t:128 * t + 128], ysp[:, j, c * 512:c * 512 + 512],
                               p == 0 and j == 0, p in (15, 18) and j == 1, y, v, acc[2 * t + c].rel,
                               inc=(j == 1 and c == 1))
                fin[t] = m
            yfree[0] = m
            ptp.put(pt, m)

        fin = [None, None]
        def span(lo, hi):
            get[0] = stream(plan(lo, hi))
            V.loose = A.loose = True
            for p in range(lo, hi):
                new = (p - lo) % 2 and p + 1 < hi
                if new:
                    sel_tok = select(p + 1)
                gate_up(p)
                if p >= lo + 2:
                    scatter(p - 2)
                if new:
                    gather(p + 1, sel_tok)
                if p >= lo + 1:
                    down_p(p - 1)
                turn(p)
                if p == 6:
                    read_flag(spilt)
            scatter(hi - 2)
            down_p(hi - 1)
            scatter(hi - 1)
            V.loose = A.loose = False

        def rest():
            gather(16, select(16))
            span(16, 19)

        gather(0, select(0))
        spilt = spill()
        gate_row(i)
        span(0, 16)
        when(flag, rest)
        return norm(acc, fin, True, rows_of[0] if last else None)

    lt = moe(0, 1, lt)

    open_stage(24800, mark[0], False)
    xt = transposed(lt, after(5), rows_of[0])
    rows_of[0] = load_rows(6)
    tables("silu_and_others")
    qk = take(16 * 256).rearrange("p (n m) -> p n m", n=16)
    gTf = take(16 * 256)
    gT = gTf.rearrange("p (n m) -> p n m", n=16)
    vr = take(4096).rearrange("p (t n) -> p t n", t=2)
    dec = take(2048)
    cs_ = take(512)
    tmpr = Pool([take(512) for _ in range(3)])
    A.raw(lambda e: e.dma_start(dec, ins["dec"]).then_inc(s_dec, 16))
    A.raw(lambda e: e.dma_start(posi[:, :], ins["pos"].broadcast_to([128, 256])).then_inc(s_dec, 16))
    DEC = (s_dec, 32)
    cosT, sinT = cs_[:, 0:256], cs_[:, 256:512]
    tb = tmpr.get()
    ang, kq = tb.ap[:, 0:256], tb.ap[:, 256:512]
    cpy(V, ang, posi[:, :], DEC)
    ts(V, ang, ang, K("freq"), None, ALU.mult, None)
    ki = posi[:, :]
    C1, C2 = 6.28125, 2 * math.pi - 6.28125
    C2a = float(np.float32(np.round(C2 * 2 ** 20) / 2 ** 20))
    C2b = C2 - C2a
    for dst, shift in ((sinT, 0.0), (cosT, 0.25)):
        ts(V, kq, ang, 1.0 / (2 * math.pi), shift, ALU.mult, ALU.add)
        cpy(V, ki, kq)
        cpy(V, kq, ki)
        stt(dst, kq, -C1, ang, ALU.mult, ALU.add)
        stt(dst, kq, -C2a, dst, ALU.mult, ALU.add)
        stt(dst, kq, -C2b, dst, ALU.mult, ALU.add)
        if shift:
            ts(V, dst, dst, math.pi / 2, None, ALU.add, None)
        r = ts(V, dst, dst, math.pi, -math.pi, ALU.min, ALU.max)
        rc = act(dst, dst, ACT.Sin, r)
    tmpr.put(tb, V.now())
    qtok = {}

    def evac_ret(c0):
        def f(c, ps, r):
            n = c0 + c
            if n >= 16:
                r = act(gT[:, n - 16, :], ps, ACT.Silu, r)
                return r
            tb = tmpr.get()
            raw, t2 = tb.ap[:, 0:256], tb.ap[:, 256:512]
            rel = act(raw, ps, ACT.Copy, r, tb.rel, scale=1.0 if n < 8 else 128 ** -0.5)
            b = PS.get()
            k = mm(b.ap[:, 0:256], K("rot"), raw, True, True, rel, b.rel, inc=True)
            r1 = tt(V, t2, b.ap[:, 0:256], sinT, ALU.mult, k, rc)
            PS.put(b, r1)
            tt(V, raw, raw, cosT, ALU.mult)
            qtok[n] = tt(V, qk[:, n, :], raw, t2, ALU.add)
            tmpr.put(tb, qtok[n])
            return rel
        return f

    run([proj_T(ins["wr"][j], 4, xt, evac_ret(4 * j)) for j in range(8)], 1)
    row_tok = []
    run([proj_rows(ins["wrv"][j], 512, xt, evac_rows(vr, 512 * j, A if j % 2 else V)) for j in range(4)], 1)
    gate_row(2)
    tables("natural_log_exp_and_others")
    rtmp = Pool([take(384) for _ in range(3)])
    otmp = Pool([take(512) for _ in range(3)])
    gtok = A.now()
    ret_tok = []

    def ret_unit(h):
        b = PS.get()
        mm(b.ap[:, 0:256], qk[:, 8 + h, 0:128], qk[:, h, :], True, True, b.rel, qtok[h], qtok[8 + h])
        k = mm(b.ap[:, 256:384], qk[:, 8 + h, 128:256], qk[:, h, 128:256], True, True, inc=True)
        p = rtmp.get()
        tt(V, p.ap[:, 0:256], b.ap[:, 0:256], dec[:, h * 256:h * 256 + 256], ALU.mult, k, p.rel, DEC)
        r = tt(V, p.ap[:, 256:384], b.ap[:, 256:384], dec[:, h * 256:h * 256 + 128], ALU.mult)
        PS.put(b, r)
        yield 1
        b = PS.get()
        for d in range(2):
            c = h * 256 + d * 128
            mm(b.ap[:, d * 256:d * 256 + 256], vr[:, 0, c:c + 128], p.ap[:, 0:256], True, False, r, b.rel, row_tok)
            k = mm(b.ap[:, d * 256 + 128:d * 256 + 256], vr[:, 1, c:c + 128], p.ap[:, 256:384], False, True, inc=True)
        rtmp.put(p, k)
        o = otmp.get()
        r = cpy(A, o.ap, b.ap, k, o.rel)
        PS.put(b, r)
        yield 1
        b = PS.get()
        mm(b.ap[:, 0:256], ones[:, :], o.ap[:, 0:256], True, False, r, b.rel)
        k = mm(b.ap[:, 0:256], ones[:, :], o.ap[:, 256:512], False, True, inc=True)
        for d in range(2):
            r = stt(o.ap[:, d * 256:d * 256 + 256], b.ap[:, 0:256], -1.0 / 256, o.ap[:, d * 256:d * 256 + 256],
                    ALU.mult, ALU.add, k)
        PS.put(b, r)
        tb = tmpr.get()
        r = act(tb.ap, o.ap, ACT.Square, r, tb.rel)
        yield 1
        b = PS.get()
        mm(b.ap[:, 0:256], ones[:, :], tb.ap[:, 0:256], True, False, r, b.rel)
        k = mm(b.ap[:, 0:256], ones[:, :], tb.ap[:, 256:512], False, True, inc=True)
        r1, r2 = inv_sqrt(tb.ap[:, 0:256], b.ap[:, 0:256], 1.0 / 256, 1e-5, None, k)
        PS.put(b, r1)
        for d in range(2):
            od = o.ap[:, d * 256:d * 256 + 256]
            tt(V, od, od, tb.ap[:, 0:256], ALU.mult, r2)
            r = stt(gT[:, 2 * h + d, :], od, C("rgn", 2 * h + d, 2 * h + d + 1), gT[:, 2 * h + d, :],
                    ALU.mult, ALU.mult, gtok)
        tmpr.put(tb, r)
        otmp.put(o, r)
        ret_tok.append(r)
        yield 1

    run([ret_unit(h) for h in range(8)], 3, adaln(3))
    banks, k = down([ins["wro"][j] for j in range(4)], gT, ret_tok)
    lt = norm(banks, k, True)
    moe(1, 3, lt, True)
    A.wait((s_out, 32))
    A.wait(*[q.now() for q in (T, V, G)])

    stage[0].close()
    block = ctx.enter_context(nc.Block())

    @block.tensor
    def _(e):
        for f in T.ops:
            f(e)

    @block.vector
    def _(e):
        for f in V.ops:
            f(e)

    @block.scalar
    def _(e):
        for f in A.ops:
            f(e)

    @block.gpsimd
    def _(e):
        for f in G.ops:
            f(e)

    @block.sync
    def _(e):
        for f in S.ops:
            f(e)


def kernel(**inputs):
    import numpy as _np
    import concourse.bacc as _bacc
    from concourse import mybir as _mybir
    from concourse.bass_utils import run_bass_kernel_spmd as _run

    a = {k: _np.ascontiguousarray(v) for k, v in inputs.items()}

    def tiles(w, kt, cols):
        n = w.shape[1] // cols
        return w.reshape(kt, 128, n, cols).transpose(2, 1, 0, 3).reshape(n, 128, kt * cols)

    def rowtiles(w, kt):
        n = w.shape[0] // (kt * 128)
        return w.reshape(n, kt, 128, w.shape[1]).transpose(0, 2, 1, 3).reshape(n, 128, kt * w.shape[1])

    def col(v, n):
        v = v.reshape(-1, n, 128)
        return v.transpose(2, 1, 0).reshape(128, -1)

    def pad(v):
        return _np.concatenate([v, _np.zeros((128 - v.shape[0], v.shape[1]), v.dtype)])

    we, wo = a["w_in_even"][0], a["w_in_odd"][0]
    ins = {"x": a["x"][0]}
    ins["we"] = tiles(_np.concatenate([we[:, 0:3072], we[:, 3084:4620]], 1), 8, 512)
    ins["wev"] = tiles(we[:, 4620:5132], 8, 512)
    ins["wev2"] = tiles(we[:, 5132:5388], 8, 256)
    ins["woe"] = rowtiles(a["w_out_even"][0], 4)
    ins["woo"] = rowtiles(a["w_out_odd"][0], 4)
    ins["wo"] = tiles(_np.concatenate([wo[:, 0:1024], wo[:, 1536:2048], wo[:, 2560:3072]], 1), 8, 512)
    ins["wov"] = tiles(_np.concatenate([wo[:, 1024:1536], wo[:, 2048:2560]], 1), 8, 512)
    for l in range(2):
        u = a["ffn_w_up"][l].reshape(1024, 2, 11, 256).transpose(0, 2, 1, 3).reshape(1024, 5632)
        ins[f"wu{l}"] = tiles(u, 8, 512)
        d = a["ffn_w_down"][l]
        ins[f"wd{l}"] = rowtiles(d[0:2560], 4)
        ins[f"wdl{l}"] = rowtiles(d[2560:2816], 2)
    ins["ada"] = _np.concatenate([tiles(w, 8, 512) for w in a["ada_w_2"].reshape(4, 1024, 3072)])
    ins["ws"] = tiles(a["sb_w_in_2"][0], 8, 512)
    ins["wso"] = rowtiles(a["sb_w_out_2"][0], 4)
    wr = a["ret_w_in_2"][0]
    ins["wr"] = tiles(_np.concatenate([wr[:, 0:2048], wr[:, 4096:6144]], 1), 8, 512)
    ins["wrv"] = tiles(wr[:, 2048:4096], 8, 512)
    ins["wro"] = rowtiles(a["ret_w_out_2"][0], 4)
    ins["mg"] = _np.concatenate([tiles(w, 8, 512) for w in a["moe_w_gate_2"].reshape(32, 1024, 512)])
    ins["mu"] = _np.concatenate([tiles(w, 8, 512) for w in a["moe_w_up_2"].reshape(32, 1024, 512)])
    ins["md"] = _np.concatenate([rowtiles(w, 4) for w in a["moe_w_down_2"].reshape(32, 512, 1024)])
    adab = a["ada_b_2"].reshape(4, 3072)
    g1, b1 = a["ln_g"].reshape(4, 1024), a["ln_b"].reshape(4, 1024)
    g2, b2 = a["ln_g_2"].reshape(4, 1024), a["ln_b_2"].reshape(4, 1024)
    par = {
        "gconv": col(a["gdn_conv_w"][0], 18), "fw0": col(a["ffn_conv_w"][0], 44), "fb0": col(a["ffn_conv_b"][0], 44),
        "fw1": col(a["ffn_conv_w"][1], 44), "fb1": col(a["ffn_conv_b"][1], 44), "gnw": col(a["gdn_norm_w"][0], 1),
        "dnw": col(a["diff_norm_w"][0], 1), "lnw": col(a["gla_norm_w"][0], 1), "lbg": col(a["gla_b_gate"][0], 2),
        "rgn": col(a["ret_gn_g_2"][0], 16), "adab": _np.concatenate([col(b, 24) for b in adab], 1),
        "lng": _np.concatenate([col(v, 8) for v in _np.concatenate([g1, g2])], 1),
        "lnb": _np.concatenate([col(v, 8) for v in _np.concatenate([b1, b2])], 1),
        "c": col(a["c_2"][0], 8), "dl": pad(a["diff_lambda"][0].T), "rb": pad(a["rel_bias"]),
        "lwg": pad(a["gla_w_gate"][0]), "rw": tiles(a["router_w_2"], 8, 16)[0],
        "wba": tiles(we[:, 3072:3084], 8, 12)[0], "wgd": tiles(wo[:, 3072:3088], 8, 16)[0],
    }
    assert all(par[n].shape == (128, w) for n, w in PARAMS), {n: par[n].shape for n, _ in PARAMS}
    ins["cp"] = _np.concatenate([par[n] for n, _ in PARAMS], 1)
    ins["rp"] = _np.concatenate([a["gdn_a_log"][0], a["gdn_dt_bias"][0], a["router_b_2"]])[None, :]
    rows = []
    for g, b in zip(_np.concatenate([g1, g2]), _np.concatenate([b1, b2])):
        rows += [g, b]
    ins["rows"] = _np.stack(rows)
    ins["kc"], _, ins["dec"] = consts()
    ins["pos"] = a["positions_2"]

    nc = _bacc.Bacc("TRN2", target_bir_lowering=False, num_devices=1)
    arrays, args = {}, {}
    for name, v in ins.items():
        v = _np.ascontiguousarray(v)
        arrays[f"in_{name}"] = v
        args[name] = nc.dram_tensor(f"in_{name}", v.shape, _mybir.dt.from_np(v.dtype), kind="ExternalInput").ap()
    out = nc.dram_tensor("out_0", (256, 1024), _mybir.dt.float32, kind="ExternalOutput").ap()
    build(nc, args, out)
    r = _run(nc, [arrays], core_ids=[0])
    return r.results[0]["out_0"].reshape(1, 256, 1024)
```
